# Optimizing a Trainium2 kernel written in Bass

```python
import jax, jax.numpy as jnp
from jax import lax
import numpy as np

D_MODEL = 1024
BATCH = 1
SEQ = 2048
DEPTH = 1
DEC_BATCH = 8
DEC_SEQ = 16
PAST_LEN = 1024

CHUNK = 64
D_MIX = D_MODEL
D_A = D_MIX // 2
A_GROUPS = 4
A_GROUP_DIM = D_A // A_GROUPS
GMLP_CHUNK = 128
D_B = D_MIX - D_A
B_HEADS = 8
B_HEAD_DIM = D_B // B_HEADS
CONV_WIDTH = 4
LRU_C = 8.0
N_GROUPS = 4
EXPERTS_PER_GROUP = 8
N_EXPERTS = N_GROUPS * EXPERTS_PER_GROUP
TOP_K_INNER = 2
D_EXPERT = D_MODEL // 2
MOE_BLOCK = 128
EPS = 1e-6

kernel_name = "hymba_gmlp_rglru_hier_moe_stream_step"

def rms_norm(x, g):
    xf = x.astype(jnp.float32)
    y = xf * lax.rsqrt(jnp.mean(xf * xf, axis=-1, keepdims=True) + EPS)
    return (y * g.astype(jnp.float32)).astype(x.dtype)

def group_layer_norm(v, g, b):
    vf = v.astype(jnp.float32)
    mu = jnp.mean(vf, axis=-1, keepdims=True)
    var = jnp.mean(jnp.square(vf - mu), axis=-1, keepdims=True)
    y = (vf - mu) * lax.rsqrt(var + EPS)
    y = y * g.astype(jnp.float32).reshape(A_GROUPS, A_GROUP_DIM) + b.astype(jnp.float32).reshape(A_GROUPS, A_GROUP_DIM)
    return y.astype(v.dtype)

def gmlp_spatial_gate(u, v, ln_g, ln_b, w_s, b_s):
    B, T, _ = v.shape
    L = min(T, GMLP_CHUNK)
    vn = group_layer_norm(v.reshape(B, T, A_GROUPS, A_GROUP_DIM), ln_g, ln_b)
    mask = jnp.tril(jnp.ones((L, L), dtype=bool))
    w = jnp.where(mask, w_s[:, :L, :L], jnp.zeros((), w_s.dtype))
    vc = vn.reshape(B, T // L, L, A_GROUPS, A_GROUP_DIM)
    s = jnp.einsum('gts,bcsgd->bctgd', w, vc) + b_s[:, :L].T[None, None, :, :, None]
    out = u * s.reshape(B, T, D_A).astype(u.dtype)
    return out, vn.reshape(B, T, D_A)

def causal_depthwise_conv(xpad, w, b):
    T = xpad.shape[1] - (CONV_WIDTH - 1)
    y = b
    for k in range(CONV_WIDTH):
        y = y + xpad[:, k:k + T] * w[k]
    return y

def _lru_combine(c1, c2):
    a1, b1 = c1
    a2, b2 = c2
    return a1 * a2, a2 * b1 + b2

def rglru(xc, h0, w_a, b_a, w_x, b_x, lam):
    B, T, _ = xc.shape
    xh = xc.astype(jnp.float32).reshape(B, T, B_HEADS, B_HEAD_DIM)
    r = jax.nn.sigmoid(jnp.einsum('bthi,hij->bthj', xh, w_a.astype(jnp.float32)) + b_a.astype(jnp.float32)).reshape(B, T, D_B)
    i = jax.nn.sigmoid(jnp.einsum('bthi,hij->bthj', xh, w_x.astype(jnp.float32)) + b_x.astype(jnp.float32)).reshape(B, T, D_B)
    log_a = -LRU_C * r * jax.nn.softplus(-lam.astype(jnp.float32))
    a = jnp.exp(log_a)
    gain = jnp.sqrt(-jnp.expm1(2.0 * log_a))
    bterm = gain * i * xh.reshape(B, T, D_B)
    a_cum, h = lax.associative_scan(_lru_combine, (a, bterm), axis=1)
    h = h + a_cum * h0.astype(jnp.float32)[:, None]
    return h, h[:, -1]

def expert_ffn(xb, wg, wu, wd):
    return (jax.nn.silu(xb @ wg) * (xb @ wu)) @ wd

def hier_moe(x, rg_w, rg_b, re_w, re_b, w_gate, w_up, w_down):
    N, D = x.shape
    xf = x.astype(jnp.float32)
    g_logits = xf @ rg_w.astype(jnp.float32) + rg_b.astype(jnp.float32)
    g_prob = jax.nn.softmax(g_logits, axis=-1)
    grp = jnp.argmax(g_logits, axis=-1).astype(jnp.int32)
    p_grp = jnp.take_along_axis(g_prob, grp[:, None], axis=1)
    e_logits = (xf @ re_w.astype(jnp.float32) + re_b.astype(jnp.float32)).reshape(N, N_GROUPS, EXPERTS_PER_GROUP)
    e_in = jnp.take_along_axis(e_logits, grp[:, None, None], axis=1)[:, 0]
    top_v, top_i = lax.top_k(e_in, TOP_K_INNER)
    gates = p_grp * jax.nn.softmax(top_v, axis=-1)
    expert = grp[:, None] * EXPERTS_PER_GROUP + top_i.astype(jnp.int32)
    A = N * TOP_K_INNER
    flat_e = expert.reshape(-1)
    order = jnp.argsort(flat_e, stable=True)
    sorted_e = flat_e[order]
    tok_sorted = (order // TOP_K_INNER).astype(jnp.int32)
    sizes = jnp.bincount(flat_e, length=N_EXPERTS)
    padded = (sizes + MOE_BLOCK - 1) // MOE_BLOCK * MOE_BLOCK
    starts = jnp.cumsum(sizes) - sizes
    pad_ends = jnp.cumsum(padded)
    pad_starts = pad_ends - padded
    dest = pad_starts[sorted_e] + jnp.arange(A, dtype=jnp.int32) - starts[sorted_e]
    n_blocks = -(-A // MOE_BLOCK) + N_EXPERTS
    P = n_blocks * MOE_BLOCK
    slot_tok = jnp.full((P,), N, dtype=jnp.int32).at[dest].set(tok_sorted)
    x_ext = jnp.concatenate([x, jnp.zeros((1, D), x.dtype)], axis=0)
    xb = x_ext[slot_tok].reshape(n_blocks, MOE_BLOCK, D)
    blk_expert = jnp.minimum(jnp.searchsorted(pad_ends, jnp.arange(n_blocks) * MOE_BLOCK, side='right'), N_EXPERTS - 1)
    yb = lax.map(lambda a: expert_ffn(a[0], w_gate[a[1]], w_up[a[1]], w_down[a[1]]), (xb, blk_expert))
    y_sorted = yb.reshape(P, D)[dest]
    g_sorted = gates.reshape(-1)[order]
    y = jax.ops.segment_sum(y_sorted.astype(jnp.float32) * g_sorted[:, None], tok_sorted, num_segments=N)
    return y.astype(x.dtype)

def encoder_layer(x, conv_cache, h0, lp):
    B, T, D = x.shape
    h = rms_norm(x, lp['norm1_g'])
    z = h @ lp['w_in']
    u_a = z[..., :D_A]
    v_a = z[..., D_A:2 * D_A]
    x_b = z[..., 2 * D_A:2 * D_A + D_B]
    g_b = z[..., 2 * D_A + D_B:]
    out_a, v_rows = gmlp_spatial_gate(u_a, v_a, lp['gmlp_ln_g'], lp['gmlp_ln_b'], lp['gmlp_w_s'], lp['gmlp_b_s'])
    xpad = jnp.concatenate([conv_cache.astype(x_b.dtype), x_b], axis=1)
    xc = causal_depthwise_conv(xpad, lp['conv_w'], lp['conv_b'])
    new_conv = xpad[:, -(CONV_WIDTH - 1):]
    hseq, h_last = rglru(xc, h0, lp['lru_w_a'], lp['lru_b_a'], lp['lru_w_x'], lp['lru_b_x'], lp['lru_lambda'])
    out_b = hseq.astype(x.dtype) * jax.nn.gelu(g_b)
    x = x + jnp.concatenate([out_a, out_b], axis=-1) @ lp['w_out']
    h2 = rms_norm(x, lp['norm2_g'])
    moe = hier_moe(h2.reshape(B * T, D), lp['router_group_w'], lp['router_group_b'], lp['router_expert_w'], lp['router_expert_b'],
                   lp['expert_w_gate'], lp['expert_w_up'], lp['expert_w_down'])
    x = x + moe.reshape(B, T, D)
    return x, v_rows, new_conv, h_last

def setup_inputs(seed: int = 0) -> dict:
    key = jax.random.key(seed)
    ks = jax.random.split(key, 24)
    f32 = jnp.float32
    nrm = lambda k, shape, scale: jax.random.normal(k, shape, f32) * scale
    u = jax.random.uniform(ks[12], (DEPTH, D_B), f32, 0.9, 0.999)
    s = u ** (1.0 / LRU_C)
    lru_lambda = jnp.log(s) - jnp.log1p(-s)
    return {
        "x_prompt": nrm(ks[0], (BATCH, SEQ, D_MODEL), 1.0),
        "x_sample": nrm(ks[1], (DEC_BATCH, DEC_SEQ, D_MODEL), 1.0),
        "state_conv": nrm(ks[2], (DEPTH, DEC_BATCH, CONV_WIDTH - 1, D_B), 1.0),
        "state_rglru": nrm(ks[3], (DEPTH, DEC_BATCH, D_B), 1.0),
        "norm1_g": 1.0 + nrm(ks[4], (DEPTH, D_MODEL), 0.02),
        "w_in": nrm(ks[5], (DEPTH, D_MODEL, 2 * D_A + 2 * D_B), D_MODEL ** -0.5),
        "gmlp_ln_g": 1.0 + nrm(ks[6], (DEPTH, D_A), 0.02),
        "gmlp_ln_b": nrm(ks[7], (DEPTH, D_A), 0.02),
        "gmlp_w_s": nrm(ks[8], (DEPTH, A_GROUPS, GMLP_CHUNK, GMLP_CHUNK), GMLP_CHUNK ** -0.5),
        "gmlp_b_s": 1.0 + nrm(ks[9], (DEPTH, A_GROUPS, GMLP_CHUNK), 0.01),
        "conv_w": nrm(ks[10], (DEPTH, CONV_WIDTH, D_B), CONV_WIDTH ** -0.5),
        "conv_b": nrm(ks[11], (DEPTH, D_B), 0.01),
        "lru_w_a": nrm(ks[13], (DEPTH, B_HEADS, B_HEAD_DIM, B_HEAD_DIM), B_HEAD_DIM ** -0.5),
        "lru_b_a": nrm(ks[14], (DEPTH, B_HEADS, B_HEAD_DIM), 0.01),
        "lru_w_x": nrm(ks[15], (DEPTH, B_HEADS, B_HEAD_DIM, B_HEAD_DIM), B_HEAD_DIM ** -0.5),
        "lru_b_x": nrm(ks[16], (DEPTH, B_HEADS, B_HEAD_DIM), 0.01),
        "lru_lambda": lru_lambda,
        "w_out": nrm(ks[17], (DEPTH, D_MIX, D_MODEL), D_MIX ** -0.5),
        "norm2_g": 1.0 + nrm(ks[18], (DEPTH, D_MODEL), 0.02),
        "router_group_w": nrm(ks[19], (DEPTH, D_MODEL, N_GROUPS), D_MODEL ** -0.5),
        "router_group_b": nrm(ks[20], (DEPTH, N_GROUPS), 0.01),
        "router_expert_w": nrm(ks[21], (DEPTH, D_MODEL, N_EXPERTS), D_MODEL ** -0.5),
        "router_expert_b": nrm(ks[22], (DEPTH, N_EXPERTS), 0.01),
        "expert_w_gate": nrm(jax.random.fold_in(ks[23], 0), (DEPTH, N_EXPERTS, D_MODEL, D_EXPERT), D_MODEL ** -0.5),
        "expert_w_up": nrm(jax.random.fold_in(ks[23], 1), (DEPTH, N_EXPERTS, D_MODEL, D_EXPERT), D_MODEL ** -0.5),
        "expert_w_down": nrm(jax.random.fold_in(ks[23], 2), (DEPTH, N_EXPERTS, D_EXPERT, D_MODEL), D_EXPERT ** -0.5),
        "final_norm_g": 1.0 + nrm(jax.random.fold_in(ks[23], 3), (D_MODEL,), 0.02),
    }

def reference(x_prompt, x_sample, state_conv, state_rglru, norm1_g, w_in, gmlp_ln_g, gmlp_ln_b, gmlp_w_s, gmlp_b_s,
              conv_w, conv_b, lru_w_a, lru_b_a, lru_w_x, lru_b_x, lru_lambda, w_out, norm2_g,
              router_group_w, router_group_b, router_expert_w, router_expert_b,
              expert_w_gate, expert_w_up, expert_w_down, final_norm_g):
    yp, ys = x_prompt, x_sample
    conv_p, h_p, v_s, conv_s, h_s = [], [], [], [], []
    zero_conv = jnp.zeros((x_prompt.shape[0], CONV_WIDTH - 1, D_B), x_prompt.dtype)
    zero_h = jnp.zeros((x_prompt.shape[0], D_B), jnp.float32)
    for l in range(DEPTH):
        lp = dict(norm1_g=norm1_g[l], w_in=w_in[l], gmlp_ln_g=gmlp_ln_g[l], gmlp_ln_b=gmlp_ln_b[l],
                  gmlp_w_s=gmlp_w_s[l], gmlp_b_s=gmlp_b_s[l], conv_w=conv_w[l], conv_b=conv_b[l],
                  lru_w_a=lru_w_a[l], lru_b_a=lru_b_a[l], lru_w_x=lru_w_x[l], lru_b_x=lru_b_x[l],
                  lru_lambda=lru_lambda[l], w_out=w_out[l], norm2_g=norm2_g[l],
                  router_group_w=router_group_w[l], router_group_b=router_group_b[l],
                  router_expert_w=router_expert_w[l], router_expert_b=router_expert_b[l],
                  expert_w_gate=expert_w_gate[l], expert_w_up=expert_w_up[l], expert_w_down=expert_w_down[l])
        yp, _, cp, hp = encoder_layer(yp, zero_conv, zero_h, lp)
        conv_p.append(cp)
        h_p.append(hp)
        ys, vs, cs, hs = encoder_layer(ys, state_conv[l], state_rglru[l], lp)
        v_s.append(vs)
        conv_s.append(cs)
        h_s.append(hs)
    y_prompt = rms_norm(yp, final_norm_g)
    y_sample = rms_norm(ys, final_norm_g)
    return (y_prompt, y_sample, jnp.stack(conv_p), jnp.stack(h_p), jnp.stack(v_s), jnp.stack(conv_s), jnp.stack(h_s))


_drawn_inputs = setup_inputs


def setup_inputs(seed=0):
    import zlib

    import numpy as np

    out = dict(_drawn_inputs(seed))
    spreads = {}
    factors = {'gmlp_ln_g': 7.508,
     'gmlp_ln_b': 7.805,
     'gmlp_b_s': 19.55,
     'lru_b_a': 22.381,
     'lru_b_x': 8.0,
     'router_group_b': 27.402,
     'router_expert_b': 22.148,
     'final_norm_g': 8.572,
     'norm2_g': 5.655}
    for name, (base, spread) in spreads.items():
        noise = np.random.default_rng([zlib.crc32(name.encode()), seed]).standard_normal(out[name].shape)
        drawn = base * np.exp(spread * noise) if base else spread * noise
        out[name] = __import__('jax').numpy.asarray(drawn.astype(out[name].dtype))
    for name, factor in factors.items():
        out[name] = (out[name] * factor).astype(out[name].dtype)
    return out
```

```python
from contextlib import ExitStack

import concourse.bass as bass
from concourse import mybir

ALU = mybir.AluOpType
ACT = mybir.ActivationFunctionType
AX = mybir.AxisListType
F32 = mybir.dt.float32
U32 = mybir.dt.uint32
I32 = mybir.dt.int32

P = 128
D = 1024
KD = D // P
DA = 512
NC = DA // P
GT = 2
G = GT * P
SEQ = 2048
NPG = SEQ // G
STREAMS, FRAMES = 8, 16
NTOK = SEQ + STREAMS * FRAMES
NTILE = NTOK // P
TAPS = 4
NG, EPG = 4, 8
NE = NG * EPG
DE = 512
KE = DE // P
CH = 160
HF = CH // 2
CPE = -(-NTOK // CH)
SLOTS = CPE * CH
NROW = NTOK + CH
EPS = 1e-6
GELU_C = 0.7978845608028654
BANKS = 8
BANK = 512


class PsumJobs:

    def __init__(self, segments):
        self.first, self.per, self.where = {}, {}, {}
        done = [0] * BANKS
        for name, times, jobs in segments:
            per = [0] * BANKS
            for j, job in enumerate(jobs):
                self.where[name, job] = (j % BANKS, per[j % BANKS])
                per[j % BANKS] += 1
            self.first[name], self.per[name] = list(done), per
            done = [d + times * p for d, p in zip(done, per)]

    def bank(self, seg, job):
        return self.where[seg, job][0]

    def before(self, seg, it, job):
        b, u = self.where[seg, job]
        return it * self.per[seg][b] + (self.first[seg][b] + u)


def group_jobs(tiles, prev):
    jobs = [f"xT{j}" for j in range(4)] + ["xb0", "xb1"]
    for t in range(prev):
        jobs += [f"h2T{t}a", f"h2T{t}b", f"lg{t}"]
    jobs += [f"v{t}" for t in range(tiles)] + [f"ga{c}" for c in range(NC)]
    jobs += ["pf"] if prev else []
    jobs += ["gg0", "gg1"] + [f"s{t}" for t in range(tiles)] + ["u0", "u1"]
    return jobs + [f"o{t}{h}" for t in range(tiles) for h in range(2)]


XT3 = ((0, 3), (3, 6), (6, 8))
JOBS = PsumJobs([
    ("first", 1, group_jobs(GT, 0)),
    ("loop", NPG - 1, group_jobs(GT, GT)),
    ("last", 1, group_jobs(1, GT)),
    ("tail", 1, ["h2T0a", "h2T0b", "lg0", "pf"]),
    ("plan", 1, ["plan"]),
    ("pre", 1, ["xT0", "xT1", "xT2"]),
    ("chunk", 1, [f"gu{f}" for f in range(KE)] + ["xT0", "xT1", "xT2", "y0", "y1", "y2"]
     + ["r00", "r01", "r10", "r11"]),
])


def hymba_step(nc, a):
    with ExitStack() as ctx:
        def sb(name, shape, dt=F32):
            return ctx.enter_context(nc.sbuf_tensor(name, shape, dt))

        def sem(name):
            return ctx.enter_context(nc.semaphore(name))

        acc = nc.dram_tensor("acc_rows", [NROW, D], F32).ap()
        h2_rows = nc.dram_tensor("h2_rows", [NROW, D], F32).ap()
        table = nc.dram_tensor("slot_table", [NE * SLOTS, 2], U32).ap()

        w_in = sb("w_in_sb", [P, KD * 2048])
        w_out = sb("w_out_sb", [P, KD * D])
        w_in_v = w_in[:].rearrange("p (k n) -> p k n", k=KD)
        w_out_v = w_out[:].rearrange("p (k n) -> p k n", k=KD)
        xa = sb("xa", [P, GT, D])
        xr = sb("xr", [P, GT, D])
        h2T = sb("h2T", [P, KD, P])
        hT = sb("hT", [P, KD, G])
        xbT = sb("xbT", [P, NC, TAPS - 1 + G])
        xbs = sb("xbs", [P, NC, STREAMS, TAPS - 1 + FRAMES])
        xcT = sb("xcT", [P, NC, G])
        ri = sb("ri", [P, 2, NC, G])
        aT = sb("aT", [P, NC, G])
        qT = sb("qT", [P, NC, G])
        gS = sb("gS", [P, NC, G])
        gt = sb("gt", [P, NC, G])
        sS = sb("sS", [P, NC, G])
        catT = sb("catT", [P, KD, G])
        vn = sb("vn", [P, GT, DA])
        g1b = sb("g1b", [P, D])
        g2b = sb("g2b", [P, D])
        lngb = sb("lngb", [P, DA])
        lnbb = sb("lnbb", [P, DA])
        bsb = sb("bsb", [P, NC, P])
        wsT = sb("wsT", [P, NC, P])
        wsTs = sb("wsTs", [P, NC, P])
        wgate = sb("wgate", [P, 2, NC, P])
        rw = sb("rw", [P, KD, NG + NE])
        rb = sb("rb", [P, NG + NE])
        ident = sb("ident", [P, P])
        before = sb("before", [P, P])
        ones = sb("ones", [P, P])
        cw = sb("cw", [P, NC, TAPS])
        cb = sb("cb", [P, NC])
        nb = sb("nb", [P, 2, NC])
        lam = sb("lam", [P, NC])
        lamt = sb("lamt", [P, 3, NC])
        nsp = sb("nsp", [P, NC])
        hlast = sb("hlast", [P, NC])
        h0s = sb("h0s", [P, NC, STREAMS])
        mhalf = sb("mhalf", [P, NC])
        pad = sb("pad", [P, 64])
        ssq = sb("ssq", [P, 2 * GT])
        rstd = sb("rstd", [P, 2 * GT])
        vst = sb("vst", [P, GT, NC, 6])
        vmv = sb("vmv", [P, GT, NC, 2])
        vrs = sb("vrs", [P, GT, NC])
        gl = sb("gl", [P, GT, 8])
        el = sb("el", [P, GT, NE])
        m8 = sb("m8", [P, GT, 2, 8])
        i8 = sb("i8", [P, GT, 2, 8], U32)
        rf = sb("rf", [P, GT, 16])
        dv = sb("dv", [P, GT, 8])
        mk = sb("mk", [P, GT, NG])
        ein = sb("ein", [P, GT, EPG])
        hot = sb("hot", [P, GT, 3, NE])
        iota32 = sb("iota32", [P, NE])
        ebase = sb("ebase", [P, NE])
        tokf = sb("tokf", [P, 1])
        pcol = sb("pcol", [P, 1])
        count = sb("count", [P, NE])
        rk = sb("rk", [P, NE])
        rkj = sb("rkj", [P, NE])
        slotf = sb("slotf", [P, GT, 2])
        slot = sb("slot", [P, GT, 2], U32)
        pay = sb("pay", [P, GT, 2, 2], U32)
        nch = sb("nch", [P, NE])
        cend = sb("cend", [P, NE])
        ple = sb("ple", [P, 2, NE])
        pq = sb("pq", [P, 4])
        diag = sb("diag", [P, 2, P])
        plan = sb("plan", [1, 2 * P + 1], I32)
        idx_in = sb("idx_in", [HF, 2, 2], U32)
        idx_out = sb("idx_out", [HF, 2, 2], U32)
        o = 0
        wg_e = w_in[:, o:o + KD * DE].rearrange("p (k f) -> p k f", k=KD)
        o += KD * DE
        wu_e = w_in[:, o:o + KD * DE].rearrange("p (k f) -> p k f", k=KD)
        o += KD * DE
        wd_e = w_in[:, o:o + KE * D].rearrange("p (f d) -> p f d", f=KE)
        o += KE * D
        xg = w_in[0:HF, o:o + 2 * D].rearrange("p (h d) -> p h d", h=2)
        o += 2 * D
        ysb = w_in[0:HF, o:o + 2 * D].rearrange("p (h d) -> p h d", h=2)
        o = 0
        xTm = w_out[:, o:o + KD * CH].rearrange("p (k n) -> p k n", k=KD)
        o += KD * CH
        hTm = w_out[:, o:o + KE * CH].rearrange("p (k n) -> p k n", k=KE)
        o += KE * CH
        sg = w_out[:, o:o + KE * CH].rearrange("p (k n) -> p k n", k=KE)
        o += KE * CH
        yT = w_out[:, o:o + KD * CH].rearrange("p (k n) -> p k n", k=KD)
        tinit = aT[:].rearrange("p a b -> p (a b)")[:, 0:2 * CH].bitcast(U32).rearrange("p (n t) -> p n t", t=2)
        zrow = qT[:].rearrange("p a b -> p (a b)")
        fb = [xa[:, 0], xa[:, 1], xr[:, 0], xr[:, 1]]

        ps = [ctx.enter_context(nc.psum_tensor(f"ps{b}", [P, BANK], F32)) for b in range(BANKS)]

        psum_full = [sem(f"psum_full{b}") for b in range(BANKS)]
        psum_read = [sem(f"psum_read{b}") for b in range(BANKS)]
        const_w1 = sem("const_w1")
        const_w2 = sem("const_w2")
        const_dma = sem("const_dma")
        const_dve = sem("const_dve")
        const_pool = sem("const_pool")
        pool_link = sem("pool_link")
        act_link = sem("act_link")
        table_ready = sem("table_ready")
        xa_loaded = [sem(f"xa_loaded{t}") for t in range(GT)]
        xr_loaded = [sem(f"xr_loaded{t}") for t in range(GT)]
        sq_ready = sem("sq_ready")
        rs_ready = sem("rs_ready")
        rs_link = sem("rs_link")
        xn_ready = sem("xn_ready")
        halo_ready = sem("halo_ready")
        xc_ready = sem("xc_ready")
        var_ready = sem("var_ready")
        vrs_ready = sem("vrs_ready")
        vrs_link = sem("vrs_link")
        vn_ready = sem("vn_ready")
        sig_ready = sem("sig_ready")
        at_ready = sem("at_ready")
        q_ready = sem("q_ready")
        gain_ready = sem("gain_ready")
        gin_ready = sem("gin_ready")
        gth_ready = sem("gth_ready")
        h_ready = sem("h_ready")
        cat_ready = sem("cat_ready")
        acc_stored = [sem(f"acc_stored{t}") for t in range(GT)]
        h2_ready = [sem(f"h2_ready{t}") for t in range(GT)]
        h2_stored = [sem(f"h2_stored{t}") for t in range(GT)]
        dv_ready = sem("dv_ready")
        dve_exp = sem("dve_exp")
        hot_ready = sem("hot_ready")
        slot_ready = sem("slot_ready")
        scattered = sem("scattered")
        pay_free = sem("pay_free")
        state_out = sem("state_out")
        dve_main = sem("dve_main")
        dve_choose = sem("dve_choose")
        dve_assign = sem("dve_assign")
        count_ready = sem("count_ready")
        dve_plan = sem("dve_plan")
        diag_ready = sem("diag_ready")
        plan_ready = sem("plan_ready")
        w_loaded = [sem(f"w_loaded{i}") for i in range(4)]
        ix_loaded = sem("ix_loaded")
        io_loaded = sem("io_loaded")
        xg_loaded = sem("xg_loaded")
        sg_ready = sem("sg_ready")
        y_added = sem("y_added")
        moe_done = sem("moe_done")
        moe_carry = sem("moe_carry")
        fg_loaded = sem("fg_loaded")
        f_loaded = [sem(f"f_loaded{b}") for b in range(4)]
        f_sq = sem("f_sq")
        f_link = sem("f_link")
        f_rs = sem("f_rs")
        f_ready = sem("f_ready")
        f_stored = [sem(f"f_stored{b}") for b in range(4)]

        def wait(eng, s, value):
            if not (isinstance(value, int) and value <= 0):
                eng.wait_ge(s, value)

        def wait_full(eng, seg, it, job):
            eng.wait_ge(psum_full[JOBS.bank(seg, job)], JOBS.before(seg, it, job) + 1)
            return ps[JOBS.bank(seg, job)]

        def wait_free(eng, seg, it, job):
            wait(eng, psum_read[JOBS.bank(seg, job)], JOBS.before(seg, it, job))
            return ps[JOBS.bank(seg, job)]

        def wait_out(eng, seg, it, job):
            eng.wait_ge(psum_read[JOBS.bank(seg, job)], JOBS.before(seg, it, job) + 1)

        def full(seg, job):
            return psum_full[JOBS.bank(seg, job)]

        def read(seg, job):
            return psum_read[JOBS.bank(seg, job)]

        pads = iter(range(64))

        def carry(eng):
            n = next(pads)
            return eng.tensor_tensor(pad[:, n:n + 1], mhalf[:, 0:1], mhalf[:, 0:1], ALU.mult)

        N_CONST = 19
        block = ctx.enter_context(nc.Block())

        @block.sync
        def _(sp):
            def load_x(g, t, dst, s):
                sp.dma_start(dst[:, t], a["x"].rearrange("(n p) d -> n p d", p=P)[bass.ds(g * GT + t, 1)]
                             .rearrange("a p d -> p (a d)")).then_inc(s[t], 16)

            for t in range(GT):
                load_x(0, t, xa, xa_loaded)
            small = [
                (g1b[:], a["norm1_g"].broadcast_to([P, D])),
                (cw[:], a["conv_w"]), (cb[:], a["conv_b"]), (lam[:], a["lam"]),
                (nb[:], a["gate_b"]), (h0s[:], a["h0"]),
                (xbs[:, :, :, 0:TAPS - 1], a["conv_state"]),
                (lngb[:], a["ln_g"].broadcast_to([P, DA])), (lnbb[:], a["ln_b"].broadcast_to([P, DA])),
                (bsb[:], a["b_s"].rearrange("a (g t) -> a g t", g=NC).broadcast_to([P, NC, P])),
                (wsT[:], a["w_sT"].rearrange("g s t -> s g t")),
                (g2b[:], a["norm2_g"].broadcast_to([P, D])),
                (rb[:], a["router_b"].broadcast_to([P, NG + NE])),
                (rw[:, :, 0:NG], a["router_gw"].rearrange("(k p) n -> p k n", p=P)),
                (rw[:, :, NG:NG + NE], a["router_ew"].rearrange("(k p) n -> p k n", p=P)),
            ]
            for dst, src in small[:7]:
                sp.dma_start(dst, src).then_inc(const_dma, 16)
            win = a["w_in"].rearrange("(k p) n -> p k n", p=P)
            for lo in (2 * DA, DA, 3 * DA, 0):
                sp.dma_start(w_in_v[:, :, lo:lo + DA], win[:, :, lo:lo + DA]).then_inc(const_w1, 16)
            for dst, src in small[7:]:
                sp.dma_start(dst, src).then_inc(const_dma, 16)
            for t in range(GT):
                load_x(0, t, xr, xr_loaded)
            sp.dma_start(w_out_v, a["w_out"].rearrange("(k p) n -> p k n", p=P)).then_inc(const_w2, 16)
            sp.wait_ge(const_dve, 2)
            for m in range(2):
                for half in range(2):
                    r = slice(64 * half, 64 * half + 64)
                    sp.dma_start(wgate[r, m, :, 64 * half:64 * half + 64],
                                 a["lru_w"][m].rearrange("(c h) i j -> h i c j", h=2)[half]).then_inc(const_dma, 16)
            for s in range(STREAMS):
                r = slice(FRAMES * s, FRAMES * (s + 1))
                sp.dma_start(wsTs[r, :, FRAMES * s:FRAMES * (s + 1)],
                             a["w_sT"].rearrange("g s t -> s g t")[0:FRAMES, :, 0:FRAMES]).then_inc(const_w2, 16)
            sp.wait_ge(const_pool, 5)
            tv = table.rearrange("(q p n) c -> q p (n c)", p=NE * CPE // 4, n=CH)
            for q in range(4):
                sp.dma_start(tv[q], tinit[0:NE * CPE // 4].rearrange("p n t -> p (n t)")).then_inc(table_ready, 16)
            sp.wait_ge(const_dve, 3)
            for dst in (acc, h2_rows):
                for h in range(2):
                    r = NTOK + HF * h
                    sp.dma_start(dst[r:r + HF], zrow[0:HF]).then_inc(table_ready, 16)

            def rows(dst, g, t):
                n = g * GT + t
                return dst[0:NTOK].rearrange("(n p) d -> n p d", p=P)[bass.ds(n, 1)].rearrange("a p d -> p (a d)")

            def group(seg, g, nxt):
                it = g - 1 if seg == "loop" else 0
                for t in range(nxt):
                    if t == 0:
                        wait_full(sp, seg, it, "xT3")
                    load_x(g + 1, t, xa, xa_loaded)
                for t in range(GT if seg != "last" else 1):
                    wait_out(sp, seg, it, f"o{t}1")
                    sp.dma_start(rows(acc, g, t), xr[:, t]).then_inc(acc_stored[t], 16)
                for t in range(GT if seg != "last" else 1):
                    sp.wait_ge(h2_ready[t], g + 1)
                    sp.dma_start(rows(h2_rows, g, t), xr[:, t]).then_inc(h2_stored[t], 16)

            def next_xr(seg, g, tiles):
                for t in range(tiles):
                    sp.wait_ge(h2_stored[t], 16 * g)
                    wait_full(sp, seg, g - 1 if seg == "loop" else 0, f"h2T{t}b")
                    load_x(g, t, xr, xr_loaded)

            group("first", 0, GT)
            with sp.Fori(1, NPG - 1) as g:
                next_xr("loop", g, GT)
                group("loop", g, GT)
            next_xr("loop", NPG - 1, GT)
            group("loop", NPG - 1, 1)
            sp.wait_ge(halo_ready, 1 + NPG)
            sp.dma_start(a["conv_p"], xbT[:, :, 0:TAPS - 1]).then_inc(state_out, 16)
            sp.wait_ge(h_ready, NPG)
            sp.dma_start(a["h_p"], hlast[:]).then_inc(state_out, 16)
            next_xr("last", NPG, 1)
            sp.wait_ge(vn_ready, GT * NPG + 1)
            sp.dma_start(a["v_s"], vn[:, 0]).then_inc(state_out, 16)
            wait_out(sp, "last", 0, "xb1")
            for c in range(NC):
                sp.dma_start(a["conv_s"][:, c], xbs[:, c, :, FRAMES:FRAMES + TAPS - 1]).then_inc(state_out, 16)
            sp.wait_ge(h_ready, NPG + 1)
            sp.dma_start(a["h_s"], h0s[:]).then_inc(state_out, 16)
            wait_full(sp, "last", 0, "u1")

            def weights(e, piece):
                wgd = a["w_gate"].rearrange("e (k p) f -> e p k f", p=P)
                wud = a["w_up"].rearrange("e (k p) f -> e p k f", p=P)
                wdd = a["w_down"].rearrange("e (f p) d -> e p f d", p=P)

                def at(x, lo, hi):
                    return x[bass.ds(e, 1)].rearrange("a p k f -> p (a k) f")[:, :, lo:hi]

                if piece < 2:
                    lo, hi = DE // 2 * piece, DE // 2 * (piece + 1)
                    sp.dma_start(wg_e[:, :, lo:hi], at(wgd, lo, hi)).then_inc(w_loaded[piece], 16)
                    sp.dma_start(wu_e[:, :, lo:hi], at(wud, lo, hi)).then_inc(w_loaded[piece], 16)
                else:
                    lo, hi = ((0, 6 * P), (6 * P, D))[piece - 2]
                    sp.dma_start(wd_e[:, :, lo:hi], at(wdd, lo, hi)).then_inc(w_loaded[piece], 16)

            for piece in range(4):
                weights(0, piece)
            group("last", NPG, 0)
            wait_out(sp, "plan", 0, "plan")
            chunks = sp.value_load(plan[0:1, 2 * P:2 * P + 1], min_val=2, max_val=P - 1)
            with sp.Fori(1, chunks) as q:
                e = sp.value_load(plan[0:1, bass.ds(q, 1)], min_val=0, max_val=NE - 1)
                for piece, job in enumerate(("gu1", "gu3", "y1", "y2")):
                    wait_full(sp, "chunk", q - 1, job)
                    weights(e, piece)
            wait_full(sp, "last", 0, "xT3")
            sp.wait_ge(xn_ready, GT * NPG + 1)
            sp.dma_start(g1b[:], a["final_g"].broadcast_to([P, D])).then_inc(fg_loaded, 16)
            sp.wait_ge(moe_done, 1)

            def load_f(it, b):
                wait(sp, f_stored[b], 16 * it)
                sp.dma_start(fb[b], acc[0:NTOK].rearrange("(n p) d -> n p d", p=P)[bass.ds(it * 4 + b, 1)]
                             .rearrange("a p d -> p (a d)")).then_inc(f_loaded[b], 16)

            for b in range(4):
                load_f(0, b)
            with sp.Fori(1, NTILE // 4) as it:
                for b in range(4):
                    load_f(it, b)
            load_f(NTILE // 4, 0)
            sp.wait_ge(state_out, 16 * (NC + 4))
            for t in range(GT):
                n = NPG + (t == 0)
                sp.wait_ge(acc_stored[t], 16 * n)
                sp.wait_ge(h2_stored[t], 16 * n)
            for b in range(4):
                sp.wait_ge(f_stored[b], 16 * (NTILE // 4 + (b == 0)))

        @block.gpsimd
        def _(pool):
            def made(ins, s=const_pool):
                ins.then_inc(s, 1)

            pool.nop().then_inc(pay_free, 1)
            nc.gpsimd.memset(ident[:], 0.0).then_inc(pool_link, 1)
            nc.gpsimd.memset(before[:], 1.0).then_inc(pool_link, 1)
            nc.gpsimd.memset(mhalf[:], -0.5).then_inc(pool_link, 1)
            pool.wait_ge(pool_link, 3)
            made(nc.gpsimd.affine_select(out=ident[:], in_=ident[:], compare_op=ALU.not_equal, fill=1.0, base=0,
                                         pattern=[[-1, P]], channel_multiplier=1))
            made(nc.gpsimd.affine_select(out=before[:], in_=before[:], compare_op=ALU.is_gt, fill=0.0, base=0,
                                         pattern=[[1, P]], channel_multiplier=-1))
            nc.gpsimd.memset(tinit, 0).then_inc(pool_link, 1)
            pool.wait_ge(pool_link, 4)
            made(nc.gpsimd.iota(tinit[:, :, 0], [[1, CH]], base=NTOK, channel_multiplier=0))
            made(nc.gpsimd.iota(iota32[:], [[1, NE]], base=0, channel_multiplier=0,
                                allow_small_or_imprecise_dtypes=True))
            made(nc.gpsimd.iota(ebase[:], [[SLOTS, NE]], base=0, channel_multiplier=0,
                                allow_small_or_imprecise_dtypes=True))
            made(nc.gpsimd.iota(pcol[:], [[0, 1]], base=0, channel_multiplier=1,
                                allow_small_or_imprecise_dtypes=True))
            made(nc.gpsimd.iota(tokf[:], [[0, 1]], base=0, channel_multiplier=1,
                                allow_small_or_imprecise_dtypes=True))
            pool.wait_ge(const_dma, 16 * N_CONST)
            pool.wait_ge(const_w2, 16 * (1 + STREAMS))
            made(nc.gpsimd.affine_select(out=wsT[:], in_=wsT[:], compare_op=ALU.is_ge, fill=0.0, base=0,
                                         pattern=[[0, NC], [1, P]], channel_multiplier=-1))
            made(nc.gpsimd.affine_select(out=wsTs[:], in_=wsTs[:], compare_op=ALU.is_ge, fill=0.0, base=0,
                                         pattern=[[0, NC], [1, P]], channel_multiplier=-1))

            def root(i, n, link_n, src=None):
                carry(pool)
                nc.gpsimd.tensor_scalar(rstd[:, i:i + 1], ssq[:, i:i + 1], 1.0 / D, EPS, ALU.mult,
                                        ALU.add).then_inc(rs_link, 1)
                pool.wait_ge(rs_link, link_n)
                nc.gpsimd.tensor_tensor(rstd[:, i:i + 1], rstd[:, i:i + 1], mhalf[:, 0:1], ALU.pow).then_inc(rs_ready, 1)

            def scatter(n, t):
                pool.wait_ge(slot_ready, n + 1)
                carry(pool)
                for k in range(2):
                    pool.indirect_dma_start(table, bass.IndirectOffsetOnAxis(ap=slot[:, t, k:k + 1], axis=0),
                                            pay[:, t, k, :], None).then_inc(scattered, 16)

            def group(g, tiles, prev):
                for t in range(tiles):
                    k = g * 2 * GT + t
                    pool.wait_ge(sq_ready, k + 1)
                    root(t, k + 1, k + 1)
                for t in range(tiles):
                    pool.wait_ge(var_ready, g * GT + t + 1)
                    carry(pool)
                    nc.gpsimd.tensor_scalar(vrs[:, t], vmv[:, t, :, 1], EPS, None, ALU.add).then_inc(vrs_link, 1)
                    pool.wait_ge(vrs_link, g * GT + t + 1)
                    nc.gpsimd.tensor_tensor(vrs[:, t], vrs[:, t], mhalf[:], ALU.pow).then_inc(vrs_ready, 1)
                for t in range(prev):
                    scatter((g - 1) * GT + t, t)
                for t in range(tiles):
                    k = g * 2 * GT + tiles + t
                    pool.wait_ge(sq_ready, k + 1)
                    root(GT + t, k + 1, k + 1)
                if prev:
                    pool.wait_ge(scattered, 16 * 2 * GT * g)
                    pool.nop().then_inc(pay_free, 1)

            group(0, GT, 0)
            pool.wait_ge(table_ready, 16 * 8)
            with pool.Fori(1, NPG) as g:
                group(g, GT, GT)
            group(NPG, 1, GT)
            scatter(GT * NPG, 0)

            pool.wait_ge(scattered, 16 * 2 * NTILE)
            wait_out(pool, "plan", 0, "plan")
            chunks = pool.value_load(plan[0:1, 2 * P:2 * P + 1], min_val=2, max_val=P - 1)

            def load_index(q, dst, s):
                row = pool.value_load(plan[0:1, bass.ds(q + P, 1)], min_val=0, max_val=NE * SLOTS - CH)
                pool.dma_start(dst[:], table[bass.ds(row, CH)].rearrange("(h p) c -> p h c", h=2)).then_inc(s, 16)

            def gather():
                for h in range(2):
                    pool.indirect_dma_start(xg[:, h, :], None, h2_rows,
                                            bass.IndirectOffsetOnAxis(ap=idx_in[:, h, 0:1], axis=0)).then_inc(xg_loaded, 16)

            for t in range(GT):
                pool.wait_ge(h2_stored[t], 16 * (NPG + (t == 0)))
                pool.wait_ge(acc_stored[t], 16 * (NPG + (t == 0)))
            wait_full(pool, "last", 0, "o01")
            load_index(0, idx_in, ix_loaded)
            pool.wait_ge(ix_loaded, 16)
            gather()
            wait_full(pool, "pre", 0, "xT2")
            pool.nop().then_inc(moe_carry, 1)
            with pool.Fori(0, chunks) as q:
                pool.wait_ge(xg_loaded, 32 * q + 32)
                load_index(q + 1, idx_in, ix_loaded)
                load_index(q, idx_out, io_loaded)
                pool.wait_ge(ix_loaded, 16 * q + 32)
                pool.wait_ge(moe_carry, 2 * q + 1)
                carry(pool).then_inc(moe_carry, 1)
                gather()
                wait_out(pool, "chunk", q, "r10")
                wait_out(pool, "chunk", q, "r11")
                pool.wait_ge(io_loaded, 16 * q + 16)
                pool.wait_ge(moe_carry, 2 * q + 2)
                carry(pool).then_inc(moe_carry, 1)
                for h in range(2):
                    pool.indirect_dma_start(acc, bass.IndirectOffsetOnAxis(ap=idx_out[:, h, 0:1], axis=0),
                                            ysb[:, h, :], None, compute_op=ALU.add).then_inc(y_added, 16)
                wait_full(pool, "chunk", q, "xT2")
                pool.wait_ge(y_added, 32 * q + 32)
            pool.wait_ge(xg_loaded, 32 * chunks + 32)
            pool.nop().then_inc(moe_done, 1)

            def final(it, b):
                k = it * 4 + b
                pool.wait_ge(f_sq, k + 2)
                carry(pool)
                nc.gpsimd.tensor_scalar(rstd[:, b:b + 1], ssq[:, b:b + 1], 1.0 / D, EPS, ALU.mult,
                                        ALU.add).then_inc(f_link, 1)
                pool.wait_ge(f_link, k + 1)
                nc.gpsimd.tensor_tensor(rstd[:, b:b + 1], rstd[:, b:b + 1], mhalf[:, 0:1], ALU.pow).then_inc(f_rs, 1)

            with pool.Fori(0, NTILE // 4) as it:
                for b in range(4):
                    final(it, b)
            final(NTILE // 4, 0)

        @block.tensor
        def _(pe):
            def group(seg, it, g, tiles, prev):
                n = tiles * P
                pe.wait_ge(xn_ready, g * GT + tiles)
                for j in range(4):
                    bank = wait_free(pe, seg, it, f"xT{j}")
                    for kk in range(2):
                        for t in range(tiles):
                            mm = pe.transpose(bank[:, kk * n + t * P:kk * n + (t + 1) * P],
                                              xa[:, t, (2 * j + kk) * P:(2 * j + kk + 1) * P], ident[:])
                    mm.then_inc(full(seg, f"xT{j}"), 1)

                def channels(kind, lo, p):
                    bank = wait_free(pe, seg, it, f"{kind}{p}")
                    for cc in range(2):
                        col = lo + (2 * p + cc) * P
                        for k in range(KD):
                            mm = pe.matmul(bank[:, cc * n:(cc + 1) * n], w_in_v[:, k, col:col + P], hT[:, k, 0:n],
                                           start=(k == 0), stop=(k == KD - 1))
                    mm.then_inc(full(seg, f"{kind}{p}"), 1)

                wait_out(pe, seg, it, "xT3")
                if seg == "first":
                    pe.wait_ge(const_w1, 16 * 4)
                for p in range(2):
                    channels("xb", 2 * DA, p)
                for t in range(prev):
                    route(seg, it, t, g - 1)
                for t in range(tiles):
                    bank = wait_free(pe, seg, it, f"v{t}")
                    for k in range(KD):
                        mm = pe.matmul(bank[:, :], hT[:, k, t * P:(t + 1) * P], w_in_v[:, k, DA:2 * DA],
                                       start=(k == 0), stop=(k == KD - 1))
                    mm.then_inc(full(seg, f"v{t}"), 1)
                for c in range(NC):
                    bank = wait_free(pe, seg, it, f"ga{c}")
                    pe.wait_ge(xc_ready, NC * g + c + 1)
                    for m in range(2):
                        mm = pe.matmul(bank[:, m * n:(m + 1) * n], wgate[:, m, c, :], xcT[:, c, 0:n], start=True, stop=True)
                    mm.then_inc(full(seg, f"ga{c}"), 1)
                if prev:
                    places(seg, it, prev, g - 1)
                for p in range(2):
                    channels("gg", 3 * DA, p)
                for t in range(tiles):
                    bank = wait_free(pe, seg, it, f"s{t}")
                    pe.wait_ge(vn_ready, g * GT + t + 1)
                    ws = wsTs if seg == "last" else wsT
                    for c in range(NC):
                        mm = pe.matmul(bank[:, c * P:(c + 1) * P], vn[:, t, c * P:(c + 1) * P], ws[:, c, :],
                                       start=True, stop=True)
                    mm.then_inc(full(seg, f"s{t}"), 1)
                for p in range(2):
                    channels("u", 0, p)
                wait_out(pe, seg, it, "u1")
                pe.wait_ge(cat_ready, g + 1)
                for t in range(tiles):
                    for h in range(2):
                        bank = wait_free(pe, seg, it, f"o{t}{h}")
                        for k in range(KD):
                            mm = pe.matmul(bank[:, :], catT[:, k, t * P:(t + 1) * P],
                                           w_out_v[:, k, h * BANK:(h + 1) * BANK], start=(k == 0), stop=(k == KD - 1))
                        mm.then_inc(full(seg, f"o{t}{h}"), 1)

            def route(seg, it, t, gp):
                pe.wait_ge(h2_ready[t], gp + 1)
                for i, half in enumerate("ab"):
                    bank = wait_free(pe, seg, it, f"h2T{t}{half}")
                    for k in range(4):
                        kk = 4 * i + k
                        mm = pe.transpose(bank[:, k * P:(k + 1) * P], xr[:, t, kk * P:(kk + 1) * P], ident[:])
                    mm.then_inc(full(seg, f"h2T{t}{half}"), 1)
                bank = wait_free(pe, seg, it, f"lg{t}")
                wait_out(pe, seg, it, f"h2T{t}b")
                for k in range(KD):
                    mm = pe.matmul(bank[:, 0:NG + NE], h2T[:, k, :], rw[:, k, :], start=(k == 0), stop=(k == KD - 1))
                mm.then_inc(full(seg, f"lg{t}"), 1)

            def places(seg, it, tiles, gp):
                bank = wait_free(pe, seg, it, "pf")
                for t in range(tiles):
                    pe.wait_ge(hot_ready, gp * GT + t + 1)
                    pe.matmul(bank[:, 64 * t:64 * t + NE], before[:], hot[:, t, 2, :], start=True, stop=True)
                    mm = pe.matmul(bank[:, 64 * t + NE:64 * t + 2 * NE], ones[:], hot[:, t, 2, :], start=True, stop=True)
                mm.then_inc(full(seg, "pf"), 1)

            pe.wait_ge(const_pool, 9)
            pe.wait_ge(const_dma, 16 * N_CONST)
            pe.wait_ge(const_w2, 16 * (1 + STREAMS))
            pe.wait_ge(const_dve, 5)
            group("first", 0, 0, GT, 0)
            with pe.Fori(1, NPG) as g:
                group("loop", g - 1, g, GT, GT)
            group("last", 0, NPG, 1, GT)
            route("tail", 0, 0, NPG)
            places("tail", 0, 1, NPG)
            bank = wait_free(pe, "plan", 0, "plan")
            pe.wait_ge(diag_ready, 1)
            for i in range(2):
                mm = pe.matmul(bank[:, i * P:(i + 1) * P], ones[:], diag[:, i, :], start=True, stop=True)
            mm.then_inc(full("plan", "plan"), 1)

            def columns(seg, q, n):
                pe.wait_ge(xg_loaded, 32 * n + 32)
                for j, (lo, hi) in enumerate(XT3):
                    bank = wait_free(pe, seg, q, f"xT{j}")
                    for k in range(lo, hi):
                        for h in range(2):
                            at = (k - lo) * CH + h * HF
                            mm = pe.transpose(bank[:, at:at + HF], xg[:, h, k * P:(k + 1) * P], ident[0:HF, 0:HF])
                    mm.then_inc(full(seg, f"xT{j}"), 1)

            wait_out(pe, "plan", 0, "plan")
            chunks = pe.value_load(plan[0:1, 2 * P:2 * P + 1], min_val=2, max_val=P - 1)
            columns("pre", 0, 0)
            wait_out(pe, "pre", 0, "xT2")
            with pe.Fori(0, chunks) as q:
                for f in range(KE):
                    bank = wait_free(pe, "chunk", q, f"gu{f}")
                    if f % 2 == 0:
                        pe.wait_ge(w_loaded[f // 2], 32 * q + 32)
                    for m, w in enumerate((wg_e, wu_e)):
                        for k in range(KD):
                            mm = pe.matmul(bank[:, m * CH:(m + 1) * CH], w[:, k, f * P:(f + 1) * P], xTm[:, k, :],
                                           start=(k == 0), stop=(k == KD - 1))
                    mm.then_inc(full("chunk", f"gu{f}"), 1)
                columns("chunk", q, q + 1)
                wait_out(pe, "chunk", q, f"gu{KE - 1}")
                for j, (lo, hi) in enumerate(XT3):
                    bank = wait_free(pe, "chunk", q, f"y{j}")
                    if j != 1:
                        pe.wait_ge(w_loaded[2 + j // 2], 16 * q + 16)
                    for d in range(lo, hi):
                        for f in range(KE):
                            mm = pe.matmul(bank[:, (d - lo) * CH:(d - lo + 1) * CH], wd_e[:, f, d * P:(d + 1) * P],
                                           hTm[:, f, :], start=(f == 0), stop=(f == KE - 1))
                    mm.then_inc(full("chunk", f"y{j}"), 1)
                for i in range(2):
                    wait_out(pe, "chunk", q, f"y{1 + i}")
                    for h in range(2):
                        bank = wait_free(pe, "chunk", q, f"r{i}{h}")
                        for d in range(4):
                            mm = pe.transpose(bank[0:HF, d * P:(d + 1) * P], yT[:, 4 * i + d, h * HF:(h + 1) * HF], ident[:])
                        mm.then_inc(full("chunk", f"r{i}{h}"), 1)
                wait_out(pe, "chunk", q, "xT2")

        @block.scalar
        def _(act):
            def copy_out(seg, it, job, dst, width, s):
                bank = wait_full(act, seg, it, job)
                nc.scalar.copy(dst, bank[:, 0:width]).then_inc(read(seg, job), 1)

            act.wait_ge(const_dma, 16 * N_CONST)
            nc.scalar.activation(lamt[:, 0], lam[:], ACT.Relu, scale=-1.0).then_inc(act_link, 1)
            nc.scalar.activation(lamt[:, 1], lam[:], ACT.Abs).then_inc(act_link, 1)
            act.wait_ge(act_link, 2)
            nc.scalar.activation(lamt[:, 1], lamt[:, 1], ACT.Exp, scale=-1.0).then_inc(act_link, 1)
            act.wait_ge(act_link, 3)
            act.wait_ge(const_dve, 4)
            nc.scalar.activation(lamt[:, 2], lamt[:, 1], ACT.Ln, bias=ones[:, 0:1]).then_inc(act_link, 1)

            def h2_columns(seg, it, t, gp, sq_n):
                act.wait_ge(sq_ready, sq_n)
                for i, half in enumerate("ab"):
                    bank = wait_full(act, seg, it, f"h2T{t}{half}")
                    nc.scalar.copy(h2T[:, 4 * i:4 * i + 4, :], bank[:, :].rearrange("p (k n) -> p k n", k=4))\
                        .then_inc(read(seg, f"h2T{t}{half}"), 1)

            def router_exp(t, gp):
                act.wait_ge(dv_ready, gp * GT + t + 1)
                nc.scalar.activation(dv[:, t, 0:NG + 1], dv[:, t, 0:NG + 1], ACT.Exp).then_inc(dve_exp, 1)

            def group(seg, it, g, tiles, prev):
                n = tiles * P
                for t in range(tiles):
                    act.wait_ge(xa_loaded[t], 16 * g + 16)
                    wait(act, sq_ready, g * 2 * GT + t)
                    nc.scalar.activation(h2T[:].rearrange("p a b -> p (a b)"), xa[:, t], ACT.Square,
                                         accum_out=ssq[:, t:t + 1]).then_inc(sq_ready, 1)
                for j in range(4):
                    bank = wait_full(act, seg, it, f"xT{j}")
                    nc.scalar.copy(hT[:, 2 * j:2 * j + 2, 0:n], bank[:, 0:2 * n].rearrange("p (k n) -> p k n", k=2))\
                        .then_inc(read(seg, f"xT{j}"), 1)
                act.wait_ge(halo_ready, g + 1)
                for p in range(2):
                    bank = wait_full(act, seg, it, f"xb{p}")
                    if seg == "last":
                        for cc in range(2):
                            ins = nc.scalar.copy(xbs[:, 2 * p + cc, :, TAPS - 1:],
                                                 bank[:, cc * n:(cc + 1) * n].rearrange("p (s f) -> p s f", f=FRAMES))
                    else:
                        ins = nc.scalar.copy(xbT[:, 2 * p:2 * p + 2, TAPS - 1:],
                                             bank[:, 0:2 * n].rearrange("p (c n) -> p c n", c=2))
                    ins.then_inc(read(seg, f"xb{p}"), 1)
                for t in range(prev):
                    h2_columns(seg, it, t, g - 1, g * 2 * GT + tiles)
                for c in range(NC):
                    bank = wait_full(act, seg, it, f"ga{c}")
                    for m in range(2):
                        ins = nc.scalar.activation(ri[:, m, c, 0:n], bank[:, m * n:(m + 1) * n], ACT.Exp,
                                                   bias=nb[:, m, c:c + 1], scale=-1.0)
                    ins.then_inc(read(seg, f"ga{c}"), 1)
                for t in range(prev):
                    router_exp(t, g - 1)
                for c in range(NC):
                    act.wait_ge(sig_ready, NC * g + c + 1)
                    nc.scalar.activation(aT[:, c, 0:n], ri[:, 0, c, 0:n], ACT.Exp, scale=nsp[:, c:c + 1])
                    nc.scalar.activation(ri[:, 0, c, 0:n], ri[:, 0, c, 0:n], ACT.Tanh, scale=nsp[:, c:c + 1])\
                        .then_inc(at_ready, 1)
                for p in range(2):
                    bank = wait_full(act, seg, it, f"gg{p}")
                    v = bank[:, 0:2 * n].rearrange("p (c n) -> p c n", c=2)
                    nc.scalar.copy(gS[:, 2 * p:2 * p + 2, 0:n], v)
                    nc.scalar.activation(gt[:, 2 * p:2 * p + 2, 0:n], v, ACT.Square)\
                        .then_inc(read(seg, f"gg{p}"), 1)
                act.wait_ge(gin_ready, g + 1)
                nc.scalar.activation(gt[:, :, 0:n], gt[:, :, 0:n], ACT.Tanh, scale=GELU_C).then_inc(gth_ready, 1)
                act.wait_ge(q_ready, g + 1)
                nc.scalar.activation(qT[:, :, 0:n], qT[:, :, 0:n], ACT.Sqrt, scale=-1.0).then_inc(gain_ready, 1)
                for t in range(tiles):
                    wait_out(act, seg, it, f"o{t}1")
                    wait(act, sq_ready, g * 2 * GT + tiles + t)
                    nc.scalar.activation(h2T[:].rearrange("p a b -> p (a b)"), xr[:, t], ACT.Square,
                                         accum_out=ssq[:, GT + t:GT + t + 1]).then_inc(sq_ready, 1)

            group("first", 0, 0, GT, 0)
            with act.Fori(1, NPG) as g:
                group("loop", g - 1, g, GT, GT)
            group("last", 0, NPG, 1, GT)
            h2_columns("tail", 0, 0, NPG, NPG * 2 * GT + 2)
            router_exp(0, NPG)

            wait_out(act, "plan", 0, "plan")
            chunks = act.value_load(plan[0:1, 2 * P:2 * P + 1], min_val=2, max_val=P - 1)

            def x_columns(seg, q):
                for j, (lo, hi) in enumerate(XT3):
                    bank = wait_full(act, seg, q, f"xT{j}")
                    nc.scalar.copy(xTm[:, lo:hi, :], bank[:, 0:(hi - lo) * CH].rearrange("p (k n) -> p k n", n=CH))\
                        .then_inc(read(seg, f"xT{j}"), 1)

            x_columns("pre", 0)
            with act.Fori(0, chunks) as q:
                for f in range(KE):
                    bank = wait_full(act, "chunk", q, f"gu{f}")
                    nc.scalar.activation(sg[:, f, :], bank[:, 0:CH], ACT.Silu).then_inc(sg_ready, 1)
                x_columns("chunk", q)
                act.wait_ge(io_loaded, 16 * q + 16)
                for i in range(2):
                    bank = wait_full(act, "chunk", q, f"r{i}0")
                    nc.scalar.activation(ysb[:, 0, i * BANK:(i + 1) * BANK], bank[0:HF, :], ACT.Copy,
                                         scale=idx_out[:, 0, 1:2].bitcast(F32)).then_inc(read("chunk", f"r{i}0"), 1)

            def final(it, b):
                act.wait_ge(f_loaded[b], 16 * it + 16)
                act.wait_ge(f_sq, it * 4 + 1)
                unused = (catT[:, 0:4], catT[:, 4:8], gS[:], gt[:])[b]
                nc.scalar.activation(unused.rearrange("p a b -> p (a b)"), fb[b], ACT.Square,
                                     accum_out=ssq[:, b:b + 1]).then_inc(f_sq, 1)

            def store(it, b):
                act.wait_ge(f_ready, it * 4 + b + 1)
                act.dma_start(a["y"].rearrange("(n p) d -> n p d", p=P)[bass.ds(it * 4 + b, 1)]
                              .rearrange("a p d -> p (a d)"), fb[b]).then_inc(f_stored[b], 16)

            act.nop().then_inc(f_sq, 1)
            with act.Fori(0, NTILE // 4) as it:
                for b in range(4):
                    final(it, b)
                for b in range(4):
                    store(it, b)
            final(NTILE // 4, 0)
            store(NTILE // 4, 0)

        @block.vector
        def _(dve):
            V = nc.vector

            def linked(s):
                state = [0, 0]

                def start(base):
                    state[0], state[1] = base, 0

                def link(ins):
                    state[1] += 1
                    ins.then_inc(s, 1)
                    dve.wait_ge(s, state[0] + state[1])

                return start, link, state

            start_m, link, main = linked(dve_main)
            start_c, clink, choose_n = linked(dve_choose)
            start_a, alink, assign_n = linked(dve_assign)
            start_p, plink, plan_n = linked(dve_plan)

            V.memset(wgate[:], 0.0).then_inc(const_dve, 1)
            V.memset(wsTs[:], 0.0).then_inc(const_dve, 1)
            V.memset(zrow[:], 0.0).then_inc(const_dve, 1)
            V.memset(ones[:], 1.0).then_inc(const_dve, 1)
            V.memset(gl[:], -3.0e38).then_inc(const_dve, 1)
            V.memset(count[:], 0.0).then_inc(const_dve, 1)
            V.memset(hlast[:], 0.0).then_inc(const_dve, 1)
            V.memset(xbT[:, :, 0:TAPS - 1], 0.0).then_inc(halo_ready, 1)
            dve.wait_ge(const_dve, 7)
            dve.wait_ge(const_dma, 16 * N_CONST)
            dve.wait_ge(const_pool, 9)
            V.tensor_scalar(nb[:], nb[:], -1.0, None, ALU.mult).then_inc(const_dve, 1)
            dve.wait_ge(act_link, 4)
            V.tensor_tensor(lamt[:, 0], lamt[:, 0], lamt[:, 2], ALU.add).then_inc(const_dve, 1)
            dve.wait_ge(const_dve, 9)
            V.tensor_scalar(nsp[:], lamt[:, 0], -8.0, None, ALU.mult).then_inc(const_dve, 1)
            dve.wait_ge(table_ready, 16 * 8)

            MAIN, CHOOSE, ASSIGN = 26, 13, 9

            def group(seg, it, g, tiles, prev):
                n = tiles * P
                start_m(g * MAIN)
                for t in range(tiles):
                    dve.wait_ge(rs_ready, g * 2 * GT + t + 1)
                    V.scalar_tensor_tensor(out=xa[:, t], in0=xa[:, t], scalar=rstd[:, t:t + 1], in1=g1b[:],
                                           op0=ALU.mult, op1=ALU.mult).then_inc(xn_ready, 1)
                for c in range(NC):
                    if c % 2 == 0:
                        wait_out(dve, seg, it, f"xb{c // 2}")
                    if seg == "last":
                        src = [xbs[:, c, :, k:k + FRAMES] for k in range(TAPS)]
                        dst = xcT[:, c, 0:n].rearrange("p (s f) -> p s f", f=FRAMES)
                    else:
                        src = [xbT[:, c, k:k + n] for k in range(TAPS)]
                        dst = xcT[:, c, :]
                    link(V.tensor_scalar(dst, src[0], cw[:, c, 0:1], cb[:, c:c + 1], ALU.mult, ALU.add))
                    for k in range(1, TAPS):
                        ins = V.scalar_tensor_tensor(out=dst, in0=src[k], scalar=cw[:, c, k:k + 1], in1=dst,
                                                     op0=ALU.mult, op1=ALU.add)
                        if k < TAPS - 1:
                            link(ins)
                    ins.then_inc(xc_ready, 1)
                if seg != "last":
                    V.tensor_copy(xbT[:, :, 0:TAPS - 1], xbT[:, :, G:G + TAPS - 1]).then_inc(halo_ready, 1)
                for t in range(tiles):
                    bank = wait_full(dve, seg, it, f"v{t}")
                    for c in range(NC):
                        ins = V.bn_stats(vst[:, t, c, :], bank[:, c * P:(c + 1) * P])
                    link(ins)
                    carry(dve)
                    for c in range(NC):
                        ins = V.bn_aggr(vmv[:, t, c, :], vst[:, t, c, :])
                    ins.then_inc(var_ready, 1)
                    dve.wait_ge(vrs_ready, g * GT + t + 1)
                    for c in range(NC):
                        ins = V.tensor_scalar(vn[:, t, c * P:(c + 1) * P], bank[:, c * P:(c + 1) * P],
                                              vmv[:, t, c, 0:1], vrs[:, t, c:c + 1], ALU.subtract, ALU.mult)
                    ins.then_inc(read(seg, f"v{t}"), 1)
                    wait_out(dve, seg, it, f"v{t}")
                    link(V.tensor_tensor(vn[:, t], vn[:, t], lngb[:], ALU.mult))
                    V.tensor_tensor(vn[:, t], vn[:, t], lnbb[:], ALU.add).then_inc(vn_ready, 1)
                for t in range(prev):
                    choose(seg, it, t, g - 1)
                for c in range(NC):
                    wait_out(dve, seg, it, f"ga{c}")
                    v = ri[:, :, c, 0:n]
                    link(V.tensor_scalar(v, v, 1.0, None, ALU.add))
                    V.reciprocal(v, v).then_inc(sig_ready, 1)
                dve.wait_ge(sig_ready, NC * g + NC)
                iv, rv, av, qv = ri[:, 1, :, 0:n], ri[:, 0, :, 0:n], aT[:, :, 0:n], qT[:, :, 0:n]
                link(V.tensor_tensor(iv, iv, xcT[:, :, 0:n], ALU.mult))
                dve.wait_ge(at_ready, NC * g + NC)
                link(V.tensor_tensor(qv, av, av, ALU.mult))
                V.scalar_tensor_tensor(out=qv, in0=qv, scalar=1.0, in1=rv, op0=ALU.add, op1=ALU.mult).then_inc(q_ready, 1)
                wait_out(dve, seg, it, "gg1")
                gv, tv = gS[:, :, 0:n], gt[:, :, 0:n]
                link(V.tensor_scalar(tv, tv, 0.044715, 1.0, ALU.mult, ALU.add))
                V.tensor_tensor(tv, tv, gv, ALU.mult).then_inc(gin_ready, 1)
                dve.wait_ge(gain_ready, g + 1)
                link(V.tensor_tensor(iv, iv, qv, ALU.mult))
                for c in range(NC):
                    if seg == "last":
                        for s in range(STREAMS):
                            r = slice(FRAMES * s, FRAMES * (s + 1))
                            ins = V.tensor_tensor_scan(qT[:, c, r], aT[:, c, r], ri[:, 1, c, r], h0s[:, c, s:s + 1],
                                                       ALU.mult, ALU.add)
                    else:
                        ins = V.tensor_tensor_scan(qT[:, c, :], aT[:, c, :], ri[:, 1, c, :], hlast[:, c:c + 1],
                                                   ALU.mult, ALU.add)
                link(ins)
                if seg != "last":
                    V.tensor_copy(hlast[:], qT[:, :, G - 1]).then_inc(h_ready, 1)
                else:
                    V.tensor_copy(h0s[:], qT[:, :, FRAMES - 1:P:FRAMES]).then_inc(h_ready, 1)
                dve.wait_ge(gth_ready, g + 1)
                link(V.scalar_tensor_tensor(out=tv, in0=tv, scalar=1.0, in1=gv, op0=ALU.add, op1=ALU.mult))
                V.scalar_tensor_tensor(out=catT[:, NC:, 0:n], in0=tv, scalar=0.5, in1=qv, op0=ALU.mult,
                                       op1=ALU.mult).then_inc(cat_ready, 1)
                if prev:
                    assign(seg, it, prev, g - 1)
                for t in range(tiles):
                    bank = wait_full(dve, seg, it, f"s{t}")
                    if seg == "last":
                        for c in range(NC):
                            ins = V.tensor_tensor(
                                sS[:, c, 0:n].rearrange("p (s f) -> p s f", f=FRAMES),
                                bank[:, c * P:(c + 1) * P].rearrange("p (s f) -> p s f", f=FRAMES),
                                bsb[:, c:c + 1, 0:FRAMES].broadcast_to([P, STREAMS, FRAMES]), ALU.add)
                    else:
                        ins = V.tensor_tensor(sS[:, :, t * P:(t + 1) * P], bank[:, :].rearrange("p (c n) -> p c n", c=NC),
                                              bsb[:], ALU.add)
                    ins.then_inc(read(seg, f"s{t}"), 1)
                    wait_out(dve, seg, it, f"s{t}")
                for p in range(2):
                    bank = wait_full(dve, seg, it, f"u{p}")
                    V.tensor_tensor(catT[:, 2 * p:2 * p + 2, 0:n], bank[:, 0:2 * n].rearrange("p (c n) -> p c n", c=2),
                                    sS[:, 2 * p:2 * p + 2, 0:n], ALU.mult).then_inc(read(seg, f"u{p}"), 1)
                for t in range(tiles):
                    dve.wait_ge(xr_loaded[t], 16 * g + 16)
                    for h in range(2):
                        bank = wait_full(dve, seg, it, f"o{t}{h}")
                        x = xr[:, t, h * BANK:(h + 1) * BANK]
                        V.tensor_tensor(x, bank[:, :], x, ALU.add).then_inc(read(seg, f"o{t}{h}"), 1)
                for t in range(tiles):
                    dve.wait_ge(rs_ready, g * 2 * GT + tiles + t + 1)
                    dve.wait_ge(acc_stored[t], 16 * g + 16)
                    V.scalar_tensor_tensor(out=xr[:, t], in0=xr[:, t], scalar=rstd[:, GT + t:GT + t + 1], in1=g2b[:],
                                           op0=ALU.mult, op1=ALU.mult).then_inc(h2_ready[t], 1)
                if seg == "first":
                    assert main[1] == MAIN, main[1]

            def choose(seg, it, t, gp):
                start_c((gp * GT + t) * CHOOSE)
                bank = wait_full(dve, seg, it, f"lg{t}")
                V.tensor_tensor(gl[:, t, 0:NG], bank[:, 0:NG], rb[:, 0:NG], ALU.add)
                V.tensor_tensor(el[:, t], bank[:, NG:NG + NE], rb[:, NG:], ALU.add).then_inc(read(seg, f"lg{t}"), 1)
                wait_out(dve, seg, it, f"lg{t}")
                carry(dve)
                clink(V.max(m8[:, t, 0], gl[:, t]))
                carry(dve)
                clink(V.max_index(i8[:, t, 0], m8[:, t, 0], gl[:, t]))
                clink(V.tensor_copy(rf[:, t, 0:1], i8[:, t, 0, 0:1]))
                clink(V.tensor_scalar(mk[:, t], iota32[:, 0:NG], rf[:, t, 0:1], None, ALU.is_equal))
                clink(V.tensor_scalar(ein[:, t], el[:, t, 0:EPG], mk[:, t, 0:1], None, ALU.mult))
                for j in range(1, NG):
                    clink(V.scalar_tensor_tensor(out=ein[:, t], in0=el[:, t, j * EPG:(j + 1) * EPG],
                                                 scalar=mk[:, t, j:j + 1], in1=ein[:, t], op0=ALU.mult, op1=ALU.add))
                carry(dve)
                clink(V.max(m8[:, t, 1], ein[:, t]))
                carry(dve)
                clink(V.max_index(i8[:, t, 1], m8[:, t, 1], ein[:, t]))
                V.tensor_scalar(rf[:, t, 3:4], rf[:, t, 0:1], float(EPG), None, ALU.mult)
                clink(V.tensor_copy(rf[:, t, 1:3], i8[:, t, 1, 0:2]))
                clink(V.tensor_scalar(rf[:, t, 1:3], rf[:, t, 1:3], rf[:, t, 3:4], None, ALU.add))
                V.tensor_scalar(hot[:, t, 0], iota32[:], rf[:, t, 1:2], None, ALU.is_equal)
                clink(V.tensor_scalar(hot[:, t, 1], iota32[:], rf[:, t, 2:3], None, ALU.is_equal))
                V.tensor_tensor(hot[:, t, 2], hot[:, t, 0], hot[:, t, 1], ALU.add).then_inc(hot_ready, 1)
                V.tensor_scalar(dv[:, t, 0:NG], gl[:, t, 0:NG], m8[:, t, 0, 0:1], None, ALU.subtract)
                V.tensor_tensor(dv[:, t, NG:NG + 1], m8[:, t, 1, 1:2], m8[:, t, 1, 0:1], ALU.subtract).then_inc(dv_ready, 1)
                assert choose_n[1] == CHOOSE, choose_n[1]

            def assign(seg, it, tiles, gp):
                bank = wait_full(dve, seg, it, "pf")
                for t in range(tiles):
                    start_a((gp * GT + t) * ASSIGN)
                    dve.wait_ge(pay_free, gp + 1)
                    dve.wait_ge(dve_exp, gp * GT + t + 1)
                    alink(V.reduce_sum(rf[:, t, 4:5], dv[:, t, 0:NG], AX.X))
                    alink(V.scalar_tensor_tensor(out=rf[:, t, 5:6], in0=dv[:, t, NG:NG + 1], scalar=1.0,
                                                 in1=rf[:, t, 4:5], op0=ALU.add, op1=ALU.mult))
                    alink(V.reciprocal(rf[:, t, 6:7], rf[:, t, 5:6]))
                    V.tensor_copy(pay[:, t, 0, 1:2].bitcast(F32), rf[:, t, 6:7])
                    alink(V.tensor_tensor(pay[:, t, 1, 1:2].bitcast(F32), rf[:, t, 6:7], dv[:, t, NG:NG + 1], ALU.mult))
                    V.tensor_copy(pay[:, t, 0, 0:1], tokf[:])
                    V.tensor_copy(pay[:, t, 1, 0:1], tokf[:])
                    alink(V.tensor_scalar(tokf[:], tokf[:], float(P), None, ALU.add))
                    alink(V.tensor_tensor(rk[:], bank[:, 64 * t:64 * t + NE], count[:], ALU.add))
                    alink(V.tensor_tensor(rk[:], rk[:], ebase[:], ALU.add))
                    for k in range(2):
                        alink(V.tensor_tensor_reduce(rkj[:], hot[:, t, k], rk[:], 1.0, 0.0, ALU.mult, ALU.add,
                                                     slotf[:, t, k:k + 1]))
                    V.tensor_copy(slot[:, t], slotf[:, t]).then_inc(slot_ready, 1)
                    ins = V.tensor_tensor(count[:], count[:], bank[:, 64 * t + NE:64 * t + 2 * NE], ALU.add)
                    if t < tiles - 1:
                        ins.then_inc(count_ready, 1)
                        dve.wait_ge(count_ready, gp + 1)
                    assert assign_n[1] == ASSIGN, assign_n[1]
                ins.then_inc(read(seg, "pf"), 1)
                wait_out(dve, seg, it, "pf")

            group("first", 0, 0, GT, 0)
            with dve.Fori(1, NPG) as g:
                group("loop", g - 1, g, GT, GT)
            group("last", 0, NPG, 1, GT)
            choose("tail", 0, 0, NPG)
            assign("tail", 0, 1, NPG)

            start_p(0)
            plink(V.tensor_scalar(nch[:], count[:], 0.0, None, ALU.is_gt))
            plink(V.memset(nch[:, 0:2], 1.0))
            for j in range(1, CPE):
                plink(V.scalar_tensor_tensor(out=nch[:], in0=count[:], scalar=float(j * CH), in1=nch[:],
                                             op0=ALU.is_gt, op1=ALU.add))
            plink(V.tensor_tensor_scan(cend[:], ones[:, 0:NE], nch[:], 0.0, ALU.mult, ALU.add))
            plink(V.tensor_scalar(ple[:, 0], cend[:], pcol[:, 0:1], None, ALU.is_le))
            plink(V.reduce_sum(pq[:, 0:1], ple[:, 0], AX.X))
            plink(V.tensor_tensor_reduce(ple[:, 1], ple[:, 0], nch[:], 1.0, 0.0, ALU.mult, ALU.add, pq[:, 1:2]))
            plink(V.tensor_scalar(pq[:, 0:1], pq[:, 0:1], float(NE - 1), None, ALU.min))
            plink(V.tensor_tensor(pq[:, 1:2], pcol[:], pq[:, 1:2], ALU.subtract))
            plink(V.tensor_scalar(pq[:, 1:2], pq[:, 1:2], float(CPE - 1), float(CH), ALU.min, ALU.mult))
            plink(V.tensor_scalar(pq[:, 2:3], pq[:, 0:1], float(SLOTS), None, ALU.mult))
            plink(V.tensor_tensor(pq[:, 1:2], pq[:, 1:2], pq[:, 2:3], ALU.add))
            V.tensor_scalar(diag[:, 0], ident[:], pq[:, 0:1], None, ALU.mult)
            V.tensor_scalar(diag[:, 1], ident[:], pq[:, 1:2], None, ALU.mult).then_inc(diag_ready, 1)
            bank = wait_full(dve, "plan", 0, "plan")
            V.tensor_copy(plan[0:1, 2 * P:2 * P + 1], cend[0:1, NE - 1:NE]).then_inc(plan_ready, 1)
            dve.wait_ge(plan_ready, 1)
            V.tensor_copy(plan[0:1, 0:2 * P], bank[0:1, 0:2 * P]).then_inc(read("plan", "plan"), 1)
            wait_out(dve, "plan", 0, "plan")
            chunks = dve.value_load(plan[0:1, 2 * P:2 * P + 1], min_val=2, max_val=P - 1)
            with dve.Fori(0, chunks) as q:
                for f in range(KE):
                    bank = ps[JOBS.bank("chunk", f"gu{f}")]
                    dve.wait_ge(sg_ready, KE * q + f + 1)
                    V.tensor_tensor(hTm[:, f, :], bank[:, CH:2 * CH], sg[:, f, :], ALU.mult)\
                        .then_inc(read("chunk", f"gu{f}"), 1)
                for j, (lo, hi) in enumerate(XT3):
                    bank = wait_full(dve, "chunk", q, f"y{j}")
                    V.tensor_copy(yT[:, lo:hi, :], bank[:, 0:(hi - lo) * CH].rearrange("p (k n) -> p k n", n=CH))\
                        .then_inc(read("chunk", f"y{j}"), 1)
                dve.wait_ge(io_loaded, 16 * q + 16)
                for i in range(2):
                    bank = wait_full(dve, "chunk", q, f"r{i}1")
                    V.tensor_scalar(ysb[:, 1, i * BANK:(i + 1) * BANK], bank[0:HF, :],
                                    idx_out[:, 1, 1:2].bitcast(F32), None, ALU.mult)\
                        .then_inc(read("chunk", f"r{i}1"), 1)

            dve.wait_ge(fg_loaded, 16)

            def final(it, b):
                dve.wait_ge(f_rs, it * 4 + b + 1)
                V.scalar_tensor_tensor(out=fb[b], in0=fb[b], scalar=rstd[:, b:b + 1], in1=g1b[:],
                                       op0=ALU.mult, op1=ALU.mult).then_inc(f_ready, 1)

            with dve.Fori(0, NTILE // 4) as it:
                for b in range(4):
                    final(it, b)
            final(NTILE // 4, 0)


def kernel(**inputs):
    import numpy as np
    import concourse.bacc as bacc
    from concourse.bass_utils import run_bass_kernel_spmd

    x = {n: np.ascontiguousarray(v) for n, v in inputs.items()}
    cols = lambda v: np.ascontiguousarray(v.reshape(-1, NC, P).transpose(2, 1, 0))
    arrays = {
        "x": np.concatenate([x["x_prompt"].reshape(SEQ, D), x["x_sample"].reshape(-1, D)]),
        "conv_state": cols(x["state_conv"][0].reshape(-1, DA)).reshape(P, NC, STREAMS, TAPS - 1),
        "h0": cols(x["state_rglru"][0]),
        "norm1_g": x["norm1_g"], "w_in": x["w_in"][0], "ln_g": x["gmlp_ln_g"], "ln_b": x["gmlp_ln_b"],
        "w_sT": np.ascontiguousarray(x["gmlp_w_s"][0].transpose(0, 2, 1)),
        "b_s": x["gmlp_b_s"][0].reshape(1, NC * P),
        "conv_w": cols(x["conv_w"][0]), "conv_b": cols(x["conv_b"])[:, :, 0].copy(),
        "lru_w": np.stack([x["lru_w_a"][0], x["lru_w_x"][0]]),
        "gate_b": np.stack([cols(x[n].reshape(1, DA))[:, :, 0] for n in ("lru_b_a", "lru_b_x")], axis=1),
        "lam": cols(x["lru_lambda"])[:, :, 0].copy(),
        "w_out": x["w_out"][0], "norm2_g": x["norm2_g"],
        "router_gw": x["router_group_w"][0], "router_ew": x["router_expert_w"][0],
        "router_b": np.concatenate([x["router_group_b"], x["router_expert_b"]], axis=1),
        "w_gate": x["expert_w_gate"][0], "w_up": x["expert_w_up"][0], "w_down": x["expert_w_down"][0],
        "final_g": x["final_norm_g"].reshape(1, D),
    }
    outs = {"y": (NTOK, D), "conv_p": (P, NC, TAPS - 1), "h_p": (P, NC), "v_s": (STREAMS * FRAMES, DA),
            "conv_s": (P, NC, STREAMS, TAPS - 1), "h_s": (P, NC, STREAMS)}
    nc = bacc.Bacc("TRN2", target_bir_lowering=False, num_devices=1)
    aps = {n: nc.dram_tensor(f"in_{n}", v.shape, F32, kind="ExternalInput").ap() for n, v in arrays.items()}
    aps |= {n: nc.dram_tensor(f"out_{n}", v, F32, kind="ExternalOutput").ap() for n, v in outs.items()}
    hymba_step(nc, aps)
    r = run_bass_kernel_spmd(nc, [{f"in_{n}": v for n, v in arrays.items()}], core_ids=[0]).results[0]
    y = r["out_y"]
    rows = lambda v: np.moveaxis(v, (1, 0), (-2, -1)).reshape(*v.shape[2:], DA)
    return (y[:SEQ].reshape(1, SEQ, D), y[SEQ:].reshape(STREAMS, FRAMES, D),
            rows(r["out_conv_p"]).reshape(1, 1, TAPS - 1, DA), rows(r["out_h_p"]).reshape(1, 1, DA),
            r["out_v_s"].reshape(1, STREAMS, FRAMES, DA), rows(r["out_conv_s"]).reshape(1, STREAMS, TAPS - 1, DA),
            rows(r["out_h_s"]).reshape(1, STREAMS, DA))
```

```python
from contextlib import ExitStack

import concourse.bass as bass
from concourse import mybir

ALU = mybir.AluOpType
ACT = mybir.ActivationFunctionType
AX = mybir.AxisListType
F32 = mybir.dt.float32
U32 = mybir.dt.uint32
I32 = mybir.dt.int32

P = 128
D = 1024
KD = D // P
DA = 512
NC = DA // P
GT = 2
G = GT * P
SEQ = 2048
NPG = SEQ // G
STREAMS, FRAMES = 8, 16
NTOK = SEQ + STREAMS * FRAMES
NTILE = NTOK // P
TAPS = 4
NG, EPG = 4, 8
NE = NG * EPG
DE = 512
KE = DE // P
CH = 160
HF = CH // 2
CPE = -(-NTOK // CH)
SLOTS = CPE * CH
NROW = NTOK + CH
EPS = 1e-6
GELU_C = 0.7978845608028654
BANKS = 8
BANK = 512
N_PAD = 96


class PsumJobs:

    def __init__(self, segments):
        self.first, self.per, self.where = {}, {}, {}
        done = [0] * BANKS
        for name, times, jobs in segments:
            per = [0] * BANKS
            for j, job in enumerate(jobs):
                self.where[name, job] = (j % BANKS, per[j % BANKS])
                per[j % BANKS] += 1
            self.first[name], self.per[name] = list(done), per
            done = [d + times * p for d, p in zip(done, per)]

    def bank(self, seg, job):
        return self.where[seg, job][0]

    def before(self, seg, it, job):
        b, u = self.where[seg, job]
        return it * self.per[seg][b] + (self.first[seg][b] + u)


def group_jobs(tiles, prev, ahead):
    jobs = ["xb0", "xb1"]
    for t in range(prev):
        jobs += [f"h2T{t}a", f"h2T{t}b", f"lg{t}"]
    jobs += [f"v{t}" for t in range(tiles)] + [f"ga{c}" for c in range(NC)]
    jobs += ["pf"] if prev else []
    jobs += ["gg0", "gg1"] + [f"s{t}" for t in range(tiles)] + ["u0", "u1"]
    jobs += [f"xT{j}" for j in range(4)] if ahead else []
    return jobs + [f"o{t}{h}" for t in range(tiles) for h in range(2)]


XT3 = ((0, 3), (3, 6), (6, 8))
JOBS = PsumJobs([
    ("start", 1, [f"xT{j}" for j in range(4)]),
    ("first", 1, group_jobs(GT, 0, GT)),
    ("loop", NPG - 2, group_jobs(GT, GT, GT)),
    ("final", 1, group_jobs(GT, GT, 1)),
    ("last", 1, group_jobs(1, GT, 0)),
    ("tail", 1, ["h2T0a", "h2T0b", "lg0", "pf"]),
    ("plan", 1, ["plan"]),
    ("pre", 1, ["xT0", "xT1", "xT2"]),
    ("chunk", 1, [f"gu{f}" for f in range(KE)] + ["xT0", "xT1", "xT2", "y0", "y1", "y2"]
     + ["r00", "r01", "r10", "r11"]),
])


def squares(g, what, t):
    if what == "in":
        if isinstance(g, int) and g == 0:
            return t
        return (g - 1) * 2 * GT + GT + t
    if isinstance(g, int) and g >= NPG - 1:
        return (NPG - 1) * 2 * GT + GT + 1 + (g - NPG + 1) * GT + t
    return g * 2 * GT + 2 * GT + t


def hymba_step(nc, a):
    with ExitStack() as ctx:
        def sb(name, shape, dt=F32):
            return ctx.enter_context(nc.sbuf_tensor(name, shape, dt))

        def sem(name):
            return ctx.enter_context(nc.semaphore(name))

        acc = nc.dram_tensor("acc_rows", [NROW, D], F32).ap()
        h2_rows = nc.dram_tensor("h2_rows", [NROW, D], F32).ap()
        table = nc.dram_tensor("slot_table", [NE * SLOTS, 2], U32).ap()

        w_in = sb("w_in_sb", [P, KD * 2048])
        w_out = sb("w_out_sb", [P, KD * D])
        w_in_v = w_in[:].rearrange("p (k n) -> p k n", k=KD)
        w_out_v = w_out[:].rearrange("p (k n) -> p k n", k=KD)
        xa = sb("xa", [P, GT, D])
        xr = sb("xr", [P, GT, D])
        h2T = sb("h2T", [P, KD, P])
        hT = sb("hT", [P, KD, G])
        xbT = sb("xbT", [P, NC, TAPS - 1 + G])
        xbs = sb("xbs", [P, NC, STREAMS, TAPS - 1 + FRAMES])
        xcT = sb("xcT", [P, NC, G])
        ri = sb("ri", [P, 2, NC, G])
        aT = sb("aT", [P, NC, G])
        qT = sb("qT", [P, NC, G])
        gS = sb("gS", [P, NC, G])
        gt = sb("gt", [P, NC, G])
        sS = sb("sS", [P, NC, G])
        catT = sb("catT", [P, KD, G])
        vn = sb("vn", [P, GT, DA])
        g1b = sb("g1b", [P, D])
        g2b = sb("g2b", [P, D])
        lngb = sb("lngb", [P, DA])
        lnbb = sb("lnbb", [P, DA])
        bsb = sb("bsb", [P, NC, P])
        wsT = sb("wsT", [P, NC, P])
        wsTs = sb("wsTs", [P, NC, P])
        wgate = sb("wgate", [P, 2, NC, P])
        rw = sb("rw", [P, KD, NG + NE])
        rb = sb("rb", [P, NG + NE])
        ident = sb("ident", [P, P])
        before = sb("before", [P, P])
        ones = sb("ones", [P, P])
        cw = sb("cw", [P, NC, TAPS])
        cb = sb("cb", [P, NC])
        nb = sb("nb", [P, 2, NC])
        lam = sb("lam", [P, NC])
        lamt = sb("lamt", [P, 3, NC])
        nsp = sb("nsp", [P, NC])
        hlast = sb("hlast", [P, NC])
        h0s = sb("h0s", [P, NC, STREAMS])
        mhalf = sb("mhalf", [P, NC])
        pad = sb("pad", [P, N_PAD])
        ssq = sb("ssq", [P, 2 * GT])
        rstd = sb("rstd", [P, 2 * GT])
        vst = sb("vst", [P, GT, NC, 6])
        vmv = sb("vmv", [P, GT, NC, 2])
        vrs = sb("vrs", [P, GT, NC])
        gl = sb("gl", [P, GT, 8])
        el = sb("el", [P, GT, NE])
        m8 = sb("m8", [P, GT, 2, 8])
        i8 = sb("i8", [P, GT, 2, 8], U32)
        rf = sb("rf", [P, GT, 16])
        dv = sb("dv", [P, GT, 8])
        mk = sb("mk", [P, GT, NG])
        ein = sb("ein", [P, GT, EPG])
        hot = sb("hot", [P, GT, 3, NE])
        iota32 = sb("iota32", [P, NE])
        ebase = sb("ebase", [P, NE])
        tokf = sb("tokf", [P, 1])
        pcol = sb("pcol", [P, 1])
        count = sb("count", [P, NE])
        rk = sb("rk", [P, NE])
        rkj = sb("rkj", [P, NE])
        slotf = sb("slotf", [P, GT, 2])
        slot = sb("slot", [P, GT, 2], U32)
        pay = sb("pay", [P, GT, 2, 2], U32)
        nch = sb("nch", [P, NE])
        cend = sb("cend", [P, NE])
        ple = sb("ple", [P, 2, NE])
        pq = sb("pq", [P, 4])
        diag = sb("diag", [P, 2, P])
        plan = sb("plan", [1, 2 * P + 1], I32)
        idx_in = sb("idx_in", [HF, 2, 2], U32)
        idx_out = sb("idx_out", [HF, 2, 2], U32)
        o = 0
        wg_e = w_in[:, o:o + KD * DE].rearrange("p (k f) -> p k f", k=KD)
        o += KD * DE
        wu_e = w_in[:, o:o + KD * DE].rearrange("p (k f) -> p k f", k=KD)
        o += KD * DE
        wd_e = w_in[:, o:o + KE * D].rearrange("p (f d) -> p f d", f=KE)
        o += KE * D
        xg = w_in[0:HF, o:o + 2 * D].rearrange("p (h d) -> p h d", h=2)
        o += 2 * D
        ysb = w_in[0:HF, o:o + 2 * D].rearrange("p (h d) -> p h d", h=2)
        o = 0
        xTm = w_out[:, o:o + KD * CH].rearrange("p (k n) -> p k n", k=KD)
        o += KD * CH
        hTm = w_out[:, o:o + KE * CH].rearrange("p (k n) -> p k n", k=KE)
        o += KE * CH
        sg = w_out[:, o:o + KE * CH].rearrange("p (k n) -> p k n", k=KE)
        o += KE * CH
        yT = w_out[:, o:o + KD * CH].rearrange("p (k n) -> p k n", k=KD)
        tinit = aT[:].rearrange("p a b -> p (a b)")[:, 0:2 * CH].bitcast(U32).rearrange("p (n t) -> p n t", t=2)
        zrow = qT[:].rearrange("p a b -> p (a b)")
        fb = [xa[:, 0], xa[:, 1], xr[:, 0], xr[:, 1]]

        ps = [ctx.enter_context(nc.psum_tensor(f"ps{b}", [P, BANK], F32)) for b in range(BANKS)]

        psum_full = [sem(f"psum_full{b}") for b in range(BANKS)]
        psum_read = [sem(f"psum_read{b}") for b in range(BANKS)]
        w1_loaded = [sem(f"w1_loaded{i}") for i in range(4)]
        g1_loaded = sem("g1_loaded")
        const_w2 = sem("const_w2")
        const_dma = sem("const_dma")
        const_dve = sem("const_dve")
        const_pool = sem("const_pool")
        pool_link = sem("pool_link")
        act_link = sem("act_link")
        table_ready = sem("table_ready")
        xa_loaded = [sem(f"xa_loaded{t}") for t in range(GT)]
        xr_loaded = [sem(f"xr_loaded{t}") for t in range(GT)]
        sq_ready = sem("sq_ready")
        rs_ready = sem("rs_ready")
        rs_link = sem("rs_link")
        xn_ready = sem("xn_ready")
        halo_ready = sem("halo_ready")
        xc_ready = sem("xc_ready")
        var_ready = sem("var_ready")
        vrs_ready = sem("vrs_ready")
        vrs_link = sem("vrs_link")
        vn_ready = sem("vn_ready")
        at_ready = sem("at_ready")
        q_ready = sem("q_ready")
        gain_ready = sem("gain_ready")
        gin_ready = sem("gin_ready")
        gth_ready = sem("gth_ready")
        h_ready = sem("h_ready")
        cat_ready = sem("cat_ready")
        acc_stored = [sem(f"acc_stored{t}") for t in range(GT)]
        h2_ready = [sem(f"h2_ready{t}") for t in range(GT)]
        h2_stored = [sem(f"h2_stored{t}") for t in range(GT)]
        dv_ready = sem("dv_ready")
        dve_exp = sem("dve_exp")
        hot_ready = sem("hot_ready")
        slot_ready = sem("slot_ready")
        scattered = sem("scattered")
        pay_free = sem("pay_free")
        state_out = sem("state_out")
        dve_main = sem("dve_main")
        dve_choose = sem("dve_choose")
        dve_assign = sem("dve_assign")
        count_ready = sem("count_ready")
        dve_plan = sem("dve_plan")
        diag_ready = sem("diag_ready")
        plan_ready = sem("plan_ready")
        w_loaded = [sem(f"w_loaded{i}") for i in range(4)]
        ix_loaded = sem("ix_loaded")
        io_loaded = sem("io_loaded")
        xg_loaded = sem("xg_loaded")
        sg_ready = sem("sg_ready")
        y_added = sem("y_added")
        moe_done = sem("moe_done")
        moe_carry = sem("moe_carry")
        fg_loaded = sem("fg_loaded")
        f_loaded = [sem(f"f_loaded{b}") for b in range(4)]
        f_sq = sem("f_sq")
        f_link = sem("f_link")
        f_rs = sem("f_rs")
        f_ready = sem("f_ready")
        f_stored = [sem(f"f_stored{b}") for b in range(4)]

        def wait(eng, s, value):
            if not (isinstance(value, int) and value <= 0):
                eng.wait_ge(s, value)

        def wait_full(eng, seg, it, job):
            eng.wait_ge(psum_full[JOBS.bank(seg, job)], JOBS.before(seg, it, job) + 1)
            return ps[JOBS.bank(seg, job)]

        def wait_free(eng, seg, it, job):
            wait(eng, psum_read[JOBS.bank(seg, job)], JOBS.before(seg, it, job))
            return ps[JOBS.bank(seg, job)]

        def wait_out(eng, seg, it, job):
            eng.wait_ge(psum_read[JOBS.bank(seg, job)], JOBS.before(seg, it, job) + 1)

        def full(seg, job):
            return psum_full[JOBS.bank(seg, job)]

        def read(seg, job):
            return psum_read[JOBS.bank(seg, job)]

        pads = iter(range(N_PAD))

        def carry(eng):
            n = next(pads)
            return eng.tensor_tensor(pad[:, n:n + 1], mhalf[:, 0:1], mhalf[:, 0:1], ALU.mult)

        N_CONST = 18
        block = ctx.enter_context(nc.Block())

        @block.sync
        def _(sp):
            def load_x(g, t, dst, s):
                sp.dma_start(dst[:, t], a["x"].rearrange("(n p) d -> n p d", p=P)[bass.ds(g * GT + t, 1)]
                             .rearrange("a p d -> p (a d)")).then_inc(s[t], 16)

            for t in range(GT):
                load_x(0, t, xa, xa_loaded)
            small = [
                (cw[:], a["conv_w"]), (cb[:], a["conv_b"]), (lam[:], a["lam"]),
                (nb[:], a["gate_b"]), (h0s[:], a["h0"]),
                (xbs[:, :, :, 0:TAPS - 1], a["conv_state"]),
                (lngb[:], a["ln_g"].broadcast_to([P, DA])), (lnbb[:], a["ln_b"].broadcast_to([P, DA])),
                (bsb[:], a["b_s"].rearrange("a (g t) -> a g t", g=NC).broadcast_to([P, NC, P])),
                (wsT[:], a["w_sT"].rearrange("g s t -> s g t")),
                (g2b[:], a["norm2_g"].broadcast_to([P, D])),
                (rb[:], a["router_b"].broadcast_to([P, NG + NE])),
                (rw[:, :, 0:NG], a["router_gw"].rearrange("(k p) n -> p k n", p=P)),
                (rw[:, :, NG:NG + NE], a["router_ew"].rearrange("(k p) n -> p k n", p=P)),
            ]
            sp.dma_start(g1b[:], a["norm1_g"].broadcast_to([P, D])).then_inc(g1_loaded, 16)
            for dst, src in small[:6]:
                sp.dma_start(dst, src).then_inc(const_dma, 16)
            win = a["w_in"].rearrange("(k p) n -> p k n", p=P)
            for lo in (2 * DA, DA, 3 * DA, 0):
                sp.dma_start(w_in_v[:, :, lo:lo + DA], win[:, :, lo:lo + DA]).then_inc(w1_loaded[lo // DA], 16)
            for dst, src in small[6:]:
                sp.dma_start(dst, src).then_inc(const_dma, 16)
            for t in range(GT):
                load_x(0, t, xr, xr_loaded)
            sp.dma_start(w_out_v, a["w_out"].rearrange("(k p) n -> p k n", p=P)).then_inc(const_w2, 16)
            sp.wait_ge(const_dve, 2)
            for m in range(2):
                for half in range(2):
                    r = slice(64 * half, 64 * half + 64)
                    sp.dma_start(wgate[r, m, :, 64 * half:64 * half + 64],
                                 a["lru_w"][m].rearrange("(c h) i j -> h i c j", h=2)[half]).then_inc(const_dma, 16)
            for s in range(STREAMS):
                r = slice(FRAMES * s, FRAMES * (s + 1))
                sp.dma_start(wsTs[r, :, FRAMES * s:FRAMES * (s + 1)],
                             a["w_sT"].rearrange("g s t -> s g t")[0:FRAMES, :, 0:FRAMES]).then_inc(const_w2, 16)
            wait_full(sp, "start", 0, "xT3")
            for t in range(GT):
                load_x(1, t, xa, xa_loaded)
            sp.wait_ge(const_pool, 5)
            tv = table.rearrange("(q p n) c -> q p (n c)", p=NE * CPE // 4, n=CH)
            for q in range(4):
                sp.dma_start(tv[q], tinit[0:NE * CPE // 4].rearrange("p n t -> p (n t)")).then_inc(table_ready, 16)
            sp.wait_ge(const_dve, 3)
            for dst in (acc, h2_rows):
                for h in range(2):
                    r = NTOK + HF * h
                    sp.dma_start(dst[r:r + HF], zrow[0:HF]).then_inc(table_ready, 16)

            def rows(dst, g, t):
                n = g * GT + t
                return dst[0:NTOK].rearrange("(n p) d -> n p d", p=P)[bass.ds(n, 1)].rearrange("a p d -> p (a d)")

            def group(seg, it, g, nxt, tiles):
                for t in range(nxt):
                    if t == 0:
                        wait_full(sp, seg, it, "xT3")
                    load_x(g + 2, t, xa, xa_loaded)
                for t in range(tiles):
                    wait_out(sp, seg, it, f"o{t}1")
                    sp.dma_start(rows(acc, g, t), xr[:, t]).then_inc(acc_stored[t], 16)
                for t in range(tiles):
                    sp.wait_ge(h2_ready[t], g + 1)
                    sp.dma_start(rows(h2_rows, g, t), xr[:, t]).then_inc(h2_stored[t], 16)

            def next_xr(seg, it, g, tiles):
                for t in range(tiles):
                    sp.wait_ge(h2_stored[t], 16 * g)
                    wait_full(sp, seg, it, f"h2T{t}b")
                    load_x(g, t, xr, xr_loaded)

            group("first", 0, 0, GT, GT)
            with sp.Fori(1, NPG - 2) as g:
                next_xr("loop", g - 1, g, GT)
                group("loop", g - 1, g, GT, GT)
            next_xr("loop", NPG - 3, NPG - 2, GT)
            group("loop", NPG - 3, NPG - 2, 1, GT)
            next_xr("final", 0, NPG - 1, GT)
            group("final", 0, NPG - 1, 0, GT)
            sp.wait_ge(halo_ready, 1 + NPG)
            sp.dma_start(a["conv_p"], xbT[:, :, 0:TAPS - 1]).then_inc(state_out, 16)
            sp.wait_ge(h_ready, NPG)
            sp.dma_start(a["h_p"], hlast[:]).then_inc(state_out, 16)
            next_xr("last", 0, NPG, 1)
            sp.wait_ge(vn_ready, GT * NPG + 1)
            sp.dma_start(a["v_s"], vn[:, 0]).then_inc(state_out, 16)
            wait_out(sp, "last", 0, "xb1")
            for c in range(NC):
                sp.dma_start(a["conv_s"][:, c], xbs[:, c, :, FRAMES:FRAMES + TAPS - 1]).then_inc(state_out, 16)
            sp.wait_ge(h_ready, NPG + 1)
            sp.dma_start(a["h_s"], h0s[:]).then_inc(state_out, 16)
            wait_full(sp, "last", 0, "u1")

            def weights(e, piece):
                wgd = a["w_gate"].rearrange("e (k p) f -> e p k f", p=P)
                wud = a["w_up"].rearrange("e (k p) f -> e p k f", p=P)
                wdd = a["w_down"].rearrange("e (f p) d -> e p f d", p=P)

                def at(x, lo, hi):
                    return x[bass.ds(e, 1)].rearrange("a p k f -> p (a k) f")[:, :, lo:hi]

                if piece < 2:
                    lo, hi = DE // 2 * piece, DE // 2 * (piece + 1)
                    sp.dma_start(wg_e[:, :, lo:hi], at(wgd, lo, hi)).then_inc(w_loaded[piece], 16)
                    sp.dma_start(wu_e[:, :, lo:hi], at(wud, lo, hi)).then_inc(w_loaded[piece], 16)
                else:
                    lo, hi = ((0, 6 * P), (6 * P, D))[piece - 2]
                    sp.dma_start(wd_e[:, :, lo:hi], at(wdd, lo, hi)).then_inc(w_loaded[piece], 16)

            for piece in range(4):
                weights(0, piece)
            group("last", 0, NPG, 0, 1)
            wait_out(sp, "plan", 0, "plan")
            chunks = sp.value_load(plan[0:1, 2 * P:2 * P + 1], min_val=2, max_val=P - 1)
            with sp.Fori(1, chunks) as q:
                e = sp.value_load(plan[0:1, bass.ds(q, 1)], min_val=0, max_val=NE - 1)
                for piece, job in enumerate(("gu1", "gu3", "y1", "y2")):
                    wait_full(sp, "chunk", q - 1, job)
                    weights(e, piece)
            sp.wait_ge(xn_ready, GT * NPG + 1)
            sp.dma_start(g1b[:], a["final_g"].broadcast_to([P, D])).then_inc(fg_loaded, 16)
            sp.wait_ge(moe_done, 1)

            def load_f(it, b):
                wait(sp, f_stored[b], 16 * it)
                sp.dma_start(fb[b], acc[0:NTOK].rearrange("(n p) d -> n p d", p=P)[bass.ds(it * 4 + b, 1)]
                             .rearrange("a p d -> p (a d)")).then_inc(f_loaded[b], 16)

            for b in range(4):
                load_f(0, b)
            with sp.Fori(1, NTILE // 4) as it:
                for b in range(4):
                    load_f(it, b)
            load_f(NTILE // 4, 0)
            sp.wait_ge(state_out, 16 * (NC + 4))
            for t in range(GT):
                n = NPG + (t == 0)
                sp.wait_ge(acc_stored[t], 16 * n)
                sp.wait_ge(h2_stored[t], 16 * n)
            for b in range(4):
                sp.wait_ge(f_stored[b], 16 * (NTILE // 4 + (b == 0)))

        @block.gpsimd
        def _(pool):
            def made(ins, s=const_pool):
                ins.then_inc(s, 1)

            pool.nop().then_inc(pay_free, 1)
            nc.gpsimd.memset(ident[:], 0.0).then_inc(pool_link, 1)
            nc.gpsimd.memset(before[:], 1.0).then_inc(pool_link, 1)
            nc.gpsimd.memset(mhalf[:], -0.5).then_inc(pool_link, 1)
            pool.wait_ge(pool_link, 3)
            made(nc.gpsimd.affine_select(out=ident[:], in_=ident[:], compare_op=ALU.not_equal, fill=1.0, base=0,
                                         pattern=[[-1, P]], channel_multiplier=1))
            made(nc.gpsimd.affine_select(out=before[:], in_=before[:], compare_op=ALU.is_gt, fill=0.0, base=0,
                                         pattern=[[1, P]], channel_multiplier=-1))
            nc.gpsimd.memset(tinit, 0).then_inc(pool_link, 1)
            pool.wait_ge(pool_link, 4)
            made(nc.gpsimd.iota(tinit[:, :, 0], [[1, CH]], base=NTOK, channel_multiplier=0))
            made(nc.gpsimd.iota(iota32[:], [[1, NE]], base=0, channel_multiplier=0,
                                allow_small_or_imprecise_dtypes=True))
            made(nc.gpsimd.iota(ebase[:], [[SLOTS, NE]], base=0, channel_multiplier=0,
                                allow_small_or_imprecise_dtypes=True))
            made(nc.gpsimd.iota(pcol[:], [[0, 1]], base=0, channel_multiplier=1,
                                allow_small_or_imprecise_dtypes=True))
            made(nc.gpsimd.iota(tokf[:], [[0, 1]], base=0, channel_multiplier=1,
                                allow_small_or_imprecise_dtypes=True))

            def root(col, n):
                pool.wait_ge(sq_ready, n + 1)
                carry(pool)
                nc.gpsimd.tensor_scalar(rstd[:, col:col + 1], ssq[:, col:col + 1], 1.0 / D, EPS, ALU.mult,
                                        ALU.add).then_inc(rs_link, 1)
                pool.wait_ge(rs_link, n + 1)
                nc.gpsimd.tensor_tensor(rstd[:, col:col + 1], rstd[:, col:col + 1], mhalf[:, 0:1],
                                        ALU.pow).then_inc(rs_ready, 1)

            for t in range(GT):
                root(t, squares(0, "in", t))
            pool.wait_ge(const_dma, 16 * N_CONST)
            pool.wait_ge(const_w2, 16 * (1 + STREAMS))
            made(nc.gpsimd.affine_select(out=wsT[:], in_=wsT[:], compare_op=ALU.is_ge, fill=0.0, base=0,
                                         pattern=[[0, NC], [1, P]], channel_multiplier=-1))
            made(nc.gpsimd.affine_select(out=wsTs[:], in_=wsTs[:], compare_op=ALU.is_ge, fill=0.0, base=0,
                                         pattern=[[0, NC], [1, P]], channel_multiplier=-1))

            def scatter(n, t):
                pool.wait_ge(slot_ready, n + 1)
                carry(pool)
                for k in range(2):
                    pool.indirect_dma_start(table, bass.IndirectOffsetOnAxis(ap=slot[:, t, k:k + 1], axis=0),
                                            pay[:, t, k, :], None).then_inc(scattered, 16)

            def group(g, tiles, prev, ahead):
                for t in range(tiles):
                    pool.wait_ge(var_ready, g * GT + t + 1)
                    carry(pool)
                    nc.gpsimd.tensor_scalar(vrs[:, t], vmv[:, t, :, 1], EPS, None, ALU.add).then_inc(vrs_link, 1)
                    pool.wait_ge(vrs_link, g * GT + t + 1)
                    nc.gpsimd.tensor_tensor(vrs[:, t], vrs[:, t], mhalf[:], ALU.pow).then_inc(vrs_ready, 1)
                for t in range(ahead):
                    root(t, squares(g + 1, "in", t))
                for t in range(prev):
                    scatter((g - 1) * GT + t, t)
                for t in range(tiles):
                    root(GT + t, squares(g, "x1", t))
                if prev:
                    pool.wait_ge(scattered, 16 * 2 * GT * g)
                    pool.nop().then_inc(pay_free, 1)

            group(0, GT, 0, GT)
            pool.wait_ge(table_ready, 16 * 8)
            with pool.Fori(1, NPG - 1) as g:
                group(g, GT, GT, GT)
            group(NPG - 1, GT, GT, 1)
            group(NPG, 1, GT, 0)
            scatter(GT * NPG, 0)

            pool.wait_ge(scattered, 16 * 2 * NTILE)
            wait_out(pool, "plan", 0, "plan")
            chunks = pool.value_load(plan[0:1, 2 * P:2 * P + 1], min_val=2, max_val=P - 1)

            def load_index(q, dst, s):
                row = pool.value_load(plan[0:1, bass.ds(q + P, 1)], min_val=0, max_val=NE * SLOTS - CH)
                pool.dma_start(dst[:], table[bass.ds(row, CH)].rearrange("(h p) c -> p h c", h=2)).then_inc(s, 16)

            def gather():
                for h in range(2):
                    pool.indirect_dma_start(xg[:, h, :], None, h2_rows,
                                            bass.IndirectOffsetOnAxis(ap=idx_in[:, h, 0:1], axis=0)).then_inc(xg_loaded, 16)

            for t in range(GT):
                pool.wait_ge(h2_stored[t], 16 * (NPG + (t == 0)))
                pool.wait_ge(acc_stored[t], 16 * (NPG + (t == 0)))
            wait_full(pool, "last", 0, "o01")
            load_index(0, idx_in, ix_loaded)
            pool.wait_ge(ix_loaded, 16)
            gather()
            pool.wait_ge(xg_loaded, 32)
            load_index(1, idx_in, ix_loaded)
            pool.wait_ge(ix_loaded, 32)
            wait_full(pool, "pre", 0, "xT2")
            gather()
            pool.nop().then_inc(moe_carry, 1)
            with pool.Fori(0, chunks) as q:
                load_index(q, idx_out, io_loaded)
                pool.wait_ge(xg_loaded, 32 * q + 64)
                load_index(q + 2, idx_in, ix_loaded)
                pool.wait_ge(ix_loaded, 16 * q + 48)
                wait_full(pool, "chunk", q, "xT2")
                pool.wait_ge(moe_carry, 2 * q + 1)
                carry(pool).then_inc(moe_carry, 1)
                gather()
                wait_out(pool, "chunk", q, "r10")
                wait_out(pool, "chunk", q, "r11")
                pool.wait_ge(io_loaded, 16 * q + 16)
                pool.wait_ge(moe_carry, 2 * q + 2)
                carry(pool).then_inc(moe_carry, 1)
                for h in range(2):
                    pool.indirect_dma_start(acc, bass.IndirectOffsetOnAxis(ap=idx_out[:, h, 0:1], axis=0),
                                            ysb[:, h, :], None, compute_op=ALU.add).then_inc(y_added, 16)
                pool.wait_ge(y_added, 32 * q + 32)
            pool.wait_ge(xg_loaded, 32 * chunks + 64)
            pool.nop().then_inc(moe_done, 1)

            def final(it, b):
                k = it * 4 + b
                pool.wait_ge(f_sq, k + 2)
                carry(pool)
                nc.gpsimd.tensor_scalar(rstd[:, b:b + 1], ssq[:, b:b + 1], 1.0 / D, EPS, ALU.mult,
                                        ALU.add).then_inc(f_link, 1)
                pool.wait_ge(f_link, k + 1)
                nc.gpsimd.tensor_tensor(rstd[:, b:b + 1], rstd[:, b:b + 1], mhalf[:, 0:1], ALU.pow).then_inc(f_rs, 1)

            with pool.Fori(0, NTILE // 4) as it:
                for b in range(4):
                    final(it, b)
            final(NTILE // 4, 0)

        @block.tensor
        def _(pe):
            def inputs(seg, it, tiles, have):
                n = tiles * P
                pe.wait_ge(xn_ready, have)
                for j in range(4):
                    bank = wait_free(pe, seg, it, f"xT{j}")
                    for kk in range(2):
                        for t in range(tiles):
                            mm = pe.transpose(bank[:, kk * n + t * P:kk * n + (t + 1) * P],
                                              xa[:, t, (2 * j + kk) * P:(2 * j + kk + 1) * P], ident[:])
                    mm.then_inc(full(seg, f"xT{j}"), 1)

            def group(seg, it, g, tiles, prev, ahead):
                n = tiles * P

                def channels(kind, lo, p):
                    bank = wait_free(pe, seg, it, f"{kind}{p}")
                    for cc in range(2):
                        col = lo + (2 * p + cc) * P
                        for k in range(KD):
                            mm = pe.matmul(bank[:, cc * n:(cc + 1) * n], w_in_v[:, k, col:col + P], hT[:, k, 0:n],
                                           start=(k == 0), stop=(k == KD - 1))
                    mm.then_inc(full(seg, f"{kind}{p}"), 1)

                def first_use(s, count):
                    if seg == "first":
                        pe.wait_ge(s, count)

                first_use(w1_loaded[2], 16)
                for p in range(2):
                    channels("xb", 2 * DA, p)
                for t in range(prev):
                    route(seg, it, t, g - 1)
                first_use(w1_loaded[1], 16)
                for t in range(tiles):
                    bank = wait_free(pe, seg, it, f"v{t}")
                    for k in range(KD):
                        mm = pe.matmul(bank[:, :], hT[:, k, t * P:(t + 1) * P], w_in_v[:, k, DA:2 * DA],
                                       start=(k == 0), stop=(k == KD - 1))
                    mm.then_inc(full(seg, f"v{t}"), 1)
                first_use(const_dma, 16 * N_CONST)
                for c in range(NC):
                    bank = wait_free(pe, seg, it, f"ga{c}")
                    pe.wait_ge(xc_ready, NC * g + c + 1)
                    for m in range(2):
                        mm = pe.matmul(bank[:, m * n:(m + 1) * n], wgate[:, m, c, :], xcT[:, c, 0:n], start=True, stop=True)
                    mm.then_inc(full(seg, f"ga{c}"), 1)
                if prev:
                    places(seg, it, prev, g - 1)
                first_use(w1_loaded[3], 16)
                for p in range(2):
                    channels("gg", 3 * DA, p)
                first_use(const_pool, 9)
                for t in range(tiles):
                    bank = wait_free(pe, seg, it, f"s{t}")
                    pe.wait_ge(vn_ready, g * GT + t + 1)
                    ws = wsTs if seg == "last" else wsT
                    for c in range(NC):
                        mm = pe.matmul(bank[:, c * P:(c + 1) * P], vn[:, t, c * P:(c + 1) * P], ws[:, c, :],
                                       start=True, stop=True)
                    mm.then_inc(full(seg, f"s{t}"), 1)
                first_use(w1_loaded[0], 16)
                for p in range(2):
                    channels("u", 0, p)
                if ahead:
                    inputs(seg, it, ahead, (g + 1) * GT + ahead)
                first_use(const_w2, 16 * (1 + STREAMS))
                wait_out(pe, seg, it, "u1")
                pe.wait_ge(cat_ready, g + 1)
                for t in range(tiles):
                    for h in range(2):
                        bank = wait_free(pe, seg, it, f"o{t}{h}")
                        for k in range(KD):
                            mm = pe.matmul(bank[:, :], catT[:, k, t * P:(t + 1) * P],
                                           w_out_v[:, k, h * BANK:(h + 1) * BANK], start=(k == 0), stop=(k == KD - 1))
                        mm.then_inc(full(seg, f"o{t}{h}"), 1)
                if ahead:
                    wait_out(pe, seg, it, "xT3")

            def route(seg, it, t, gp):
                pe.wait_ge(h2_ready[t], gp + 1)
                for i, half in enumerate("ab"):
                    bank = wait_free(pe, seg, it, f"h2T{t}{half}")
                    for k in range(4):
                        kk = 4 * i + k
                        mm = pe.transpose(bank[:, k * P:(k + 1) * P], xr[:, t, kk * P:(kk + 1) * P], ident[:])
                    mm.then_inc(full(seg, f"h2T{t}{half}"), 1)
                bank = wait_free(pe, seg, it, f"lg{t}")
                wait_out(pe, seg, it, f"h2T{t}b")
                for k in range(KD):
                    mm = pe.matmul(bank[:, 0:NG + NE], h2T[:, k, :], rw[:, k, :], start=(k == 0), stop=(k == KD - 1))
                mm.then_inc(full(seg, f"lg{t}"), 1)

            def places(seg, it, tiles, gp):
                bank = wait_free(pe, seg, it, "pf")
                for t in range(tiles):
                    pe.wait_ge(hot_ready, gp * GT + t + 1)
                    pe.matmul(bank[:, 64 * t:64 * t + NE], before[:], hot[:, t, 2, :], start=True, stop=True)
                    mm = pe.matmul(bank[:, 64 * t + NE:64 * t + 2 * NE], ones[:], hot[:, t, 2, :], start=True, stop=True)
                mm.then_inc(full(seg, "pf"), 1)

            pe.wait_ge(const_pool, 1)
            inputs("start", 0, GT, GT)
            wait_out(pe, "start", 0, "xT3")
            group("first", 0, 0, GT, 0, GT)
            pe.wait_ge(const_dve, 4)
            with pe.Fori(1, NPG - 1) as g:
                group("loop", g - 1, g, GT, GT, GT)
            group("final", 0, NPG - 1, GT, GT, 1)
            group("last", 0, NPG, 1, GT, 0)
            route("tail", 0, 0, NPG)
            places("tail", 0, 1, NPG)
            bank = wait_free(pe, "plan", 0, "plan")
            pe.wait_ge(diag_ready, 1)
            for i in range(2):
                mm = pe.matmul(bank[:, i * P:(i + 1) * P], ones[:], diag[:, i, :], start=True, stop=True)
            mm.then_inc(full("plan", "plan"), 1)

            def columns(seg, q, n):
                pe.wait_ge(xg_loaded, 32 * n + 32)
                for j, (lo, hi) in enumerate(XT3):
                    bank = wait_free(pe, seg, q, f"xT{j}")
                    for k in range(lo, hi):
                        for h in range(2):
                            at = (k - lo) * CH + h * HF
                            mm = pe.transpose(bank[:, at:at + HF], xg[:, h, k * P:(k + 1) * P], ident[0:HF, 0:HF])
                    mm.then_inc(full(seg, f"xT{j}"), 1)

            wait_out(pe, "plan", 0, "plan")
            chunks = pe.value_load(plan[0:1, 2 * P:2 * P + 1], min_val=2, max_val=P - 1)
            columns("pre", 0, 0)
            wait_out(pe, "pre", 0, "xT2")
            with pe.Fori(0, chunks) as q:
                for f in range(KE):
                    bank = wait_free(pe, "chunk", q, f"gu{f}")
                    if f % 2 == 0:
                        pe.wait_ge(w_loaded[f // 2], 32 * q + 32)
                    for m, w in enumerate((wg_e, wu_e)):
                        for k in range(KD):
                            mm = pe.matmul(bank[:, m * CH:(m + 1) * CH], w[:, k, f * P:(f + 1) * P], xTm[:, k, :],
                                           start=(k == 0), stop=(k == KD - 1))
                    mm.then_inc(full("chunk", f"gu{f}"), 1)
                columns("chunk", q, q + 1)
                wait_out(pe, "chunk", q, f"gu{KE - 1}")
                for j, (lo, hi) in enumerate(XT3):
                    bank = wait_free(pe, "chunk", q, f"y{j}")
                    if j != 1:
                        pe.wait_ge(w_loaded[2 + j // 2], 16 * q + 16)
                    for d in range(lo, hi):
                        for f in range(KE):
                            mm = pe.matmul(bank[:, (d - lo) * CH:(d - lo + 1) * CH], wd_e[:, f, d * P:(d + 1) * P],
                                           hTm[:, f, :], start=(f == 0), stop=(f == KE - 1))
                    mm.then_inc(full("chunk", f"y{j}"), 1)
                for i in range(2):
                    wait_out(pe, "chunk", q, f"y{1 + i}")
                    for h in range(2):
                        bank = wait_free(pe, "chunk", q, f"r{i}{h}")
                        for d in range(4):
                            mm = pe.transpose(bank[0:HF, d * P:(d + 1) * P], yT[:, 4 * i + d, h * HF:(h + 1) * HF], ident[:])
                        mm.then_inc(full("chunk", f"r{i}{h}"), 1)
                wait_out(pe, "chunk", q, "xT2")

        @block.scalar
        def _(act):
            def copy_out(seg, it, job, dst, width, s):
                bank = wait_full(act, seg, it, job)
                nc.scalar.copy(dst, bank[:, 0:width]).then_inc(read(seg, job), 1)

            def h2_columns(seg, it, t, gp, sq_n):
                act.wait_ge(sq_ready, sq_n)
                for i, half in enumerate("ab"):
                    bank = wait_full(act, seg, it, f"h2T{t}{half}")
                    nc.scalar.copy(h2T[:, 4 * i:4 * i + 4, :], bank[:, :].rearrange("p (k n) -> p k n", k=4))\
                        .then_inc(read(seg, f"h2T{t}{half}"), 1)

            def router_exp(t, gp):
                act.wait_ge(dv_ready, gp * GT + t + 1)
                nc.scalar.activation(dv[:, t, 0:NG + 1], dv[:, t, 0:NG + 1], ACT.Exp).then_inc(dve_exp, 1)

            def square(src, col, n):
                wait(act, sq_ready, n)
                nc.scalar.activation(h2T[:].rearrange("p a b -> p (a b)"), src, ACT.Square,
                                     accum_out=ssq[:, col:col + 1]).then_inc(sq_ready, 1)

            def input_columns(seg, it, tiles):
                n = tiles * P
                for j in range(4):
                    bank = wait_full(act, seg, it, f"xT{j}")
                    nc.scalar.copy(hT[:, 2 * j:2 * j + 2, 0:n], bank[:, 0:2 * n].rearrange("p (k n) -> p k n", k=2))\
                        .then_inc(read(seg, f"xT{j}"), 1)

            def group(seg, it, g, tiles, prev, ahead):
                n = tiles * P
                act.wait_ge(halo_ready, g + 1)
                for p in range(2):
                    bank = wait_full(act, seg, it, f"xb{p}")
                    if seg == "last":
                        for cc in range(2):
                            ins = nc.scalar.copy(xbs[:, 2 * p + cc, :, TAPS - 1:],
                                                 bank[:, cc * n:(cc + 1) * n].rearrange("p (s f) -> p s f", f=FRAMES))
                    else:
                        ins = nc.scalar.copy(xbT[:, 2 * p:2 * p + 2, TAPS - 1:],
                                             bank[:, 0:2 * n].rearrange("p (c n) -> p c n", c=2))
                    ins.then_inc(read(seg, f"xb{p}"), 1)
                for t in range(prev):
                    h2_columns(seg, it, t, g - 1, squares(g - 1, "x1", prev - 1) + 1)
                for t in range(prev):
                    router_exp(t, g - 1)
                for c in range(NC):
                    bank = wait_full(act, seg, it, f"ga{c}")
                    for m in range(2):
                        ins = nc.scalar.activation(ri[:, m, c, 0:n], bank[:, m * n:(m + 1) * n], ACT.Sigmoid,
                                                   bias=nb[:, m, c:c + 1])
                    ins.then_inc(read(seg, f"ga{c}"), 1)
                for t in range(ahead):
                    act.wait_ge(xa_loaded[t], 16 * g + 32)
                    square(xa[:, t], t, squares(g + 1, "in", t))
                if seg == "first":
                    act.wait_ge(table_ready, 16 * 8)
                    act.wait_ge(const_dve, 9)
                wait_out(act, seg, it, f"ga{NC - 1}")
                for c in range(NC):
                    nc.scalar.activation(aT[:, c, 0:n], ri[:, 0, c, 0:n], ACT.Exp, scale=nsp[:, c:c + 1])
                    nc.scalar.activation(ri[:, 0, c, 0:n], ri[:, 0, c, 0:n], ACT.Tanh, scale=nsp[:, c:c + 1])\
                        .then_inc(at_ready, 1)
                for p in range(2):
                    bank = wait_full(act, seg, it, f"gg{p}")
                    v = bank[:, 0:2 * n].rearrange("p (c n) -> p c n", c=2)
                    nc.scalar.copy(gS[:, 2 * p:2 * p + 2, 0:n], v)
                    nc.scalar.activation(gt[:, 2 * p:2 * p + 2, 0:n], v, ACT.Square)\
                        .then_inc(read(seg, f"gg{p}"), 1)
                act.wait_ge(gin_ready, g + 1)
                nc.scalar.activation(gt[:, :, 0:n], gt[:, :, 0:n], ACT.Tanh, scale=GELU_C).then_inc(gth_ready, 1)
                act.wait_ge(q_ready, g + 1)
                nc.scalar.activation(qT[:, :, 0:n], qT[:, :, 0:n], ACT.Sqrt, scale=-1.0).then_inc(gain_ready, 1)
                if ahead:
                    input_columns(seg, it, ahead)
                for t in range(tiles):
                    wait_out(act, seg, it, f"o{t}1")
                    square(xr[:, t], GT + t, squares(g, "x1", t))

            for t in range(GT):
                act.wait_ge(xa_loaded[t], 16)
                square(xa[:, t], t, squares(0, "in", t))
            act.wait_ge(const_dma, 16 * N_CONST)
            nc.scalar.activation(lamt[:, 0], lam[:], ACT.Relu, scale=-1.0).then_inc(act_link, 1)
            nc.scalar.activation(lamt[:, 1], lam[:], ACT.Abs).then_inc(act_link, 1)
            act.wait_ge(act_link, 2)
            nc.scalar.activation(lamt[:, 1], lamt[:, 1], ACT.Exp, scale=-1.0).then_inc(act_link, 1)
            act.wait_ge(act_link, 3)
            act.wait_ge(const_dve, 4)
            nc.scalar.activation(lamt[:, 2], lamt[:, 1], ACT.Ln, bias=ones[:, 0:1]).then_inc(act_link, 1)

            input_columns("start", 0, GT)
            group("first", 0, 0, GT, 0, GT)
            with act.Fori(1, NPG - 1) as g:
                group("loop", g - 1, g, GT, GT, GT)
            group("final", 0, NPG - 1, GT, GT, 1)
            group("last", 0, NPG, 1, GT, 0)
            h2_columns("tail", 0, 0, NPG, squares(NPG, "x1", 0) + 1)
            router_exp(0, NPG)

            wait_out(act, "plan", 0, "plan")
            chunks = act.value_load(plan[0:1, 2 * P:2 * P + 1], min_val=2, max_val=P - 1)

            def x_columns(seg, q):
                for j, (lo, hi) in enumerate(XT3):
                    bank = wait_full(act, seg, q, f"xT{j}")
                    nc.scalar.copy(xTm[:, lo:hi, :], bank[:, 0:(hi - lo) * CH].rearrange("p (k n) -> p k n", n=CH))\
                        .then_inc(read(seg, f"xT{j}"), 1)

            x_columns("pre", 0)
            with act.Fori(0, chunks) as q:
                for f in range(KE):
                    bank = wait_full(act, "chunk", q, f"gu{f}")
                    nc.scalar.activation(sg[:, f, :], bank[:, 0:CH], ACT.Silu).then_inc(sg_ready, 1)
                x_columns("chunk", q)
                act.wait_ge(io_loaded, 16 * q + 16)
                for i in range(2):
                    bank = wait_full(act, "chunk", q, f"r{i}0")
                    nc.scalar.activation(ysb[:, 0, i * BANK:(i + 1) * BANK], bank[0:HF, :], ACT.Copy,
                                         scale=idx_out[:, 0, 1:2].bitcast(F32)).then_inc(read("chunk", f"r{i}0"), 1)

            def final(it, b):
                act.wait_ge(f_loaded[b], 16 * it + 16)
                act.wait_ge(f_sq, it * 4 + 1)
                unused = (catT[:, 0:4], catT[:, 4:8], gS[:], gt[:])[b]
                nc.scalar.activation(unused.rearrange("p a b -> p (a b)"), fb[b], ACT.Square,
                                     accum_out=ssq[:, b:b + 1]).then_inc(f_sq, 1)

            def store(it, b):
                act.wait_ge(f_ready, it * 4 + b + 1)
                act.dma_start(a["y"].rearrange("(n p) d -> n p d", p=P)[bass.ds(it * 4 + b, 1)]
                              .rearrange("a p d -> p (a d)"), fb[b]).then_inc(f_stored[b], 16)

            act.nop().then_inc(f_sq, 1)
            with act.Fori(0, NTILE // 4) as it:
                for b in range(4):
                    final(it, b)
                for b in range(4):
                    store(it, b)
            final(NTILE // 4, 0)
            store(NTILE // 4, 0)

        @block.vector
        def _(dve):
            V = nc.vector

            def linked(s):
                state = [0, 0]

                def start(base):
                    state[0], state[1] = base, 0

                def link(ins):
                    state[1] += 1
                    ins.then_inc(s, 1)
                    dve.wait_ge(s, state[0] + state[1])

                return start, link, state

            start_m, link, main = linked(dve_main)
            start_c, clink, choose_n = linked(dve_choose)
            start_a, alink, assign_n = linked(dve_assign)
            start_p, plink, plan_n = linked(dve_plan)

            def input_rows(g, tiles):
                for t in range(tiles):
                    dve.wait_ge(rs_ready, squares(g, "in", t) + 1)
                    V.scalar_tensor_tensor(out=xa[:, t], in0=xa[:, t], scalar=rstd[:, t:t + 1], in1=g1b[:],
                                           op0=ALU.mult, op1=ALU.mult).then_inc(xn_ready, 1)

            V.memset(wgate[:], 0.0).then_inc(const_dve, 1)
            V.memset(wsTs[:], 0.0).then_inc(const_dve, 1)
            V.memset(zrow[:], 0.0).then_inc(const_dve, 1)
            V.memset(ones[:], 1.0).then_inc(const_dve, 1)
            V.memset(gl[:], -3.0e38).then_inc(const_dve, 1)
            V.memset(count[:], 0.0).then_inc(const_dve, 1)
            V.memset(hlast[:], 0.0).then_inc(const_dve, 1)
            V.memset(xbT[:, :, 0:TAPS - 1], 0.0).then_inc(halo_ready, 1)
            dve.wait_ge(const_dve, 7)
            dve.wait_ge(g1_loaded, 16)
            input_rows(0, GT)
            dve.wait_ge(const_dma, 16 * N_CONST)
            dve.wait_ge(act_link, 4)
            V.tensor_tensor(lamt[:, 0], lamt[:, 0], lamt[:, 2], ALU.add).then_inc(const_dve, 1)
            dve.wait_ge(const_dve, 8)
            V.tensor_scalar(nsp[:], lamt[:, 0], -8.0, None, ALU.mult).then_inc(const_dve, 1)
            MAIN, CHOOSE, ASSIGN = 22, 13, 9

            def group(seg, it, g, tiles, prev, ahead):
                n = tiles * P
                start_m(g * MAIN)
                for c in range(NC):
                    if c % 2 == 0:
                        wait_out(dve, seg, it, f"xb{c // 2}")
                    if seg == "last":
                        src = [xbs[:, c, :, k:k + FRAMES] for k in range(TAPS)]
                        dst = xcT[:, c, 0:n].rearrange("p (s f) -> p s f", f=FRAMES)
                    else:
                        src = [xbT[:, c, k:k + n] for k in range(TAPS)]
                        dst = xcT[:, c, :]
                    link(V.tensor_scalar(dst, src[0], cw[:, c, 0:1], cb[:, c:c + 1], ALU.mult, ALU.add))
                    for k in range(1, TAPS):
                        ins = V.scalar_tensor_tensor(out=dst, in0=src[k], scalar=cw[:, c, k:k + 1], in1=dst,
                                                     op0=ALU.mult, op1=ALU.add)
                        if k < TAPS - 1:
                            link(ins)
                    ins.then_inc(xc_ready, 1)
                if seg != "last":
                    V.tensor_copy(xbT[:, :, 0:TAPS - 1], xbT[:, :, G:G + TAPS - 1]).then_inc(halo_ready, 1)
                for t in range(prev):
                    choose(seg, it, t, g - 1)
                for t in range(tiles):
                    bank = wait_full(dve, seg, it, f"v{t}")
                    for c in range(NC):
                        ins = V.bn_stats(vst[:, t, c, :], bank[:, c * P:(c + 1) * P])
                    link(ins)
                    carry(dve)
                    for c in range(NC):
                        ins = V.bn_aggr(vmv[:, t, c, :], vst[:, t, c, :])
                    ins.then_inc(var_ready, 1)
                    dve.wait_ge(vrs_ready, g * GT + t + 1)
                    for c in range(NC):
                        ins = V.tensor_scalar(vn[:, t, c * P:(c + 1) * P], bank[:, c * P:(c + 1) * P],
                                              vmv[:, t, c, 0:1], vrs[:, t, c:c + 1], ALU.subtract, ALU.mult)
                    ins.then_inc(read(seg, f"v{t}"), 1)
                    wait_out(dve, seg, it, f"v{t}")
                    link(V.tensor_tensor(vn[:, t], vn[:, t], lngb[:], ALU.mult))
                    V.tensor_tensor(vn[:, t], vn[:, t], lnbb[:], ALU.add).then_inc(vn_ready, 1)
                wait_out(dve, seg, it, f"ga{NC - 1}")
                if seg == "first":
                    dve.wait_ge(table_ready, 16 * 8)
                iv, rv, av, qv = ri[:, 1, :, 0:n], ri[:, 0, :, 0:n], aT[:, :, 0:n], qT[:, :, 0:n]
                link(V.tensor_tensor(iv, iv, xcT[:, :, 0:n], ALU.mult))
                dve.wait_ge(at_ready, NC * g + NC)
                link(V.tensor_tensor(qv, av, av, ALU.mult))
                V.scalar_tensor_tensor(out=qv, in0=qv, scalar=1.0, in1=rv, op0=ALU.add, op1=ALU.mult).then_inc(q_ready, 1)
                wait_out(dve, seg, it, "gg1")
                gv, tv = gS[:, :, 0:n], gt[:, :, 0:n]
                link(V.tensor_scalar(tv, tv, 0.044715, 1.0, ALU.mult, ALU.add))
                V.tensor_tensor(tv, tv, gv, ALU.mult).then_inc(gin_ready, 1)
                dve.wait_ge(gain_ready, g + 1)
                link(V.tensor_tensor(iv, iv, qv, ALU.mult))
                for c in range(NC):
                    if seg == "last":
                        for s in range(STREAMS):
                            r = slice(FRAMES * s, FRAMES * (s + 1))
                            ins = V.tensor_tensor_scan(qT[:, c, r], aT[:, c, r], ri[:, 1, c, r], h0s[:, c, s:s + 1],
                                                       ALU.mult, ALU.add)
                    else:
                        ins = V.tensor_tensor_scan(qT[:, c, :], aT[:, c, :], ri[:, 1, c, :], hlast[:, c:c + 1],
                                                   ALU.mult, ALU.add)
                link(ins)
                if seg != "last":
                    V.tensor_copy(hlast[:], qT[:, :, G - 1]).then_inc(h_ready, 1)
                else:
                    V.tensor_copy(h0s[:], qT[:, :, FRAMES - 1:P:FRAMES]).then_inc(h_ready, 1)
                dve.wait_ge(gth_ready, g + 1)
                link(V.scalar_tensor_tensor(out=tv, in0=tv, scalar=1.0, in1=gv, op0=ALU.add, op1=ALU.mult))
                V.scalar_tensor_tensor(out=catT[:, NC:, 0:n], in0=tv, scalar=0.5, in1=qv, op0=ALU.mult,
                                       op1=ALU.mult).then_inc(cat_ready, 1)
                input_rows(g + 1, ahead)
                if prev:
                    assign(seg, it, prev, g - 1)
                for t in range(tiles):
                    bank = wait_full(dve, seg, it, f"s{t}")
                    if seg == "last":
                        for c in range(NC):
                            ins = V.tensor_tensor(
                                sS[:, c, 0:n].rearrange("p (s f) -> p s f", f=FRAMES),
                                bank[:, c * P:(c + 1) * P].rearrange("p (s f) -> p s f", f=FRAMES),
                                bsb[:, c:c + 1, 0:FRAMES].broadcast_to([P, STREAMS, FRAMES]), ALU.add)
                    else:
                        ins = V.tensor_tensor(sS[:, :, t * P:(t + 1) * P], bank[:, :].rearrange("p (c n) -> p c n", c=NC),
                                              bsb[:], ALU.add)
                    ins.then_inc(read(seg, f"s{t}"), 1)
                    wait_out(dve, seg, it, f"s{t}")
                for p in range(2):
                    bank = wait_full(dve, seg, it, f"u{p}")
                    V.tensor_tensor(catT[:, 2 * p:2 * p + 2, 0:n], bank[:, 0:2 * n].rearrange("p (c n) -> p c n", c=2),
                                    sS[:, 2 * p:2 * p + 2, 0:n], ALU.mult).then_inc(read(seg, f"u{p}"), 1)
                for t in range(tiles):
                    dve.wait_ge(xr_loaded[t], 16 * g + 16)
                    for h in range(2):
                        bank = wait_full(dve, seg, it, f"o{t}{h}")
                        x = xr[:, t, h * BANK:(h + 1) * BANK]
                        V.tensor_tensor(x, bank[:, :], x, ALU.add).then_inc(read(seg, f"o{t}{h}"), 1)
                for t in range(tiles):
                    dve.wait_ge(rs_ready, squares(g, "x1", t) + 1)
                    dve.wait_ge(acc_stored[t], 16 * g + 16)
                    V.scalar_tensor_tensor(out=xr[:, t], in0=xr[:, t], scalar=rstd[:, GT + t:GT + t + 1], in1=g2b[:],
                                           op0=ALU.mult, op1=ALU.mult).then_inc(h2_ready[t], 1)
                if seg == "first":
                    assert main[1] == MAIN, main[1]

            def choose(seg, it, t, gp):
                start_c((gp * GT + t) * CHOOSE)
                bank = wait_full(dve, seg, it, f"lg{t}")
                V.tensor_tensor(gl[:, t, 0:NG], bank[:, 0:NG], rb[:, 0:NG], ALU.add)
                V.tensor_tensor(el[:, t], bank[:, NG:NG + NE], rb[:, NG:], ALU.add).then_inc(read(seg, f"lg{t}"), 1)
                wait_out(dve, seg, it, f"lg{t}")
                carry(dve)
                clink(V.max(m8[:, t, 0], gl[:, t]))
                carry(dve)
                clink(V.max_index(i8[:, t, 0], m8[:, t, 0], gl[:, t]))
                clink(V.tensor_copy(rf[:, t, 0:1], i8[:, t, 0, 0:1]))
                clink(V.tensor_scalar(mk[:, t], iota32[:, 0:NG], rf[:, t, 0:1], None, ALU.is_equal))
                clink(V.tensor_scalar(ein[:, t], el[:, t, 0:EPG], mk[:, t, 0:1], None, ALU.mult))
                for j in range(1, NG):
                    clink(V.scalar_tensor_tensor(out=ein[:, t], in0=el[:, t, j * EPG:(j + 1) * EPG],
                                                 scalar=mk[:, t, j:j + 1], in1=ein[:, t], op0=ALU.mult, op1=ALU.add))
                carry(dve)
                clink(V.max(m8[:, t, 1], ein[:, t]))
                carry(dve)
                clink(V.max_index(i8[:, t, 1], m8[:, t, 1], ein[:, t]))
                V.tensor_scalar(rf[:, t, 3:4], rf[:, t, 0:1], float(EPG), None, ALU.mult)
                clink(V.tensor_copy(rf[:, t, 1:3], i8[:, t, 1, 0:2]))
                clink(V.tensor_scalar(rf[:, t, 1:3], rf[:, t, 1:3], rf[:, t, 3:4], None, ALU.add))
                V.tensor_scalar(hot[:, t, 0], iota32[:], rf[:, t, 1:2], None, ALU.is_equal)
                clink(V.tensor_scalar(hot[:, t, 1], iota32[:], rf[:, t, 2:3], None, ALU.is_equal))
                V.tensor_tensor(hot[:, t, 2], hot[:, t, 0], hot[:, t, 1], ALU.add).then_inc(hot_ready, 1)
                V.tensor_scalar(dv[:, t, 0:NG], gl[:, t, 0:NG], m8[:, t, 0, 0:1], None, ALU.subtract)
                V.tensor_tensor(dv[:, t, NG:NG + 1], m8[:, t, 1, 1:2], m8[:, t, 1, 0:1], ALU.subtract).then_inc(dv_ready, 1)
                assert choose_n[1] == CHOOSE, choose_n[1]

            def assign(seg, it, tiles, gp):
                bank = wait_full(dve, seg, it, "pf")
                for t in range(tiles):
                    start_a((gp * GT + t) * ASSIGN)
                    dve.wait_ge(pay_free, gp + 1)
                    dve.wait_ge(dve_exp, gp * GT + t + 1)
                    alink(V.reduce_sum(rf[:, t, 4:5], dv[:, t, 0:NG], AX.X))
                    alink(V.scalar_tensor_tensor(out=rf[:, t, 5:6], in0=dv[:, t, NG:NG + 1], scalar=1.0,
                                                 in1=rf[:, t, 4:5], op0=ALU.add, op1=ALU.mult))
                    alink(V.reciprocal(rf[:, t, 6:7], rf[:, t, 5:6]))
                    V.tensor_copy(pay[:, t, 0, 1:2].bitcast(F32), rf[:, t, 6:7])
                    alink(V.tensor_tensor(pay[:, t, 1, 1:2].bitcast(F32), rf[:, t, 6:7], dv[:, t, NG:NG + 1], ALU.mult))
                    V.tensor_copy(pay[:, t, 0, 0:1], tokf[:])
                    V.tensor_copy(pay[:, t, 1, 0:1], tokf[:])
                    alink(V.tensor_scalar(tokf[:], tokf[:], float(P), None, ALU.add))
                    alink(V.tensor_tensor(rk[:], bank[:, 64 * t:64 * t + NE], count[:], ALU.add))
                    alink(V.tensor_tensor(rk[:], rk[:], ebase[:], ALU.add))
                    for k in range(2):
                        alink(V.tensor_tensor_reduce(rkj[:], hot[:, t, k], rk[:], 1.0, 0.0, ALU.mult, ALU.add,
                                                     slotf[:, t, k:k + 1]))
                    V.tensor_copy(slot[:, t], slotf[:, t]).then_inc(slot_ready, 1)
                    ins = V.tensor_tensor(count[:], count[:], bank[:, 64 * t + NE:64 * t + 2 * NE], ALU.add)
                    if t < tiles - 1:
                        ins.then_inc(count_ready, 1)
                        dve.wait_ge(count_ready, gp + 1)
                    assert assign_n[1] == ASSIGN, assign_n[1]
                ins.then_inc(read(seg, "pf"), 1)
                wait_out(dve, seg, it, "pf")

            group("first", 0, 0, GT, 0, GT)
            dve.wait_ge(const_pool, 9)
            with dve.Fori(1, NPG - 1) as g:
                group("loop", g - 1, g, GT, GT, GT)
            group("final", 0, NPG - 1, GT, GT, 1)
            group("last", 0, NPG, 1, GT, 0)
            choose("tail", 0, 0, NPG)
            assign("tail", 0, 1, NPG)

            start_p(0)
            plink(V.tensor_scalar(nch[:], count[:], CH / 2 - 0.5, 1.0 / CH, ALU.add, ALU.mult))
            plink(V.tensor_scalar(nch[:], nch[:], 1.5 * 2 ** 23, None, ALU.add))
            plink(V.tensor_scalar(nch[:], nch[:], -1.5 * 2 ** 23, None, ALU.add))
            plink(V.tensor_scalar(nch[:, 0:2], nch[:, 0:2], 1.0, None, ALU.max))
            plink(V.tensor_tensor_scan(cend[:], ones[:, 0:NE], nch[:], 0.0, ALU.mult, ALU.add))
            plink(V.tensor_scalar(ple[:, 0], cend[:], pcol[:, 0:1], None, ALU.is_le))
            plink(V.reduce_sum(pq[:, 0:1], ple[:, 0], AX.X))
            plink(V.tensor_tensor_reduce(ple[:, 1], ple[:, 0], nch[:], 1.0, 0.0, ALU.mult, ALU.add, pq[:, 1:2]))
            plink(V.tensor_scalar(pq[:, 0:1], pq[:, 0:1], float(NE - 1), None, ALU.min))
            plink(V.tensor_tensor(pq[:, 1:2], pcol[:], pq[:, 1:2], ALU.subtract))
            plink(V.tensor_scalar(pq[:, 1:2], pq[:, 1:2], float(CPE - 1), float(CH), ALU.min, ALU.mult))
            plink(V.tensor_scalar(pq[:, 2:3], pq[:, 0:1], float(SLOTS), None, ALU.mult))
            plink(V.tensor_tensor(pq[:, 1:2], pq[:, 1:2], pq[:, 2:3], ALU.add))
            V.tensor_scalar(diag[:, 0], ident[:], pq[:, 0:1], None, ALU.mult)
            V.tensor_scalar(diag[:, 1], ident[:], pq[:, 1:2], None, ALU.mult).then_inc(diag_ready, 1)
            bank = wait_full(dve, "plan", 0, "plan")
            V.tensor_copy(plan[0:1, 2 * P:2 * P + 1], cend[0:1, NE - 1:NE]).then_inc(plan_ready, 1)
            dve.wait_ge(plan_ready, 1)
            V.tensor_copy(plan[0:1, 0:2 * P], bank[0:1, 0:2 * P]).then_inc(read("plan", "plan"), 1)
            wait_out(dve, "plan", 0, "plan")
            chunks = dve.value_load(plan[0:1, 2 * P:2 * P + 1], min_val=2, max_val=P - 1)
            with dve.Fori(0, chunks) as q:
                for f in range(KE):
                    bank = ps[JOBS.bank("chunk", f"gu{f}")]
                    dve.wait_ge(sg_ready, KE * q + f + 1)
                    V.tensor_tensor(hTm[:, f, :], bank[:, CH:2 * CH], sg[:, f, :], ALU.mult)\
                        .then_inc(read("chunk", f"gu{f}"), 1)
                for j, (lo, hi) in enumerate(XT3):
                    bank = wait_full(dve, "chunk", q, f"y{j}")
                    V.tensor_copy(yT[:, lo:hi, :], bank[:, 0:(hi - lo) * CH].rearrange("p (k n) -> p k n", n=CH))\
                        .then_inc(read("chunk", f"y{j}"), 1)
                dve.wait_ge(io_loaded, 16 * q + 16)
                for i in range(2):
                    bank = wait_full(dve, "chunk", q, f"r{i}1")
                    V.tensor_scalar(ysb[:, 1, i * BANK:(i + 1) * BANK], bank[0:HF, :],
                                    idx_out[:, 1, 1:2].bitcast(F32), None, ALU.mult)\
                        .then_inc(read("chunk", f"r{i}1"), 1)

            dve.wait_ge(fg_loaded, 16)

            def final(it, b):
                dve.wait_ge(f_rs, it * 4 + b + 1)
                V.scalar_tensor_tensor(out=fb[b], in0=fb[b], scalar=rstd[:, b:b + 1], in1=g1b[:],
                                       op0=ALU.mult, op1=ALU.mult).then_inc(f_ready, 1)

            with dve.Fori(0, NTILE // 4) as it:
                for b in range(4):
                    final(it, b)
            final(NTILE // 4, 0)


def kernel(**inputs):
    import numpy as np
    import concourse.bacc as bacc
    from concourse.bass_utils import run_bass_kernel_spmd

    x = {n: np.ascontiguousarray(v) for n, v in inputs.items()}
    cols = lambda v: np.ascontiguousarray(v.reshape(-1, NC, P).transpose(2, 1, 0))
    arrays = {
        "x": np.concatenate([x["x_prompt"].reshape(SEQ, D), x["x_sample"].reshape(-1, D)]),
        "conv_state": cols(x["state_conv"][0].reshape(-1, DA)).reshape(P, NC, STREAMS, TAPS - 1),
        "h0": cols(x["state_rglru"][0]),
        "norm1_g": x["norm1_g"], "w_in": x["w_in"][0], "ln_g": x["gmlp_ln_g"], "ln_b": x["gmlp_ln_b"],
        "w_sT": np.ascontiguousarray(x["gmlp_w_s"][0].transpose(0, 2, 1)),
        "b_s": x["gmlp_b_s"][0].reshape(1, NC * P),
        "conv_w": cols(x["conv_w"][0]), "conv_b": cols(x["conv_b"])[:, :, 0].copy(),
        "lru_w": np.stack([x["lru_w_a"][0], x["lru_w_x"][0]]),
        "gate_b": np.stack([cols(x[n].reshape(1, DA))[:, :, 0] for n in ("lru_b_a", "lru_b_x")], axis=1),
        "lam": cols(x["lru_lambda"])[:, :, 0].copy(),
        "w_out": x["w_out"][0], "norm2_g": x["norm2_g"],
        "router_gw": x["router_group_w"][0], "router_ew": x["router_expert_w"][0],
        "router_b": np.concatenate([x["router_group_b"], x["router_expert_b"]], axis=1),
        "w_gate": x["expert_w_gate"][0], "w_up": x["expert_w_up"][0], "w_down": x["expert_w_down"][0],
        "final_g": x["final_norm_g"].reshape(1, D),
    }
    outs = {"y": (NTOK, D), "conv_p": (P, NC, TAPS - 1), "h_p": (P, NC), "v_s": (STREAMS * FRAMES, DA),
            "conv_s": (P, NC, STREAMS, TAPS - 1), "h_s": (P, NC, STREAMS)}
    nc = bacc.Bacc("TRN2", target_bir_lowering=False, num_devices=1)
    aps = {n: nc.dram_tensor(f"in_{n}", v.shape, F32, kind="ExternalInput").ap() for n, v in arrays.items()}
    aps |= {n: nc.dram_tensor(f"out_{n}", v, F32, kind="ExternalOutput").ap() for n, v in outs.items()}
    hymba_step(nc, aps)
    r = run_bass_kernel_spmd(nc, [{f"in_{n}": v for n, v in arrays.items()}], core_ids=[0]).results[0]
    y = r["out_y"]
    rows = lambda v: np.moveaxis(v, (1, 0), (-2, -1)).reshape(*v.shape[2:], DA)
    return (y[:SEQ].reshape(1, SEQ, D), y[SEQ:].reshape(STREAMS, FRAMES, D),
            rows(r["out_conv_p"]).reshape(1, 1, TAPS - 1, DA), rows(r["out_h_p"]).reshape(1, 1, DA),
            r["out_v_s"].reshape(1, STREAMS, FRAMES, DA), rows(r["out_conv_s"]).reshape(1, STREAMS, TAPS - 1, DA),
            rows(r["out_h_s"]).reshape(1, STREAMS, DA))
```

```python
from contextlib import ExitStack

import concourse.bass as bass
from concourse import mybir

ALU = mybir.AluOpType
ACT = mybir.ActivationFunctionType
AX = mybir.AxisListType
F32 = mybir.dt.float32
U32 = mybir.dt.uint32
I32 = mybir.dt.int32

P = 128
D = 1024
KD = D // P
DA = 512
NC = DA // P
GT = 2
G = GT * P
SEQ = 2048
NPG = SEQ // G
STREAMS, FRAMES = 8, 16
NTOK = SEQ + STREAMS * FRAMES
NTILE = NTOK // P
TAPS = 4
NG, EPG = 4, 8
NE = NG * EPG
DE = 512
KE = DE // P
SIZES = (180, 156, 140, 132, 128)
CH = SIZES[0]
HF = CH // 2
CPE = -(-NTOK // CH)
SLOTS = CPE * CH
TMIN = 66
NW = NE + 1
NROW = NTOK + CH
EPS = 1e-6
GELU_C = 0.7978845608028654
BANKS = 8
BANK = 512
N_PAD = 96
FB = 8


class PsumJobs:

    def __init__(self, segments):
        self.first, self.per, self.where = {}, {}, {}
        done = [0] * BANKS
        for name, times, jobs in segments:
            per = [0] * BANKS
            for j, job in enumerate(jobs):
                self.where[name, job] = (j % BANKS, per[j % BANKS])
                per[j % BANKS] += 1
            self.first[name], self.per[name] = list(done), per
            done = [d + times * p for d, p in zip(done, per)]

    def bank(self, seg, job):
        return self.where[seg, job][0]

    def before(self, seg, it, job):
        b, u = self.where[seg, job]
        return it * self.per[seg][b] + (self.first[seg][b] + u)


def group_jobs(tiles, prev, ahead):
    jobs = []
    for t in range(2):
        jobs += [f"xb{t}"] + ([f"lg{t - 1}"] if 0 < t <= prev else [])
        jobs += [f"h2T{t}a", f"h2T{t}b"] if t < prev else []
    jobs += ["v0"] + (["lg1"] if prev > 1 else []) + [f"v{t}" for t in range(1, tiles)]
    jobs += [f"ga{c}" for c in range(NC)] + ["gg0", "gg1"] + (["pf"] if prev else [])
    jobs += [f"s{t}" for t in range(tiles)] + ["u0", "u1"]
    jobs += [f"xT{j}" for j in range(4)] if ahead else []
    return jobs + [f"o{t}{h}" for t in range(tiles) for h in range(2)]


PAIRS = range(KD // 2)
JOBS = PsumJobs([
    ("start", 1, [f"xT{j}" for j in range(4)]),
    ("first", 1, group_jobs(GT, 0, GT)),
    ("loop", NPG - 2, group_jobs(GT, GT, GT)),
    ("final", 1, group_jobs(GT, GT, 1)),
    ("last", 1, group_jobs(1, GT, 0)),
    ("tail", 1, ["h2T0a", "h2T0b", "lg0", "pf"]),
    ("plan", 1, ["plan"]),
    ("pre", 1, [f"xT{j}" for j in PAIRS]),
    ("chunk", 1, [f"gu{f}" for f in range(KE)] + [f"xT{j}" for j in PAIRS] + [f"y{j}" for j in PAIRS]
     + ["r00", "r01", "r10", "r11"]),
])


def squares(g, what, t):
    if what == "in":
        if isinstance(g, int) and g == 0:
            return t
        return (g - 1) * 2 * GT + GT + t
    if isinstance(g, int) and g >= NPG - 1:
        return (NPG - 1) * 2 * GT + GT + 1 + (g - NPG + 1) * GT + t
    return g * 2 * GT + 2 * GT + t


def hymba_step(nc, a):
    with ExitStack() as ctx:
        def sb(name, shape, dt=F32):
            return ctx.enter_context(nc.sbuf_tensor(name, shape, dt))

        def sem(name):
            return ctx.enter_context(nc.semaphore(name))

        acc = nc.dram_tensor("acc_rows", [NROW, D], F32).ap()
        h2_rows = nc.dram_tensor("h2_rows", [NROW, D], F32).ap()
        table = nc.dram_tensor("slot_table", [NE * SLOTS + CH, 2], U32).ap()

        w_in = sb("w_in_sb", [P, KD * 2048])
        w_out = sb("w_out_sb", [P, KD * D])
        w_in_v = w_in[:].rearrange("p (k n) -> p k n", k=KD)
        w_out_v = w_out[:].rearrange("p (k n) -> p k n", k=KD)
        xa = sb("xa", [P, GT, D])
        xr = sb("xr", [P, GT, D])
        h2T = sb("h2T", [P, KD, P])
        hT = sb("hT", [P, KD, G])
        xbT = sb("xbT", [P, NC, TAPS - 1 + G])
        xbs = sb("xbs", [P, NC, STREAMS, TAPS - 1 + FRAMES])
        xcT = sb("xcT", [P, NC, G])
        ri = sb("ri", [P, 2, NC, G])
        aT = sb("aT", [P, NC, G])
        qT = sb("qT", [P, NC, G])
        gS = sb("gS", [P, NC, G])
        gt = sb("gt", [P, NC, G])
        sS = sb("sS", [P, NC, G])
        catT = sb("catT", [P, KD, G])
        vn = sb("vn", [P, GT, DA])
        g1b = sb("g1b", [P, D])
        g2b = sb("g2b", [P, D])
        lngb = sb("lngb", [P, DA])
        lnbb = sb("lnbb", [P, DA])
        bsb = sb("bsb", [P, NC, P])
        wsT = sb("wsT", [P, NC, P])
        wsTs = sb("wsTs", [P, NC, P])
        wgate = sb("wgate", [P, 2, NC, P])
        rw = sb("rw", [P, KD, NG + NE])
        rb = sb("rb", [P, NG + NE])
        ident = sb("ident", [P, P])
        before = sb("before", [P, P])
        ones = sb("ones", [P, len(SIZES) * NW])
        cw = sb("cw", [P, NC, TAPS])
        cb = sb("cb", [P, NC])
        nb = sb("nb", [P, 2, NC])
        lam = sb("lam", [P, NC])
        lamt = sb("lamt", [P, 3, NC])
        nsp = sb("nsp", [P, NC])
        hlast = sb("hlast", [P, NC])
        h0s = sb("h0s", [P, NC, STREAMS])
        mhalf = sb("mhalf", [P, NC])
        pad = sb("pad", [P, N_PAD])
        ssq = sb("ssq", [P, FB])
        rstd = sb("rstd", [P, FB])
        vst = sb("vst", [P, GT, NC, 6])
        vmv = sb("vmv", [P, GT, NC, 2])
        vrs = sb("vrs", [P, GT, NC])
        gl = sb("gl", [P, GT, 8])
        el = sb("el", [P, GT, NE])
        m8 = sb("m8", [P, GT, 2, 8])
        i8 = sb("i8", [P, GT, 2, 8], U32)
        rf = sb("rf", [P, GT, 16])
        dv = sb("dv", [P, GT, 8])
        mk = sb("mk", [P, GT, NG])
        ein = sb("ein", [P, GT, EPG])
        hot = sb("hot", [P, GT, 3, NE])
        iota32 = sb("iota32", [P, NW])
        ebase = sb("ebase", [P, NW])
        tokf = sb("tokf", [P, 1])
        pcol = sb("pcol", [P, 1])
        count = sb("count", [P, NW])
        rk = sb("rk", [P, NE])
        places = sb("places", [P, 64 * GT])
        slotf = sb("slotf", [P, GT, 2])
        slot = sb("slot", [P, GT, 2], U32)
        pay = sb("pay", [P, GT, 2, 2], U32)
        whole = sb("whole", [P, NW])
        rest = sb("rest", [P, NW])
        rkj = whole
        nch = sb("nch", [P, len(SIZES), NW])
        cend = sb("cend", [P, len(SIZES), NW])
        n = len(SIZES) * NW
        by_size = gS[:].rearrange("p a b -> p (a b)")[:, 0:5 * n].rearrange("p (x k e) -> p x k e", x=5, e=NW)
        over = by_size[:, 4]
        cstart, cslot, mine = by_size[:, 0], by_size[:, 1], by_size[:, 2:4]
        pq = sb("pq", [P, 8])
        diag = sb("diag", [P, 2, P])
        plan = sb("plan", [1, 2 * P + len(SIZES)], I32)
        idx_in = sb("idx_in", [HF, 2, 2], U32)
        idx_out = sb("idx_out", [HF, 2, 2], U32)
        o = 0
        wg_e = w_in[:, o:o + KD * DE].rearrange("p (k f) -> p k f", k=KD)
        o += KD * DE
        wu_e = w_in[:, o:o + KD * DE].rearrange("p (k f) -> p k f", k=KD)
        o += KD * DE
        wd_e = w_in[:, o:o + KE * D].rearrange("p (f d) -> p f d", f=KE)
        o += KE * D
        xg = w_in[0:HF, o:o + 2 * D].rearrange("p (h d) -> p h d", h=2)
        o += 2 * D
        ysb = w_in[0:HF, o:o + 2 * D].rearrange("p (h d) -> p h d", h=2)
        o = 0
        xTm = w_out[:, o:o + KD * CH].rearrange("p (k h n) -> p k h n", k=KD, h=2)
        o += KD * CH
        hTm = w_out[:, o:o + KE * CH].rearrange("p (k n) -> p k n", k=KE)
        o += KE * CH
        sg = w_out[:, o:o + KE * CH].rearrange("p (k n) -> p k n", k=KE)
        o += KE * CH
        yT = w_out[:, o:o + KD * CH].rearrange("p (k n) -> p k n", k=KD)
        tinit = aT[:].rearrange("p a b -> p (a b)")[:, 0:2 * CH].bitcast(U32).rearrange("p (n t) -> p n t", t=2)
        zrow = qT[:].rearrange("p a b -> p (a b)")
        fb = [w_in[:, b * D:(b + 1) * D] for b in range(FB)]
        fsq = [w_in[:, (FB + b) * D:(FB + b + 1) * D] for b in range(FB)]

        ps = [ctx.enter_context(nc.psum_tensor(f"ps{b}", [P, BANK], F32)) for b in range(BANKS)]

        psum_full = [sem(f"psum_full{b}") for b in range(BANKS)]
        psum_read = [sem(f"psum_read{b}") for b in range(BANKS)]
        w1_loaded = [sem(f"w1_loaded{i}") for i in range(4)]
        g1_loaded = sem("g1_loaded")
        const_w2 = sem("const_w2")
        wsTs_loaded = sem("wsTs_loaded")
        conv_loaded = sem("conv_loaded")
        const_dma = sem("const_dma")
        const_dve = sem("const_dve")
        const_pool = sem("const_pool")
        pool_link = sem("pool_link")
        act_link = sem("act_link")
        table_ready = sem("table_ready")
        xa_loaded = [sem(f"xa_loaded{t}") for t in range(GT)]
        xr_loaded = [sem(f"xr_loaded{t}") for t in range(GT)]
        sq_ready = sem("sq_ready")
        rs_ready = sem("rs_ready")
        rs_link = sem("rs_link")
        xn_ready = sem("xn_ready")
        halo_ready = sem("halo_ready")
        xc_ready = sem("xc_ready")
        var_ready = sem("var_ready")
        vrs_ready = sem("vrs_ready")
        vrs_link = sem("vrs_link")
        vn_ready = sem("vn_ready")
        at_ready = sem("at_ready")
        q_ready = sem("q_ready")
        gain_ready = sem("gain_ready")
        gin_ready = sem("gin_ready")
        gth_ready = sem("gth_ready")
        h_ready = sem("h_ready")
        cat_ready = sem("cat_ready")
        acc_stored = [sem(f"acc_stored{t}") for t in range(GT)]
        h2_ready = [sem(f"h2_ready{t}") for t in range(GT)]
        h2_stored = [sem(f"h2_stored{t}") for t in range(GT)]
        dv_ready = sem("dv_ready")
        dve_exp = sem("dve_exp")
        hot_ready = sem("hot_ready")
        slot_ready = sem("slot_ready")
        scattered = sem("scattered")
        pay_free = sem("pay_free")
        state_out = sem("state_out")
        dve_main = sem("dve_main")
        dve_choose = sem("dve_choose")
        dve_assign = sem("dve_assign")
        count_ready = sem("count_ready")
        dve_plan = sem("dve_plan")
        diag_ready = sem("diag_ready")
        plan_ready = sem("plan_ready")
        w_loaded = [sem(f"w_loaded{i}") for i in range(4)]
        ix_loaded = sem("ix_loaded")
        io_loaded = sem("io_loaded")
        xg_loaded = sem("xg_loaded")
        sg_ready = sem("sg_ready")
        y_added = sem("y_added")
        moe_done = sem("moe_done")
        moe_carry = sem("moe_carry")
        fg_loaded = sem("fg_loaded")
        f_loaded = [sem(f"f_loaded{b}") for b in range(FB)]
        f_sq = sem("f_sq")
        f_link = sem("f_link")
        f_rs = sem("f_rs")
        f_ready = sem("f_ready")
        f_stored = [sem(f"f_stored{b}") for b in range(FB)]

        def wait(eng, s, value):
            if not (isinstance(value, int) and value <= 0):
                eng.wait_ge(s, value)

        def wait_full(eng, seg, it, job):
            eng.wait_ge(psum_full[JOBS.bank(seg, job)], JOBS.before(seg, it, job) + 1)
            return ps[JOBS.bank(seg, job)]

        def wait_free(eng, seg, it, job):
            wait(eng, psum_read[JOBS.bank(seg, job)], JOBS.before(seg, it, job))
            return ps[JOBS.bank(seg, job)]

        def wait_out(eng, seg, it, job):
            eng.wait_ge(psum_read[JOBS.bank(seg, job)], JOBS.before(seg, it, job) + 1)

        def full(seg, job):
            return psum_full[JOBS.bank(seg, job)]

        def read(seg, job):
            return psum_read[JOBS.bank(seg, job)]

        pads = iter(range(N_PAD))

        def carry(eng):
            n = next(pads)
            return eng.tensor_tensor(pad[:, n:n + 1], mhalf[:, 0:1], mhalf[:, 0:1], ALU.mult)

        N_CONST = 12

        def size_ends(eng):
            return [0] + [eng.value_load(plan[0:1, 2 * P + k:2 * P + k + 1], min_val=k + 1, max_val=P - 1)
                          for k in range(len(SIZES))]

        def pair(bank, size):
            return bank[:, 0:2 * CH].rearrange("p (k n) -> p k n", n=CH)[:, :, 0:size]

        block = ctx.enter_context(nc.Block())

        @block.sync
        def _(sp):
            def load_x(g, t, dst, s):
                sp.dma_start(dst[:, t], a["x"].rearrange("(n p) d -> n p d", p=P)[bass.ds(g * GT + t, 1)]
                             .rearrange("a p d -> p (a d)")).then_inc(s[t], 16)

            for t in range(GT):
                load_x(0, t, xa, xa_loaded)
            sp.dma_start(g1b[:], a["norm1_g"].broadcast_to([P, D])).then_inc(g1_loaded, 16)
            early = [
                (cw[:], a["conv_w"]), (cb[:], a["conv_b"]), (lam[:], a["lam"]),
                (nb[:], a["gate_b"]), (h0s[:], a["h0"]),
                (xbs[:, :, :, 0:TAPS - 1], a["conv_state"]),
            ]
            for dst, src in early:
                sp.dma_start(dst, src).then_inc(conv_loaded, 16)
            win = a["w_in"].rearrange("(k p) n -> p k n", p=P)

            def load_w(lo):
                sp.dma_start(w_in_v[:, :, lo:lo + DA], win[:, :, lo:lo + DA]).then_inc(w1_loaded[lo // DA], 16)

            load_w(2 * DA)
            sp.wait_ge(const_dve, 2)
            for m in range(2):
                for half in range(2):
                    r = slice(64 * half, 64 * half + 64)
                    sp.dma_start(wgate[r, m, :, 64 * half:64 * half + 64],
                                 a["lru_w"][m].rearrange("(c h) i j -> h i c j", h=2)[half]).then_inc(const_dma, 16)
            load_w(DA)
            small = [
                (lngb[:], a["ln_g"].broadcast_to([P, DA])), (lnbb[:], a["ln_b"].broadcast_to([P, DA])),
                (bsb[:], a["b_s"].rearrange("a (g t) -> a g t", g=NC).broadcast_to([P, NC, P])),
                (wsT[:], a["w_sT"].rearrange("g s t -> s g t")),
                (g2b[:], a["norm2_g"].broadcast_to([P, D])),
                (rb[:], a["router_b"].broadcast_to([P, NG + NE])),
                (rw[:, :, 0:NG], a["router_gw"].rearrange("(k p) n -> p k n", p=P)),
                (rw[:, :, NG:NG + NE], a["router_ew"].rearrange("(k p) n -> p k n", p=P)),
            ]
            for dst, src in small:
                sp.dma_start(dst, src).then_inc(const_dma, 16)
            load_w(3 * DA)
            for s in range(STREAMS):
                r = slice(FRAMES * s, FRAMES * (s + 1))
                sp.dma_start(wsTs[r, :, FRAMES * s:FRAMES * (s + 1)],
                             a["w_sT"].rearrange("g s t -> s g t")[0:FRAMES, :, 0:FRAMES]).then_inc(wsTs_loaded, 16)
            load_w(0)
            for t in range(GT):
                load_x(0, t, xr, xr_loaded)
            wait_full(sp, "start", 0, "xT3")
            for t in range(GT):
                load_x(1, t, xa, xa_loaded)
            sp.wait_ge(const_pool, 5)
            tv = table[0:NE * SLOTS].rearrange("(q p n) c -> q p (n c)", p=NE * CPE // 4, n=CH)
            for q in range(4):
                sp.dma_start(tv[q], tinit[0:NE * CPE // 4].rearrange("p n t -> p (n t)")).then_inc(table_ready, 16)
            sp.dma_start(table[NE * SLOTS:].rearrange("(a n) c -> a (n c)", a=1),
                         tinit[0:1].rearrange("p n t -> p (n t)")).then_inc(table_ready, 16)
            sp.wait_ge(const_dve, 3)
            for dst in (acc, h2_rows):
                for h in range(2):
                    r = NTOK + HF * h
                    sp.dma_start(dst[r:r + HF], zrow[0:HF]).then_inc(table_ready, 16)

            sp.dma_start(w_out_v, a["w_out"].rearrange("(k p) n -> p k n", p=P)).then_inc(const_w2, 16)

            def rows(dst, g, t):
                n = g * GT + t
                return dst[0:NTOK].rearrange("(n p) d -> n p d", p=P)[bass.ds(n, 1)].rearrange("a p d -> p (a d)")

            def group(seg, it, g, nxt, tiles):
                for t in range(nxt):
                    if t == 0:
                        wait_full(sp, seg, it, "xT3")
                    load_x(g + 2, t, xa, xa_loaded)
                for t in range(tiles):
                    wait_out(sp, seg, it, f"o{t}1")
                    sp.dma_start(rows(acc, g, t), xr[:, t]).then_inc(acc_stored[t], 16)
                for t in range(tiles):
                    sp.wait_ge(h2_ready[t], g + 1)
                    sp.dma_start(rows(h2_rows, g, t), (xa if seg == "last" else xr)[:, t]).then_inc(h2_stored[t], 16)

            def next_xr(seg, it, g, tiles):
                for t in range(tiles):
                    sp.wait_ge(h2_stored[t], 16 * g)
                    wait_full(sp, seg, it, f"h2T{t}b")
                    load_x(g, t, xr, xr_loaded)

            group("first", 0, 0, GT, GT)
            with sp.Fori(1, NPG - 2) as g:
                next_xr("loop", g - 1, g, GT)
                group("loop", g - 1, g, GT, GT)
            next_xr("loop", NPG - 3, NPG - 2, GT)
            group("loop", NPG - 3, NPG - 2, 1, GT)
            next_xr("final", 0, NPG - 1, GT)
            group("final", 0, NPG - 1, 0, GT)
            sp.wait_ge(halo_ready, 1 + NPG)
            sp.dma_start(a["conv_p"], xbT[:, :, 0:TAPS - 1]).then_inc(state_out, 16)
            sp.wait_ge(h_ready, NPG)
            sp.dma_start(a["h_p"], hlast[:]).then_inc(state_out, 16)
            next_xr("last", 0, NPG, 1)
            sp.wait_ge(vn_ready, GT * NPG + 1)
            sp.dma_start(a["v_s"], vn[:, 0]).then_inc(state_out, 16)
            wait_out(sp, "last", 0, "xb1")
            for c in range(NC):
                sp.dma_start(a["conv_s"][:, c], xbs[:, c, :, FRAMES:FRAMES + TAPS - 1]).then_inc(state_out, 16)
            sp.wait_ge(h_ready, NPG + 1)
            sp.dma_start(a["h_s"], h0s[:]).then_inc(state_out, 16)
            wait_full(sp, "last", 0, "u1")

            def weights(e, piece):
                wgd = a["w_gate"].rearrange("e (k p) f -> e p k f", p=P)
                wud = a["w_up"].rearrange("e (k p) f -> e p k f", p=P)
                wdd = a["w_down"].rearrange("e (f p) d -> e p f d", p=P)

                def at(x, lo, hi):
                    return x[bass.ds(e, 1)].rearrange("a p k f -> p (a k) f")[:, :, lo:hi]

                if piece < 2:
                    lo, hi = DE // 2 * piece, DE // 2 * (piece + 1)
                    sp.dma_start(wg_e[:, :, lo:hi], at(wgd, lo, hi)).then_inc(w_loaded[piece], 16)
                    sp.dma_start(wu_e[:, :, lo:hi], at(wud, lo, hi)).then_inc(w_loaded[piece], 16)
                else:
                    lo, hi = ((0, D - 2 * P), (D - 2 * P, D))[piece - 2]
                    sp.dma_start(wd_e[:, :, lo:hi], at(wdd, lo, hi)).then_inc(w_loaded[piece], 16)

            for piece in range(4):
                weights(0, piece)
            group("last", 0, NPG, 0, 1)
            wait_out(sp, "plan", 0, "plan")
            chunks = sp.value_load(plan[0:1, 2 * P + len(SIZES) - 1:2 * P + len(SIZES)], min_val=len(SIZES), max_val=P - 1)
            with sp.Fori(1, chunks) as q:
                e = sp.value_load(plan[0:1, bass.ds(q, 1)], min_val=0, max_val=NE - 1)
                for piece, job in enumerate(("gu1", "gu3", "y2", "y3")):
                    wait_full(sp, "chunk", q - 1, job)
                    weights(e, piece)
            sp.wait_ge(xn_ready, GT * NPG + 1)
            sp.dma_start(g1b[:], a["final_g"].broadcast_to([P, D])).then_inc(fg_loaded, 16)
            sp.wait_ge(moe_done, 1)

            def load_f(it, b):
                wait(sp, f_stored[b], 16 * it)
                sp.dma_start(fb[b], acc[0:NTOK].rearrange("(n p) d -> n p d", p=P)[bass.ds(it * FB + b, 1)]
                             .rearrange("a p d -> p (a d)")).then_inc(f_loaded[b], 16)

            for b in range(FB):
                load_f(0, b)
            with sp.Fori(1, NTILE // FB) as it:
                for b in range(FB):
                    load_f(it, b)
            load_f(NTILE // FB, 0)
            sp.wait_ge(state_out, 16 * (NC + 4))
            for t in range(GT):
                n = NPG + (t == 0)
                sp.wait_ge(acc_stored[t], 16 * n)
                sp.wait_ge(h2_stored[t], 16 * n)
            for b in range(FB):
                sp.wait_ge(f_stored[b], 16 * (NTILE // FB + (b == 0)))

        @block.gpsimd
        def _(pool):
            def made(ins, s=const_pool):
                ins.then_inc(s, 1)

            pool.nop().then_inc(pay_free, 1)
            nc.gpsimd.memset(ident[:], 0.0).then_inc(pool_link, 1)
            nc.gpsimd.memset(before[:], 1.0).then_inc(pool_link, 1)
            nc.gpsimd.memset(mhalf[:], -0.5).then_inc(pool_link, 1)
            pool.wait_ge(pool_link, 3)
            made(nc.gpsimd.affine_select(out=ident[:], in_=ident[:], compare_op=ALU.not_equal, fill=1.0, base=0,
                                         pattern=[[-1, P]], channel_multiplier=1))
            made(nc.gpsimd.affine_select(out=before[:], in_=before[:], compare_op=ALU.is_gt, fill=0.0, base=0,
                                         pattern=[[1, P]], channel_multiplier=-1))
            nc.gpsimd.memset(tinit, 0).then_inc(pool_link, 1)
            pool.wait_ge(pool_link, 4)
            made(nc.gpsimd.iota(tinit[:, :, 0], [[1, CH]], base=NTOK, channel_multiplier=0))
            made(nc.gpsimd.iota(iota32[:], [[1, NW]], base=0, channel_multiplier=0,
                                allow_small_or_imprecise_dtypes=True))
            made(nc.gpsimd.iota(ebase[:], [[SLOTS, NW]], base=0, channel_multiplier=0,
                                allow_small_or_imprecise_dtypes=True))
            made(nc.gpsimd.iota(pcol[:], [[0, 1]], base=0, channel_multiplier=1,
                                allow_small_or_imprecise_dtypes=True))
            made(nc.gpsimd.iota(tokf[:], [[0, 1]], base=0, channel_multiplier=1,
                                allow_small_or_imprecise_dtypes=True))

            def root(col, n):
                pool.wait_ge(sq_ready, n + 1)
                carry(pool)
                nc.gpsimd.tensor_scalar(rstd[:, col:col + 1], ssq[:, col:col + 1], 1.0 / D, EPS, ALU.mult,
                                        ALU.add).then_inc(rs_link, 1)
                pool.wait_ge(rs_link, n + 1)
                nc.gpsimd.tensor_tensor(rstd[:, col:col + 1], rstd[:, col:col + 1], mhalf[:, 0:1],
                                        ALU.pow).then_inc(rs_ready, 1)

            for t in range(GT):
                root(t, squares(0, "in", t))
            pool.wait_ge(const_dma, 16 * N_CONST)
            pool.wait_ge(wsTs_loaded, 16 * STREAMS)
            made(nc.gpsimd.affine_select(out=wsT[:], in_=wsT[:], compare_op=ALU.is_ge, fill=0.0, base=0,
                                         pattern=[[0, NC], [1, P]], channel_multiplier=-1))
            made(nc.gpsimd.affine_select(out=wsTs[:], in_=wsTs[:], compare_op=ALU.is_ge, fill=0.0, base=0,
                                         pattern=[[0, NC], [1, P]], channel_multiplier=-1))

            def scatter(n, t):
                pool.wait_ge(slot_ready, n + 1)
                carry(pool)
                for k in range(2):
                    pool.indirect_dma_start(table, bass.IndirectOffsetOnAxis(ap=slot[:, t, k:k + 1], axis=0),
                                            pay[:, t, k, :], None).then_inc(scattered, 16)

            def group(g, tiles, prev, ahead):
                for t in range(tiles):
                    pool.wait_ge(var_ready, g * GT + t + 1)
                    carry(pool)
                    nc.gpsimd.tensor_scalar(vrs[:, t], vmv[:, t, :, 1], EPS, None, ALU.add).then_inc(vrs_link, 1)
                    pool.wait_ge(vrs_link, g * GT + t + 1)
                    nc.gpsimd.tensor_tensor(vrs[:, t], vrs[:, t], mhalf[:], ALU.pow).then_inc(vrs_ready, 1)
                for t in range(ahead):
                    root(t, squares(g + 1, "in", t))
                for t in range(prev):
                    scatter((g - 1) * GT + t, t)
                for t in range(tiles):
                    root(GT + t, squares(g, "x1", t))
                if prev:
                    pool.wait_ge(scattered, 16 * 2 * GT * g)
                    pool.nop().then_inc(pay_free, 1)

            group(0, GT, 0, GT)
            pool.wait_ge(table_ready, 16 * 9)
            with pool.Fori(1, NPG - 1) as g:
                group(g, GT, GT, GT)
            group(NPG - 1, GT, GT, 1)
            group(NPG, 1, GT, 0)
            scatter(GT * NPG, 0)

            pool.wait_ge(scattered, 16 * 2 * NTILE)

            def load_index_at(row, dst, s):
                pool.dma_start(dst[:], table[bass.ds(row, CH)].rearrange("(p h) c -> p h c", h=2)).then_inc(s, 16)

            def gather():
                for h in range(2):
                    pool.indirect_dma_start(xg[:, h, :], None, h2_rows,
                                            bass.IndirectOffsetOnAxis(ap=idx_in[:, h, 0:1], axis=0)).then_inc(xg_loaded, 16)

            load_index_at(0, idx_in, ix_loaded)
            for t in range(GT):
                pool.wait_ge(h2_stored[t], 16 * (NPG + (t == 0)))
                pool.wait_ge(acc_stored[t], 16 * (NPG + (t == 0)))
            wait_full(pool, "last", 0, "o01")
            pool.wait_ge(ix_loaded, 16)
            gather()
            wait_out(pool, "plan", 0, "plan")
            chunks = pool.value_load(plan[0:1, 2 * P + len(SIZES) - 1:2 * P + len(SIZES)], min_val=len(SIZES), max_val=P - 1)

            def load_index(q, dst, s):
                row = pool.value_load(plan[0:1, bass.ds(q + P, 1)], min_val=0, max_val=NE * SLOTS)
                load_index_at(row, dst, s)

            pool.wait_ge(xg_loaded, 32)
            load_index(1, idx_in, ix_loaded)
            pool.wait_ge(ix_loaded, 32)
            wait_full(pool, "pre", 0, "xT3")
            gather()
            pool.nop().then_inc(moe_carry, 1)
            with pool.Fori(0, chunks) as q:
                load_index(q, idx_out, io_loaded)
                pool.wait_ge(xg_loaded, 32 * q + 64)
                load_index(q + 2, idx_in, ix_loaded)
                pool.wait_ge(ix_loaded, 16 * q + 48)
                wait_full(pool, "chunk", q, "xT3")
                pool.wait_ge(moe_carry, 2 * q + 1)
                carry(pool).then_inc(moe_carry, 1)
                gather()
                wait_out(pool, "chunk", q, "r10")
                wait_out(pool, "chunk", q, "r11")
                pool.wait_ge(io_loaded, 16 * q + 16)
                pool.wait_ge(moe_carry, 2 * q + 2)
                carry(pool).then_inc(moe_carry, 1)
                for h in range(2):
                    pool.indirect_dma_start(acc, bass.IndirectOffsetOnAxis(ap=idx_out[:, h, 0:1], axis=0),
                                            ysb[:, h, :], None, compute_op=ALU.add).then_inc(y_added, 16)
                pool.wait_ge(y_added, 32 * q + 32)
            pool.wait_ge(xg_loaded, 32 * chunks + 64)
            pool.nop().then_inc(moe_done, 1)

            def final(it, b):
                k = it * FB + b
                pool.wait_ge(f_sq, k + 2)
                carry(pool)
                nc.gpsimd.tensor_scalar(rstd[:, b:b + 1], ssq[:, b:b + 1], 1.0 / D, EPS, ALU.mult,
                                        ALU.add).then_inc(f_link, 1)
                pool.wait_ge(f_link, k + 1)
                nc.gpsimd.tensor_tensor(rstd[:, b:b + 1], rstd[:, b:b + 1], mhalf[:, 0:1], ALU.pow).then_inc(f_rs, 1)

            with pool.Fori(0, NTILE // FB) as it:
                for b in range(FB):
                    final(it, b)
            final(NTILE // FB, 0)

        @block.tensor
        def _(pe):
            def inputs(seg, it, tiles, have):
                n = tiles * P
                pe.wait_ge(xn_ready, have)
                for j in range(4):
                    bank = wait_free(pe, seg, it, f"xT{j}")
                    for kk in range(2):
                        for t in range(tiles):
                            mm = pe.transpose(bank[:, kk * n + t * P:kk * n + (t + 1) * P],
                                              xa[:, t, (2 * j + kk) * P:(2 * j + kk + 1) * P], ident[:])
                    mm.then_inc(full(seg, f"xT{j}"), 1)

            def group(seg, it, g, tiles, prev, ahead):
                n = tiles * P

                def channels(kind, lo, p):
                    bank = wait_free(pe, seg, it, f"{kind}{p}")
                    for cc in range(2):
                        col = lo + (2 * p + cc) * P
                        for k in range(KD):
                            mm = pe.matmul(bank[:, cc * n:(cc + 1) * n], w_in_v[:, k, col:col + P], hT[:, k, 0:n],
                                           start=(k == 0), stop=(k == KD - 1))
                    mm.then_inc(full(seg, f"{kind}{p}"), 1)

                def first_use(s, count):
                    if seg == "first":
                        pe.wait_ge(s, count)

                first_use(w1_loaded[2], 16)
                channels("xb", 2 * DA, 0)
                if prev > 0:
                    turn(seg, it, 0, g - 1)
                channels("xb", 2 * DA, 1)
                if prev > 0:
                    logits(seg, it, 0)
                if prev > 1:
                    turn(seg, it, 1, g - 1)
                first_use(w1_loaded[1], 16)
                for t in range(tiles):
                    if t == 1 and prev > 1:
                        logits(seg, it, 1)
                    bank = wait_free(pe, seg, it, f"v{t}")
                    for k in range(KD):
                        mm = pe.matmul(bank[:, :], hT[:, k, t * P:(t + 1) * P], w_in_v[:, k, DA:2 * DA],
                                       start=(k == 0), stop=(k == KD - 1))
                    mm.then_inc(full(seg, f"v{t}"), 1)
                if prev > 1 and tiles == 1:
                    logits(seg, it, 1)
                first_use(const_dma, 16 * N_CONST)
                for c in range(NC):
                    bank = wait_free(pe, seg, it, f"ga{c}")
                    pe.wait_ge(xc_ready, NC * g + c + 1)
                    for m in range(2):
                        mm = pe.matmul(bank[:, m * n:(m + 1) * n], wgate[:, m, c, :], xcT[:, c, 0:n], start=True, stop=True)
                    mm.then_inc(full(seg, f"ga{c}"), 1)
                first_use(w1_loaded[3], 16)
                for p in range(2):
                    channels("gg", 3 * DA, p)
                if prev:
                    count_places(seg, it, prev, g - 1)
                first_use(const_pool, 9)
                for t in range(tiles):
                    bank = wait_free(pe, seg, it, f"s{t}")
                    pe.wait_ge(vn_ready, g * GT + t + 1)
                    ws = wsTs if seg == "last" else wsT
                    for c in range(NC):
                        mm = pe.matmul(bank[:, c * P:(c + 1) * P], vn[:, t, c * P:(c + 1) * P], ws[:, c, :],
                                       start=True, stop=True)
                    mm.then_inc(full(seg, f"s{t}"), 1)
                first_use(w1_loaded[0], 16)
                for p in range(2):
                    channels("u", 0, p)
                if ahead:
                    inputs(seg, it, ahead, (g + 1) * GT + ahead)
                first_use(const_w2, 16)
                wait_out(pe, seg, it, "u1")
                pe.wait_ge(cat_ready, g + 1)
                for t in range(tiles):
                    for h in range(2):
                        bank = wait_free(pe, seg, it, f"o{t}{h}")
                        for k in range(KD):
                            mm = pe.matmul(bank[:, :], catT[:, k, t * P:(t + 1) * P],
                                           w_out_v[:, k, h * BANK:(h + 1) * BANK], start=(k == 0), stop=(k == KD - 1))
                        mm.then_inc(full(seg, f"o{t}{h}"), 1)
                if ahead:
                    wait_out(pe, seg, it, "xT3")

            def turn(seg, it, t, gp):
                rows = xa if seg == "tail" else xr
                pe.wait_ge(h2_ready[t], gp + 1)
                for i, half in enumerate("ab"):
                    bank = wait_free(pe, seg, it, f"h2T{t}{half}")
                    for k in range(4):
                        kk = 4 * i + k
                        mm = pe.transpose(bank[:, k * P:(k + 1) * P], rows[:, t, kk * P:(kk + 1) * P], ident[:])
                    mm.then_inc(full(seg, f"h2T{t}{half}"), 1)

            def logits(seg, it, t):
                bank = wait_free(pe, seg, it, f"lg{t}")
                wait_out(pe, seg, it, f"h2T{t}b")
                for k in range(KD):
                    mm = pe.matmul(bank[:, 0:NG + NE], h2T[:, k, :], rw[:, k, :], start=(k == 0), stop=(k == KD - 1))
                mm.then_inc(full(seg, f"lg{t}"), 1)

            def count_places(seg, it, tiles, gp):
                bank = wait_free(pe, seg, it, "pf")
                for t in range(tiles):
                    pe.wait_ge(hot_ready, gp * GT + t + 1)
                    pe.matmul(bank[:, 64 * t:64 * t + NE], before[:], hot[:, t, 2, :], start=True, stop=True)
                    mm = pe.matmul(bank[:, 64 * t + NE:64 * t + 2 * NE], ones[:, 0:P], hot[:, t, 2, :], start=True, stop=True)
                mm.then_inc(full(seg, "pf"), 1)

            pe.wait_ge(const_pool, 1)
            inputs("start", 0, GT, GT)
            wait_out(pe, "start", 0, "xT3")
            group("first", 0, 0, GT, 0, GT)
            pe.wait_ge(const_dve, 4)
            with pe.Fori(1, NPG - 1) as g:
                group("loop", g - 1, g, GT, GT, GT)
            group("final", 0, NPG - 1, GT, GT, 1)
            group("last", 0, NPG, 1, GT, 0)
            turn("tail", 0, 0, NPG)
            logits("tail", 0, 0)
            count_places("tail", 0, 1, NPG)
            bank = wait_free(pe, "plan", 0, "plan")
            pe.wait_ge(diag_ready, 1)
            for i in range(2):
                mm = pe.matmul(bank[:, i * P:(i + 1) * P], ones[:, 0:P], diag[:, i, :], start=True, stop=True)
            mm.then_inc(full("plan", "plan"), 1)

            def columns(seg, q, n, size):
                pe.wait_ge(xg_loaded, 32 * n + 32)
                for j in PAIRS:
                    bank = wait_free(pe, seg, q, f"xT{j}")
                    for k in range(2):
                        for h in range(2):
                            at, n = k * CH + h * HF, max(size // 2, TMIN)
                            mm = pe.transpose(bank[:, at:at + n], xg[0:n, h, (2 * j + k) * P:(2 * j + k + 1) * P],
                                              ident[0:n, 0:n])
                    mm.then_inc(full(seg, f"xT{j}"), 1)

            columns("pre", 0, 0, CH)
            wait_out(pe, "plan", 0, "plan")
            ends = size_ends(pe)
            wait_out(pe, "pre", 0, "xT3")

            def chunk(q, size):
                for f in range(KE):
                    bank = wait_free(pe, "chunk", q, f"gu{f}")
                    if f % 2 == 0:
                        pe.wait_ge(w_loaded[f // 2], 32 * q + 32)
                    for m, w in enumerate((wg_e, wu_e)):
                        for k in range(KD):
                            mm = pe.matmul(bank[:, m * CH:m * CH + size], w[:, k, f * P:(f + 1) * P],
                                           xTm[:, k, :, 0:size // 2],
                                           start=(k == 0), stop=(k == KD - 1))
                    mm.then_inc(full("chunk", f"gu{f}"), 1)
                columns("chunk", q, q + 1, size)
                wait_out(pe, "chunk", q, f"gu{KE - 1}")
                for j in PAIRS:
                    bank = wait_free(pe, "chunk", q, f"y{j}")
                    if j == 0 or j == 3:
                        pe.wait_ge(w_loaded[2 + j // 3], 16 * q + 16)
                    for k in range(2):
                        d = (2 * j + k) * P
                        for f in range(KE):
                            mm = pe.matmul(bank[:, k * CH:k * CH + size], wd_e[:, f, d:d + P], hTm[:, f, 0:size],
                                           start=(f == 0), stop=(f == KE - 1))
                    mm.then_inc(full("chunk", f"y{j}"), 1)
                for i in range(2):
                    wait_out(pe, "chunk", q, f"y{1 + 2 * i}")
                    for h in range(2):
                        bank = wait_free(pe, "chunk", q, f"r{i}{h}")
                        for d in range(4):
                            at, n = h * (size // 2), max(size // 2, TMIN)
                            mm = pe.transpose(bank[0:n, d * P:(d + 1) * P], yT[:, 4 * i + d, at:at + n], ident[:])
                        mm.then_inc(full("chunk", f"r{i}{h}"), 1)
                wait_out(pe, "chunk", q, "xT3")

            for k, size in enumerate(SIZES):
                with pe.Fori(ends[k], ends[k + 1]) as q:
                    chunk(q, size)

        @block.scalar
        def _(act):
            def h2_columns(seg, it, t, gp, sq_n):
                act.wait_ge(sq_ready, sq_n)
                for i, half in enumerate("ab"):
                    bank = wait_full(act, seg, it, f"h2T{t}{half}")
                    nc.scalar.copy(h2T[:, 4 * i:4 * i + 4, :], bank[:, :].rearrange("p (k n) -> p k n", k=4))\
                        .then_inc(read(seg, f"h2T{t}{half}"), 1)

            def router_exp(t, gp):
                act.wait_ge(dv_ready, gp * GT + t + 1)
                nc.scalar.activation(dv[:, t, 0:NG + 1], dv[:, t, 0:NG + 1], ACT.Exp).then_inc(dve_exp, 1)

            def square(src, col, n):
                wait(act, sq_ready, n)
                nc.scalar.activation(h2T[:].rearrange("p a b -> p (a b)"), src, ACT.Square,
                                     accum_out=ssq[:, col:col + 1]).then_inc(sq_ready, 1)

            def input_columns(seg, it, tiles):
                n = tiles * P
                for j in range(4):
                    bank = wait_full(act, seg, it, f"xT{j}")
                    nc.scalar.copy(hT[:, 2 * j:2 * j + 2, 0:n], bank[:, 0:2 * n].rearrange("p (k n) -> p k n", k=2))\
                        .then_inc(read(seg, f"xT{j}"), 1)

            def group(seg, it, g, tiles, prev, ahead):
                n = tiles * P
                act.wait_ge(halo_ready, g + 1)
                for p in range(2):
                    if 0 < p <= prev:
                        h2_columns(seg, it, p - 1, g - 1, squares(g - 1, "x1", prev - 1) + 1)
                    bank = wait_full(act, seg, it, f"xb{p}")
                    if seg == "last":
                        for cc in range(2):
                            ins = nc.scalar.copy(xbs[:, 2 * p + cc, :, TAPS - 1:],
                                                 bank[:, cc * n:(cc + 1) * n].rearrange("p (s f) -> p s f", f=FRAMES))
                    else:
                        ins = nc.scalar.copy(xbT[:, 2 * p:2 * p + 2, TAPS - 1:],
                                             bank[:, 0:2 * n].rearrange("p (c n) -> p c n", c=2))
                    ins.then_inc(read(seg, f"xb{p}"), 1)
                if prev > 1:
                    h2_columns(seg, it, 1, g - 1, squares(g - 1, "x1", prev - 1) + 1)
                for c in range(NC):
                    bank = wait_full(act, seg, it, f"ga{c}")
                    for m in range(2):
                        ins = nc.scalar.activation(ri[:, m, c, 0:n], bank[:, m * n:(m + 1) * n], ACT.Sigmoid,
                                                   bias=nb[:, m, c:c + 1])
                    ins.then_inc(read(seg, f"ga{c}"), 1)
                for t in range(prev):
                    router_exp(t, g - 1)
                for t in range(ahead):
                    act.wait_ge(xa_loaded[t], 16 * g + 32)
                    square(xa[:, t], t, squares(g + 1, "in", t))
                if seg == "first":
                    act.wait_ge(table_ready, 16 * 9)
                    act.wait_ge(const_dve, 9)
                wait_out(act, seg, it, f"ga{NC - 1}")
                for c in range(NC):
                    nc.scalar.activation(aT[:, c, 0:n], ri[:, 0, c, 0:n], ACT.Exp, scale=nsp[:, c:c + 1])
                    nc.scalar.activation(ri[:, 0, c, 0:n], ri[:, 0, c, 0:n], ACT.Tanh, scale=nsp[:, c:c + 1])\
                        .then_inc(at_ready, 1)
                for p in range(2):
                    bank = wait_full(act, seg, it, f"gg{p}")
                    v = bank[:, 0:2 * n].rearrange("p (c n) -> p c n", c=2)
                    nc.scalar.copy(gS[:, 2 * p:2 * p + 2, 0:n], v)
                    nc.scalar.activation(gt[:, 2 * p:2 * p + 2, 0:n], v, ACT.Square)\
                        .then_inc(read(seg, f"gg{p}"), 1)
                act.wait_ge(gin_ready, g + 1)
                nc.scalar.activation(gt[:, :, 0:n], gt[:, :, 0:n], ACT.Tanh, scale=GELU_C).then_inc(gth_ready, 1)
                act.wait_ge(q_ready, g + 1)
                nc.scalar.activation(qT[:, :, 0:n], qT[:, :, 0:n], ACT.Sqrt, scale=-1.0).then_inc(gain_ready, 1)
                if ahead:
                    input_columns(seg, it, ahead)
                for t in range(tiles):
                    wait_out(act, seg, it, f"o{t}1")
                    square(xr[:, t], GT + t, squares(g, "x1", t))

            for t in range(GT):
                act.wait_ge(xa_loaded[t], 16)
                square(xa[:, t], t, squares(0, "in", t))
            input_columns("start", 0, GT)
            act.wait_ge(conv_loaded, 16 * 6)
            nc.scalar.activation(lamt[:, 0], lam[:], ACT.Relu, scale=-1.0).then_inc(act_link, 1)
            nc.scalar.activation(lamt[:, 1], lam[:], ACT.Abs).then_inc(act_link, 1)
            act.wait_ge(act_link, 2)
            nc.scalar.activation(lamt[:, 1], lamt[:, 1], ACT.Exp, scale=-1.0).then_inc(act_link, 1)
            act.wait_ge(act_link, 3)
            act.wait_ge(const_dve, 4)
            nc.scalar.activation(lamt[:, 2], lamt[:, 1], ACT.Ln, bias=ones[:, 0:1]).then_inc(act_link, 1)
            group("first", 0, 0, GT, 0, GT)
            with act.Fori(1, NPG - 1) as g:
                group("loop", g - 1, g, GT, GT, GT)
            group("final", 0, NPG - 1, GT, GT, 1)
            group("last", 0, NPG, 1, GT, 0)
            h2_columns("tail", 0, 0, NPG, squares(NPG, "x1", 0) + 1)
            router_exp(0, NPG)


            def x_columns(seg, q, size):
                for j in PAIRS:
                    bank = wait_full(act, seg, q, f"xT{j}")
                    both = bank[:, 0:2 * CH].rearrange("p (x n) -> p x n", n=HF)[:, :, 0:size // 2]
                    nc.scalar.copy(xTm[:, 2 * j:2 * j + 2].rearrange("p k h n -> p (k h) n")[:, :, 0:size // 2], both)\
                        .then_inc(read(seg, f"xT{j}"), 1)

            def chunk(q, size):
                for f in range(KE):
                    bank = wait_full(act, "chunk", q, f"gu{f}")
                    nc.scalar.activation(sg[:, f, 0:size], bank[:, 0:size], ACT.Silu).then_inc(sg_ready, 1)
                x_columns("chunk", q, size)
                act.wait_ge(io_loaded, 16 * q + 16)
                for i in range(2):
                    bank = wait_full(act, "chunk", q, f"r{i}0")
                    nc.scalar.activation(ysb[0:size // 2, 0, i * BANK:(i + 1) * BANK], bank[0:size // 2, :], ACT.Copy,
                                         scale=idx_out[0:size // 2, 0, 1:2].bitcast(F32)).then_inc(read("chunk", f"r{i}0"), 1)

            x_columns("pre", 0, CH)
            wait_out(act, "plan", 0, "plan")
            ends = size_ends(act)
            for k, size in enumerate(SIZES):
                with act.Fori(ends[k], ends[k + 1]) as q:
                    chunk(q, size)

            def final(it, b):
                act.wait_ge(f_loaded[b], 16 * it + 16)
                act.wait_ge(f_sq, it * FB + 1)
                nc.scalar.activation(fsq[b], fb[b], ACT.Square,
                                     accum_out=ssq[:, b:b + 1]).then_inc(f_sq, 1)

            def store(it, b):
                act.wait_ge(f_ready, it * FB + b + 1)
                act.dma_start(a["y"].rearrange("(n p) d -> n p d", p=P)[bass.ds(it * FB + b, 1)]
                              .rearrange("a p d -> p (a d)"), fb[b]).then_inc(f_stored[b], 16)

            act.nop().then_inc(f_sq, 1)
            with act.Fori(0, NTILE // FB) as it:
                for b in range(FB):
                    final(it, b)
                    if b >= 2:
                        store(it, b - 2)
                for b in range(FB - 2, FB):
                    store(it, b)
            final(NTILE // FB, 0)
            store(NTILE // FB, 0)

        @block.vector
        def _(dve):
            V = nc.vector

            def linked(s):
                state = [0, 0]

                def start(base):
                    state[0], state[1] = base, 0

                def link(ins):
                    state[1] += 1
                    ins.then_inc(s, 1)
                    dve.wait_ge(s, state[0] + state[1])

                return start, link, state

            start_m, link, main = linked(dve_main)
            start_c, clink, choose_n = linked(dve_choose)
            start_a, alink, assign_n = linked(dve_assign)
            start_p, plink, plan_n = linked(dve_plan)

            def input_rows(g, tiles):
                for t in range(tiles):
                    dve.wait_ge(rs_ready, squares(g, "in", t) + 1)
                    V.scalar_tensor_tensor(out=xa[:, t], in0=xa[:, t], scalar=rstd[:, t:t + 1], in1=g1b[:],
                                           op0=ALU.mult, op1=ALU.mult).then_inc(xn_ready, 1)

            V.memset(wgate[:], 0.0).then_inc(const_dve, 1)
            V.memset(wsTs[:], 0.0).then_inc(const_dve, 1)
            V.memset(zrow[:], 0.0).then_inc(const_dve, 1)
            V.memset(ones[:], 1.0).then_inc(const_dve, 1)
            V.memset(gl[:], -3.0e38).then_inc(const_dve, 1)
            V.memset(count[:], 0.0).then_inc(const_dve, 1)
            V.memset(hlast[:], 0.0).then_inc(const_dve, 1)
            V.memset(xbT[:, :, 0:TAPS - 1], 0.0).then_inc(halo_ready, 1)
            dve.wait_ge(const_dve, 7)
            dve.wait_ge(g1_loaded, 16)
            input_rows(0, GT)
            dve.wait_ge(conv_loaded, 16 * 6)
            dve.wait_ge(act_link, 4)
            V.tensor_tensor(lamt[:, 0], lamt[:, 0], lamt[:, 2], ALU.add).then_inc(const_dve, 1)
            dve.wait_ge(const_dve, 8)
            V.tensor_scalar(nsp[:], lamt[:, 0], -8.0, None, ALU.mult).then_inc(const_dve, 1)
            MAIN, CHOOSE, ASSIGN = 22, 13, 9

            def group(seg, it, g, tiles, prev, ahead):
                n = tiles * P
                start_m(g * MAIN)
                for c in range(NC):
                    if c % 2 == 0:
                        wait_out(dve, seg, it, f"xb{c // 2}")
                    if seg == "last":
                        src = [xbs[:, c, :, k:k + FRAMES] for k in range(TAPS)]
                        dst = xcT[:, c, 0:n].rearrange("p (s f) -> p s f", f=FRAMES)
                    else:
                        src = [xbT[:, c, k:k + n] for k in range(TAPS)]
                        dst = xcT[:, c, :]
                    link(V.tensor_scalar(dst, src[0], cw[:, c, 0:1], cb[:, c:c + 1], ALU.mult, ALU.add))
                    for k in range(1, TAPS):
                        ins = V.scalar_tensor_tensor(out=dst, in0=src[k], scalar=cw[:, c, k:k + 1], in1=dst,
                                                     op0=ALU.mult, op1=ALU.add)
                        if k < TAPS - 1:
                            link(ins)
                    ins.then_inc(xc_ready, 1)
                if seg != "last":
                    V.tensor_copy(xbT[:, :, 0:TAPS - 1], xbT[:, :, G:G + TAPS - 1]).then_inc(halo_ready, 1)
                if prev > 0:
                    choose(seg, it, 0, g - 1)
                if seg == "first":
                    dve.wait_ge(const_dma, 16 * N_CONST)
                for t in range(tiles):
                    bank = wait_full(dve, seg, it, f"v{t}")
                    for c in range(NC):
                        ins = V.bn_stats(vst[:, t, c, :], bank[:, c * P:(c + 1) * P])
                    link(ins)
                    carry(dve)
                    for c in range(NC):
                        ins = V.bn_aggr(vmv[:, t, c, :], vst[:, t, c, :])
                    ins.then_inc(var_ready, 1)
                    dve.wait_ge(vrs_ready, g * GT + t + 1)
                    for c in range(NC):
                        ins = V.tensor_scalar(vn[:, t, c * P:(c + 1) * P], bank[:, c * P:(c + 1) * P],
                                              vmv[:, t, c, 0:1], vrs[:, t, c:c + 1], ALU.subtract, ALU.mult)
                    ins.then_inc(read(seg, f"v{t}"), 1)
                    if t == 0 and prev > 1:
                        choose(seg, it, 1, g - 1)
                    wait_out(dve, seg, it, f"v{t}")
                    link(V.tensor_tensor(vn[:, t], vn[:, t], lngb[:], ALU.mult))
                    V.tensor_tensor(vn[:, t], vn[:, t], lnbb[:], ALU.add).then_inc(vn_ready, 1)
                wait_out(dve, seg, it, f"ga{NC - 1}")
                if seg == "first":
                    dve.wait_ge(table_ready, 16 * 9)
                iv, rv, av, qv = ri[:, 1, :, 0:n], ri[:, 0, :, 0:n], aT[:, :, 0:n], qT[:, :, 0:n]
                link(V.tensor_tensor(iv, iv, xcT[:, :, 0:n], ALU.mult))
                dve.wait_ge(at_ready, NC * g + NC)
                link(V.tensor_tensor(qv, av, av, ALU.mult))
                V.scalar_tensor_tensor(out=qv, in0=qv, scalar=1.0, in1=rv, op0=ALU.add, op1=ALU.mult).then_inc(q_ready, 1)
                wait_out(dve, seg, it, "gg1")
                gv, tv = gS[:, :, 0:n], gt[:, :, 0:n]
                link(V.tensor_scalar(tv, tv, 0.044715, 1.0, ALU.mult, ALU.add))
                V.tensor_tensor(tv, tv, gv, ALU.mult).then_inc(gin_ready, 1)
                if prev:
                    take_places(seg, it, prev)
                for t in range(tiles):
                    bank = wait_full(dve, seg, it, f"s{t}")
                    if seg == "last":
                        for c in range(NC):
                            ins = V.tensor_tensor(
                                sS[:, c, 0:n].rearrange("p (s f) -> p s f", f=FRAMES),
                                bank[:, c * P:(c + 1) * P].rearrange("p (s f) -> p s f", f=FRAMES),
                                bsb[:, c:c + 1, 0:FRAMES].broadcast_to([P, STREAMS, FRAMES]), ALU.add)
                    else:
                        ins = V.tensor_tensor(sS[:, :, t * P:(t + 1) * P], bank[:, :].rearrange("p (c n) -> p c n", c=NC),
                                              bsb[:], ALU.add)
                    ins.then_inc(read(seg, f"s{t}"), 1)
                    wait_out(dve, seg, it, f"s{t}")
                dve.wait_ge(gain_ready, g + 1)
                link(V.tensor_tensor(iv, iv, qv, ALU.mult))
                for c in range(NC):
                    if seg == "last":
                        for s in range(STREAMS):
                            r = slice(FRAMES * s, FRAMES * (s + 1))
                            ins = V.tensor_tensor_scan(qT[:, c, r], aT[:, c, r], ri[:, 1, c, r], h0s[:, c, s:s + 1],
                                                       ALU.mult, ALU.add)
                    else:
                        ins = V.tensor_tensor_scan(qT[:, c, :], aT[:, c, :], ri[:, 1, c, :], hlast[:, c:c + 1],
                                                   ALU.mult, ALU.add)
                link(ins)
                if seg != "last":
                    V.tensor_copy(hlast[:], qT[:, :, G - 1]).then_inc(h_ready, 1)
                else:
                    V.tensor_copy(h0s[:], qT[:, :, FRAMES - 1:P:FRAMES]).then_inc(h_ready, 1)
                dve.wait_ge(gth_ready, g + 1)
                link(V.scalar_tensor_tensor(out=tv, in0=tv, scalar=1.0, in1=gv, op0=ALU.add, op1=ALU.mult))
                V.scalar_tensor_tensor(out=catT[:, NC:, 0:n], in0=tv, scalar=0.5, in1=qv, op0=ALU.mult,
                                       op1=ALU.mult).then_inc(cat_ready, 1)
                input_rows(g + 1, ahead)
                for p in range(2):
                    bank = wait_full(dve, seg, it, f"u{p}")
                    V.tensor_tensor(catT[:, 2 * p:2 * p + 2, 0:n], bank[:, 0:2 * n].rearrange("p (c n) -> p c n", c=2),
                                    sS[:, 2 * p:2 * p + 2, 0:n], ALU.mult).then_inc(read(seg, f"u{p}"), 1)
                if prev:
                    assign(seg, it, prev, g - 1)
                for t in range(tiles):
                    dve.wait_ge(xr_loaded[t], 16 * g + 16)
                    for h in range(2):
                        bank = wait_full(dve, seg, it, f"o{t}{h}")
                        x = xr[:, t, h * BANK:(h + 1) * BANK]
                        V.tensor_tensor(x, bank[:, :], x, ALU.add).then_inc(read(seg, f"o{t}{h}"), 1)
                for t in range(tiles):
                    dve.wait_ge(rs_ready, squares(g, "x1", t) + 1)
                    if seg != "last":
                        dve.wait_ge(acc_stored[t], 16 * g + 16)
                    V.scalar_tensor_tensor(out=(xa if seg == "last" else xr)[:, t], in0=xr[:, t], scalar=rstd[:, GT + t:GT + t + 1], in1=g2b[:],
                                           op0=ALU.mult, op1=ALU.mult).then_inc(h2_ready[t], 1)
                if seg == "first":
                    assert main[1] == MAIN, main[1]

            def choose(seg, it, t, gp):
                start_c((gp * GT + t) * CHOOSE)
                bank = wait_full(dve, seg, it, f"lg{t}")
                V.tensor_tensor(gl[:, t, 0:NG], bank[:, 0:NG], rb[:, 0:NG], ALU.add)
                V.tensor_tensor(el[:, t], bank[:, NG:NG + NE], rb[:, NG:], ALU.add).then_inc(read(seg, f"lg{t}"), 1)
                wait_out(dve, seg, it, f"lg{t}")
                carry(dve)
                clink(V.max(m8[:, t, 0], gl[:, t]))
                carry(dve)
                clink(V.max_index(i8[:, t, 0], m8[:, t, 0], gl[:, t]))
                clink(V.tensor_copy(rf[:, t, 0:1], i8[:, t, 0, 0:1]))
                clink(V.tensor_scalar(mk[:, t], iota32[:, 0:NG], rf[:, t, 0:1], None, ALU.is_equal))
                clink(V.tensor_scalar(ein[:, t], el[:, t, 0:EPG], mk[:, t, 0:1], None, ALU.mult))
                for j in range(1, NG):
                    clink(V.scalar_tensor_tensor(out=ein[:, t], in0=el[:, t, j * EPG:(j + 1) * EPG],
                                                 scalar=mk[:, t, j:j + 1], in1=ein[:, t], op0=ALU.mult, op1=ALU.add))
                carry(dve)
                clink(V.max(m8[:, t, 1], ein[:, t]))
                carry(dve)
                clink(V.max_index(i8[:, t, 1], m8[:, t, 1], ein[:, t]))
                V.tensor_scalar(rf[:, t, 3:4], rf[:, t, 0:1], float(EPG), None, ALU.mult)
                clink(V.tensor_copy(rf[:, t, 1:3], i8[:, t, 1, 0:2]))
                clink(V.tensor_scalar(rf[:, t, 1:3], rf[:, t, 1:3], rf[:, t, 3:4], None, ALU.add))
                V.tensor_scalar(hot[:, t, 0], iota32[:, 0:NE], rf[:, t, 1:2], None, ALU.is_equal)
                clink(V.tensor_scalar(hot[:, t, 1], iota32[:, 0:NE], rf[:, t, 2:3], None, ALU.is_equal))
                V.tensor_tensor(hot[:, t, 2], hot[:, t, 0], hot[:, t, 1], ALU.add).then_inc(hot_ready, 1)
                V.tensor_scalar(dv[:, t, 0:NG], gl[:, t, 0:NG], m8[:, t, 0, 0:1], None, ALU.subtract)
                V.tensor_tensor(dv[:, t, NG:NG + 1], m8[:, t, 1, 1:2], m8[:, t, 1, 0:1], ALU.subtract).then_inc(dv_ready, 1)
                assert choose_n[1] == CHOOSE, choose_n[1]

            def take_places(seg, it, tiles):
                bank = wait_full(dve, seg, it, "pf")
                V.tensor_copy(places[:, 0:64 * tiles], bank[:, 0:64 * tiles]).then_inc(read(seg, "pf"), 1)

            def assign(seg, it, tiles, gp):
                bank = places
                wait_out(dve, seg, it, "pf")
                for t in range(tiles):
                    start_a((gp * GT + t) * ASSIGN)
                    dve.wait_ge(pay_free, gp + 1)
                    dve.wait_ge(dve_exp, gp * GT + t + 1)
                    alink(V.reduce_sum(rf[:, t, 4:5], dv[:, t, 0:NG], AX.X))
                    alink(V.scalar_tensor_tensor(out=rf[:, t, 5:6], in0=dv[:, t, NG:NG + 1], scalar=1.0,
                                                 in1=rf[:, t, 4:5], op0=ALU.add, op1=ALU.mult))
                    alink(V.reciprocal(rf[:, t, 6:7], rf[:, t, 5:6]))
                    V.tensor_copy(pay[:, t, 0, 1:2].bitcast(F32), rf[:, t, 6:7])
                    alink(V.tensor_tensor(pay[:, t, 1, 1:2].bitcast(F32), rf[:, t, 6:7], dv[:, t, NG:NG + 1], ALU.mult))
                    V.tensor_copy(pay[:, t, 0, 0:1], tokf[:])
                    V.tensor_copy(pay[:, t, 1, 0:1], tokf[:])
                    alink(V.tensor_scalar(tokf[:], tokf[:], float(P), None, ALU.add))
                    alink(V.tensor_tensor(rk[:], bank[:, 64 * t:64 * t + NE], count[:, 0:NE], ALU.add))
                    alink(V.tensor_tensor(rk[:], rk[:], ebase[:, 0:NE], ALU.add))
                    for k in range(2):
                        alink(V.tensor_tensor_reduce(rkj[:, 0:NE], hot[:, t, k], rk[:], 1.0, 0.0, ALU.mult, ALU.add,
                                                     slotf[:, t, k:k + 1]))
                    V.tensor_copy(slot[:, t], slotf[:, t]).then_inc(slot_ready, 1)
                    ins = V.tensor_tensor(count[:, 0:NE], count[:, 0:NE], bank[:, 64 * t + NE:64 * t + 2 * NE], ALU.add)
                    ins.then_inc(count_ready, 1)
                    dve.wait_ge(count_ready, gp * GT + t + 1)
                    assert assign_n[1] == ASSIGN, assign_n[1]

            group("first", 0, 0, GT, 0, GT)
            dve.wait_ge(const_pool, 9)
            with dve.Fori(1, NPG - 1) as g:
                group("loop", g - 1, g, GT, GT, GT)
            group("final", 0, NPG - 1, GT, GT, 1)
            group("last", 0, NPG, 1, GT, 0)
            choose("tail", 0, 0, NPG)
            take_places("tail", 0, 1)
            assign("tail", 0, 1, NPG)

            start_p(0)
            last = len(SIZES) - 1
            plink(V.tensor_scalar(whole[:], count[:], -(CH - 1) / 2, 1.0 / CH, ALU.add, ALU.mult))
            plink(V.tensor_scalar(whole[:], whole[:], 1.5 * 2 ** 23, None, ALU.add))
            plink(V.tensor_scalar(whole[:], whole[:], -1.5 * 2 ** 23, None, ALU.add))
            plink(V.scalar_tensor_tensor(out=rest[:], in0=whole[:], scalar=-float(CH), in1=count[:],
                                         op0=ALU.mult, op1=ALU.add))
            for k, size in enumerate(SIZES[1:] + (0,)):
                ins = V.tensor_scalar(over[:, k], rest[:], float(size), None, ALU.is_gt)
            plink(ins)
            V.tensor_tensor(nch[:, 0], over[:, 0], whole[:], ALU.add)
            plink(V.tensor_tensor(nch[:, 1:], over[:, 1:], over[:, 0:len(SIZES) - 1], ALU.subtract))
            V.memset(nch[:, 1:, 0:1], 0.0)
            plink(V.tensor_tensor(nch[:, 0, 0:1], over[:, last, 0:1], whole[:, 0:1], ALU.add))
            plink(V.tensor_scalar(nch[:, 0, 0:1], nch[:, 0, 0:1], 1.0, None, ALU.max))
            plink(V.reduce_sum(pq[:, 4:4 + last], nch[:, 1:, 0:NE], AX.X))
            plink(V.tensor_scalar(nch[:, 1:, NE], pq[:, 4:4 + last], 0.0, None, ALU.is_equal))
            flat = lambda x: x.rearrange("p k e -> p (k e)")
            plink(V.tensor_tensor_scan(flat(cend[:]), ones[:, 0:len(SIZES) * NW], flat(nch[:]), 0.0, ALU.mult, ALU.add))
            V.tensor_copy(cslot[:, 0], ebase[:])
            for k in range(1, len(SIZES)):
                V.scalar_tensor_tensor(out=cslot[:, k], in0=whole[:], scalar=float(CH), in1=ebase[:],
                                       op0=ALU.mult, op1=ALU.add)
            plink(V.tensor_tensor(flat(cstart), flat(cend[:]), flat(nch[:]), ALU.subtract))
            plink(V.scalar_tensor_tensor(out=flat(cslot), in0=flat(cstart), scalar=-float(CH), in1=flat(cslot),
                                         op0=ALU.mult, op1=ALU.add))
            V.tensor_scalar(flat(mine[:, 0]), flat(cstart), pcol[:, 0:1], None, ALU.is_le)
            V.tensor_scalar(pq[:, 2:3], pcol[:], float(CH), None, ALU.mult)
            plink(V.tensor_scalar(flat(mine[:, 1]), flat(cend[:]), pcol[:, 0:1], None, ALU.is_le))
            V.tensor_scalar(flat(cslot), flat(cslot), pq[:, 2:3], None, ALU.add)
            plink(V.tensor_tensor(flat(mine[:, 0]), flat(mine[:, 0]), flat(mine[:, 1]), ALU.subtract))
            plink(V.tensor_tensor_reduce(flat(mine[:, 1]), flat(mine[:, 0]), flat(cslot), 1.0, 0.0, ALU.mult, ALU.add,
                                         pq[:, 1:2]))
            for k in range(len(SIZES)):
                ins = V.tensor_tensor(mine[:, 1, k], mine[:, 0, k], iota32[:], ALU.mult)
            plink(ins)
            plink(V.reduce_sum(pq[:, 0:1], flat(mine[:, 1]), AX.X))
            plink(V.tensor_scalar(pq[:, 0:1], pq[:, 0:1], float(NE - 1), None, ALU.min))
            V.tensor_scalar(diag[:, 0], ident[:], pq[:, 0:1], None, ALU.mult)
            V.tensor_scalar(diag[:, 1], ident[:], pq[:, 1:2], None, ALU.mult).then_inc(diag_ready, 1)
            bank = wait_full(dve, "plan", 0, "plan")
            V.tensor_copy(plan[0:1, 2 * P:2 * P + len(SIZES)], cend[0:1, :, NE]).then_inc(plan_ready, 1)
            dve.wait_ge(plan_ready, 1)
            V.tensor_copy(plan[0:1, 0:2 * P], bank[0:1, 0:2 * P]).then_inc(read("plan", "plan"), 1)
            wait_out(dve, "plan", 0, "plan")
            ends = size_ends(dve)

            def chunk(q, size):
                for f in range(KE):
                    bank = ps[JOBS.bank("chunk", f"gu{f}")]
                    dve.wait_ge(sg_ready, KE * q + f + 1)
                    V.tensor_tensor(hTm[:, f, 0:size], bank[:, CH:CH + size], sg[:, f, 0:size], ALU.mult)\
                        .then_inc(read("chunk", f"gu{f}"), 1)
                for j in PAIRS:
                    bank = wait_full(dve, "chunk", q, f"y{j}")
                    V.tensor_copy(yT[:, 2 * j:2 * j + 2, 0:size], pair(bank, size)).then_inc(read("chunk", f"y{j}"), 1)
                dve.wait_ge(io_loaded, 16 * q + 16)
                for i in range(2):
                    bank = wait_full(dve, "chunk", q, f"r{i}1")
                    V.tensor_scalar(ysb[0:size // 2, 1, i * BANK:(i + 1) * BANK], bank[0:size // 2, :],
                                    idx_out[0:size // 2, 1, 1:2].bitcast(F32), None, ALU.mult)\
                        .then_inc(read("chunk", f"r{i}1"), 1)

            for k, size in enumerate(SIZES):
                with dve.Fori(ends[k], ends[k + 1]) as q:
                    chunk(q, size)

            dve.wait_ge(fg_loaded, 16)

            def final(it, b):
                dve.wait_ge(f_rs, it * FB + b + 1)
                V.scalar_tensor_tensor(out=fb[b], in0=fb[b], scalar=rstd[:, b:b + 1], in1=g1b[:],
                                       op0=ALU.mult, op1=ALU.mult).then_inc(f_ready, 1)

            with dve.Fori(0, NTILE // FB) as it:
                for b in range(FB):
                    final(it, b)
            final(NTILE // FB, 0)


def kernel(**inputs):
    import numpy as np
    import concourse.bacc as bacc
    from concourse.bass_utils import run_bass_kernel_spmd

    x = {n: np.ascontiguousarray(v) for n, v in inputs.items()}
    cols = lambda v: np.ascontiguousarray(v.reshape(-1, NC, P).transpose(2, 1, 0))
    arrays = {
        "x": np.concatenate([x["x_prompt"].reshape(SEQ, D), x["x_sample"].reshape(-1, D)]),
        "conv_state": cols(x["state_conv"][0].reshape(-1, DA)).reshape(P, NC, STREAMS, TAPS - 1),
        "h0": cols(x["state_rglru"][0]),
        "norm1_g": x["norm1_g"], "w_in": x["w_in"][0], "ln_g": x["gmlp_ln_g"], "ln_b": x["gmlp_ln_b"],
        "w_sT": np.ascontiguousarray(x["gmlp_w_s"][0].transpose(0, 2, 1)),
        "b_s": x["gmlp_b_s"][0].reshape(1, NC * P),
        "conv_w": cols(x["conv_w"][0]), "conv_b": cols(x["conv_b"])[:, :, 0].copy(),
        "lru_w": np.stack([x["lru_w_a"][0], x["lru_w_x"][0]]),
        "gate_b": np.stack([cols(x[n].reshape(1, DA))[:, :, 0] for n in ("lru_b_a", "lru_b_x")], axis=1),
        "lam": cols(x["lru_lambda"])[:, :, 0].copy(),
        "w_out": x["w_out"][0], "norm2_g": x["norm2_g"],
        "router_gw": x["router_group_w"][0], "router_ew": x["router_expert_w"][0],
        "router_b": np.concatenate([x["router_group_b"], x["router_expert_b"]], axis=1),
        "w_gate": x["expert_w_gate"][0], "w_up": x["expert_w_up"][0], "w_down": x["expert_w_down"][0],
        "final_g": x["final_norm_g"].reshape(1, D),
    }
    outs = {"y": (NTOK, D), "conv_p": (P, NC, TAPS - 1), "h_p": (P, NC), "v_s": (STREAMS * FRAMES, DA),
            "conv_s": (P, NC, STREAMS, TAPS - 1), "h_s": (P, NC, STREAMS)}
    nc = bacc.Bacc("TRN2", target_bir_lowering=False, num_devices=1)
    aps = {n: nc.dram_tensor(f"in_{n}", v.shape, F32, kind="ExternalInput").ap() for n, v in arrays.items()}
    aps |= {n: nc.dram_tensor(f"out_{n}", v, F32, kind="ExternalOutput").ap() for n, v in outs.items()}
    hymba_step(nc, aps)
    r = run_bass_kernel_spmd(nc, [{f"in_{n}": v for n, v in arrays.items()}], core_ids=[0]).results[0]
    y = r["out_y"]
    rows = lambda v: np.moveaxis(v, (1, 0), (-2, -1)).reshape(*v.shape[2:], DA)
    return (y[:SEQ].reshape(1, SEQ, D), y[SEQ:].reshape(STREAMS, FRAMES, D),
            rows(r["out_conv_p"]).reshape(1, 1, TAPS - 1, DA), rows(r["out_h_p"]).reshape(1, 1, DA),
            r["out_v_s"].reshape(1, STREAMS, FRAMES, DA), rows(r["out_conv_s"]).reshape(1, STREAMS, TAPS - 1, DA),
            rows(r["out_h_s"]).reshape(1, STREAMS, DA))
```
